# Optimizing a Trainium2 kernel written in Bass

```python
import jax, jax.numpy as jnp
from jax import lax
import numpy as np
import math

D_MODEL = 1024
BATCH = 1
SEQ = 256
DEPTH = 2

HEAD_DIM = 64
N_HEADS = D_MODEL // HEAD_DIM
N_HEADS_A = N_HEADS // 2
N_KV_A = N_HEADS_A // 4
N_HEADS_B = N_HEADS - N_HEADS_A
D_FF = 4 * D_MODEL
GRID_W = 64
AXIAL_THETA = 10000.0
ROPE_THETA = 500000.0
ROPE_DIM = HEAD_DIM // 4
BLOCK_Q = 128
DILATED_PATTERNS = ((128, 1), (512, 4), (2048, 16))
NORM_EPS = 1e-6
NEG_INF = -1e30

QA_W = N_HEADS_A * HEAD_DIM
KVA_W = N_KV_A * HEAD_DIM
QB_W = N_HEADS_B * HEAD_DIM
IN_W = QA_W + 2 * KVA_W + 3 * QB_W
MIX_W = QA_W + QB_W


def rmsnorm(x, g):
    xf = x.astype(jnp.float32)
    y = xf * lax.rsqrt(jnp.mean(xf * xf, axis=-1, keepdims=True) + NORM_EPS)
    return (y * g.astype(jnp.float32)).astype(x.dtype)

def rope(x, pos, theta):
    half = x.shape[-1] // 2
    freqs = theta ** (-jnp.arange(half, dtype=jnp.float32) / half)
    ang = pos.astype(jnp.float32)[:, None] * freqs[None, :]
    cos = jnp.cos(ang)[:, None, :]
    sin = jnp.sin(ang)[:, None, :]
    xf = x.astype(jnp.float32)
    x1, x2 = xf[..., :half], xf[..., half:]
    return jnp.concatenate([x1 * cos - x2 * sin, x2 * cos + x1 * sin], axis=-1).astype(x.dtype)

def axial_rope(x, row_ids, col_ids):
    h = x.shape[-1] // 2
    return jnp.concatenate([rope(x[..., :h], row_ids, AXIAL_THETA),
                            rope(x[..., h:], col_ids, AXIAL_THETA)], axis=-1)

def partial_rope(x, pos):
    return jnp.concatenate([rope(x[..., :ROPE_DIM], pos, ROPE_THETA), x[..., ROPE_DIM:]], axis=-1)

def global_gqa(q, k, v):
    B, S, HA, hd = q.shape
    HKV = k.shape[2]
    G = HA // HKV
    nb = S // BLOCK_Q
    scale = hd ** -0.5
    qb = q.reshape(B, nb, BLOCK_Q, HKV, G, hd).transpose(1, 0, 2, 3, 4, 5)

    def one(qblk):
        s = jnp.einsum('bqkgd,bskd->bkgqs', qblk, k).astype(jnp.float32) * scale
        p = jax.nn.softmax(s, axis=-1).astype(v.dtype)
        return jnp.einsum('bkgqs,bskd->bqkgd', p, v)

    o = lax.map(one, qb)
    return o.transpose(1, 0, 2, 3, 4, 5).reshape(B, S, HA * hd)

def dilated_window_attention(q, k, v):
    B, S, H, hd = q.shape
    nb = S // BLOCK_Q
    scale = hd ** -0.5
    qb = q.reshape(B, nb, BLOCK_Q, H, hd).transpose(1, 0, 2, 3, 4)
    starts = jnp.arange(nb, dtype=jnp.int32) * BLOCK_Q

    def one(args):
        qblk, start = args
        pos = start + jnp.arange(BLOCK_Q, dtype=jnp.int32)
        outs, lses = [], []
        for window, dil in DILATED_PATTERNS:
            n_side = window // (2 * dil)
            offs = jnp.arange(-n_side, n_side + 1, dtype=jnp.int32) * dil
            idx = pos[:, None] + offs[None, :]
            valid = (idx >= 0) & (idx < S)
            idxc = jnp.clip(idx, 0, S - 1)
            kg = k[:, idxc]
            vg = v[:, idxc]
            s = jnp.einsum('bqhd,bqjhd->bhqj', qblk, kg).astype(jnp.float32) * scale
            s = jnp.where(valid[None, None], s, NEG_INF)
            lse = jax.nn.logsumexp(s, axis=-1, keepdims=True)
            p = jnp.exp(s - lse).astype(v.dtype)
            outs.append(jnp.einsum('bhqj,bqjhd->bqhd', p, vg).astype(jnp.float32))
            lses.append(lse[..., 0])
        wts = jax.nn.softmax(jnp.stack(lses, axis=0), axis=0)
        o = jnp.einsum('pbhq,pbqhd->bqhd', wts, jnp.stack(outs, axis=0))
        return o.astype(v.dtype)

    o = lax.map(one, (qb, starts))
    return o.transpose(1, 0, 2, 3, 4).reshape(B, S, H * hd)

def hybrid_layer(x, n1, w_in, q_norm, k_norm, out_norm_a, out_norm_b, w_out,
                 n2, w_mlp_in, w_mlp_out, row_ids, col_ids, pos):
    B, S, _ = x.shape
    h = rmsnorm(x, n1)
    proj = h @ w_in
    cuts = np.cumsum([QA_W, KVA_W, KVA_W, QB_W, QB_W]).tolist()
    qa, ka, va, qb, kb, vb = jnp.split(proj, cuts, axis=-1)

    qa = qa.reshape(B, S, N_HEADS_A, HEAD_DIM)
    ka = ka.reshape(B, S, N_KV_A, HEAD_DIM)
    va = va.reshape(B, S, N_KV_A, HEAD_DIM)
    qa = axial_rope(rmsnorm(qa, q_norm), row_ids, col_ids)
    ka = axial_rope(rmsnorm(ka, k_norm), row_ids, col_ids)
    ya = global_gqa(qa, ka, va)

    qb = partial_rope(qb.reshape(B, S, N_HEADS_B, HEAD_DIM), pos)
    kb = partial_rope(kb.reshape(B, S, N_HEADS_B, HEAD_DIM), pos)
    vb = vb.reshape(B, S, N_HEADS_B, HEAD_DIM)
    yb = dilated_window_attention(qb, kb, vb)

    y = jnp.concatenate([rmsnorm(ya, out_norm_a), rmsnorm(yb, out_norm_b)], axis=-1)
    x = x + y @ w_out

    u = rmsnorm(x, n2) @ w_mlp_in
    u = jnp.square(jax.nn.relu(u))
    return x + u @ w_mlp_out

def first_inputs(seed: int = 0) -> dict:
    key = jax.random.key(seed)
    ks = jax.random.split(key, 13)
    f32 = jnp.float32

    def gain(k, shape):
        return 1.0 + 0.02 * jax.random.normal(k, shape, f32)

    return {
        "x": jax.random.normal(ks[0], (BATCH, SEQ, D_MODEL), f32),
        "norm1": gain(ks[1], (DEPTH, D_MODEL)),
        "w_in": jax.random.normal(ks[2], (DEPTH, D_MODEL, IN_W), f32) * D_MODEL ** -0.5,
        "q_norm": gain(ks[3], (DEPTH, HEAD_DIM)),
        "k_norm": gain(ks[4], (DEPTH, HEAD_DIM)),
        "out_norm_a": gain(ks[5], (DEPTH, QA_W)),
        "out_norm_b": gain(ks[6], (DEPTH, QB_W)),
        "w_out": jax.random.normal(ks[7], (DEPTH, MIX_W, D_MODEL), f32) * MIX_W ** -0.5,
        "norm2": gain(ks[8], (DEPTH, D_MODEL)),
        "w_mlp_in": jax.random.normal(ks[9], (DEPTH, D_MODEL, D_FF), f32) * D_MODEL ** -0.5,
        "w_mlp_out": jax.random.normal(ks[10], (DEPTH, D_FF, D_MODEL), f32) * D_FF ** -0.5,
        "final_norm": gain(ks[11], (D_MODEL,)),
    }

def first_block(x, norm1, w_in, q_norm, k_norm, out_norm_a, out_norm_b, w_out,
              norm2, w_mlp_in, w_mlp_out, final_norm):
    S = x.shape[1]
    rows = S // GRID_W
    row_ids = jnp.repeat(jnp.arange(rows, dtype=jnp.int32), GRID_W)
    col_ids = jnp.tile(jnp.arange(GRID_W, dtype=jnp.int32), rows)
    pos = jnp.arange(S, dtype=jnp.int32)
    for l in range(DEPTH):
        x = hybrid_layer(x, norm1[l], w_in[l], q_norm[l], k_norm[l],
                         out_norm_a[l], out_norm_b[l], w_out[l], norm2[l],
                         w_mlp_in[l], w_mlp_out[l], row_ids, col_ids, pos)
    return rmsnorm(x, final_norm)


D_FF_2 = 2816
D_MIX = D_MODEL
A_HEADS = 4
A_DIM = A_HEADS * HEAD_DIM
CHUNK = 128
B_GROUPS = 4
B_DIM = B_GROUPS * HEAD_DIM
B_CONV = 3
C_HEADS = 8
C_DIM = C_HEADS * HEAD_DIM
C_CONV = 4
RG_C = 8.0
IN_COLS = 2 * A_DIM + 3 * B_DIM + 2 * C_DIM
ALPHA = (2.0 * DEPTH) ** 0.25
BETA = (8.0 * DEPTH) ** -0.25
LN_EPS = 1e-5


def layer_norm(x, g, b):
    xf = x.astype(jnp.float32)
    mu = jnp.mean(xf, axis=-1, keepdims=True)
    xc = xf - mu
    var = jnp.mean(xc * xc, axis=-1, keepdims=True)
    y = xc * lax.rsqrt(var + LN_EPS) * g.astype(jnp.float32) + b.astype(jnp.float32)
    return y.astype(x.dtype)

def swiglu(x, w_gate, w_up, w_down):
    return (jax.nn.silu(x @ w_gate) * (x @ w_up)) @ w_down

def causal_dwconv(x, w):
    k_width = w.shape[0]
    s = x.shape[1]
    xp = jnp.pad(x, ((0, 0), (k_width - 1, 0), (0, 0)))
    y = xp[:, 0:s] * w[0]
    for k in range(1, k_width):
        y = y + xp[:, k:k + s] * w[k]
    return y

def mixer_spatial_gating(z, ln_g, ln_b, w_s, b_s):
    z = jax.nn.gelu(z)
    u, v = jnp.split(z, 2, axis=-1)
    v = layer_norm(v, ln_g, ln_b)
    bsz, s, _ = v.shape
    vc = v.reshape(bsz, s // CHUNK, CHUNK, A_HEADS, HEAD_DIM)
    mask = jnp.tril(jnp.ones((CHUNK, CHUNK), dtype=bool))
    w = jnp.where(mask[None], w_s, jnp.zeros_like(w_s))
    mixed = jnp.einsum('hts,bnshd->bnthd', w, vc) + b_s.T[None, None, :, :, None]
    return u * mixed.reshape(bsz, s, A_DIM)

def mixer_short_conv(z, conv_w):
    b_gate, c_gate, xin = jnp.split(z, 3, axis=-1)
    return b_gate * causal_dwconv(c_gate * xin, conv_w)

def _lru_combine(left, right):
    a1, b1 = left
    a2, b2 = right
    return a1 * a2, a2 * b1 + b2

def mixer_rglru(z, conv_w, conv_b, w_a, b_a, w_i, b_i, lam):
    gate, xr = jnp.split(z, 2, axis=-1)
    xr = causal_dwconv(xr, conv_w) + conv_b
    bsz, s, _ = xr.shape
    xh = xr.reshape(bsz, s, C_HEADS, HEAD_DIM)
    r = jax.nn.sigmoid(jnp.einsum('bshd,hde->bshe', xh, w_a) + b_a).reshape(bsz, s, C_DIM)
    i = jax.nn.sigmoid(jnp.einsum('bshd,hde->bshe', xh, w_i) + b_i).reshape(bsz, s, C_DIM)
    log_a = -RG_C * r.astype(jnp.float32) * jax.nn.softplus(-lam.astype(jnp.float32))
    a = jnp.exp(log_a)
    mult = jnp.sqrt(jnp.maximum(1.0 - jnp.exp(2.0 * log_a), 0.0))
    bx = mult * (i * xr).astype(jnp.float32)
    _, h = lax.associative_scan(_lru_combine, (a, bx), axis=1)
    return jax.nn.gelu(gate) * h.astype(gate.dtype)

def second_inputs(seed: int = 0) -> dict:
    key = jax.random.key(seed)
    ks = jax.random.split(key, 24)

    def nrm(k, shape, fan_in, scale=1.0):
        return jax.random.normal(k, shape, jnp.float32) * (scale * fan_in ** -0.5)

    x = jax.random.normal(ks[0], (BATCH, SEQ, D_MODEL), jnp.float32)
    ln_g = 1.0 + 0.02 * jax.random.normal(ks[1], (DEPTH, 3, D_MODEL), jnp.float32)
    ln_b = 0.02 * jax.random.normal(ks[2], (DEPTH, 3, D_MODEL), jnp.float32)
    ffn_w_gate = nrm(ks[3], (DEPTH, 2, D_MODEL, D_FF_2), D_MODEL)
    ffn_w_up = nrm(ks[4], (DEPTH, 2, D_MODEL, D_FF_2), D_MODEL)
    ffn_w_down = nrm(ks[5], (DEPTH, 2, D_FF_2, D_MODEL), D_FF_2, BETA)
    w_in = nrm(ks[6], (DEPTH, D_MODEL, IN_COLS), D_MODEL)
    sgu_ln_g = 1.0 + 0.02 * jax.random.normal(ks[7], (DEPTH, A_DIM), jnp.float32)
    sgu_ln_b = 0.02 * jax.random.normal(ks[8], (DEPTH, A_DIM), jnp.float32)
    sgu_w = nrm(ks[9], (DEPTH, A_HEADS, CHUNK, CHUNK), CHUNK)
    sgu_b = 1.0 + 0.02 * jax.random.normal(ks[10], (DEPTH, A_HEADS, CHUNK), jnp.float32)
    sconv_w = nrm(ks[11], (DEPTH, B_CONV, B_DIM), B_CONV)
    rg_conv_w = nrm(ks[12], (DEPTH, C_CONV, C_DIM), C_CONV)
    rg_conv_b = 0.02 * jax.random.normal(ks[13], (DEPTH, C_DIM), jnp.float32)
    rg_w_a = nrm(ks[14], (DEPTH, C_HEADS, HEAD_DIM, HEAD_DIM), HEAD_DIM)
    rg_b_a = 0.02 * jax.random.normal(ks[15], (DEPTH, C_HEADS, HEAD_DIM), jnp.float32)
    rg_w_i = nrm(ks[16], (DEPTH, C_HEADS, HEAD_DIM, HEAD_DIM), HEAD_DIM)
    rg_b_i = 0.02 * jax.random.normal(ks[17], (DEPTH, C_HEADS, HEAD_DIM), jnp.float32)
    u = jax.random.uniform(ks[18], (DEPTH, C_DIM), jnp.float32, minval=0.9, maxval=0.999)
    a0 = u ** (1.0 / RG_C)
    rg_lambda = jnp.log(a0) - jnp.log1p(-a0)
    w_out = nrm(ks[19], (DEPTH, D_MIX, D_MODEL), D_MIX, BETA)
    return {"x": x, "ln_g": ln_g, "ln_b": ln_b, "ffn_w_gate": ffn_w_gate, "ffn_w_up": ffn_w_up,
            "ffn_w_down": ffn_w_down, "w_in": w_in, "sgu_ln_g": sgu_ln_g, "sgu_ln_b": sgu_ln_b,
            "sgu_w": sgu_w, "sgu_b": sgu_b, "sconv_w": sconv_w, "rg_conv_w": rg_conv_w,
            "rg_conv_b": rg_conv_b, "rg_w_a": rg_w_a, "rg_b_a": rg_b_a, "rg_w_i": rg_w_i,
            "rg_b_i": rg_b_i, "rg_lambda": rg_lambda, "w_out": w_out}

def second_block(x, ln_g, ln_b, ffn_w_gate, ffn_w_up, ffn_w_down, w_in, sgu_ln_g, sgu_ln_b,
              sgu_w, sgu_b, sconv_w, rg_conv_w, rg_conv_b, rg_w_a, rg_b_a, rg_w_i, rg_b_i,
              rg_lambda, w_out):
    split_a = 2 * A_DIM
    split_b = split_a + 3 * B_DIM
    for l in range(DEPTH):
        f = swiglu(x, ffn_w_gate[l, 0], ffn_w_up[l, 0], ffn_w_down[l, 0])
        x = layer_norm(ALPHA * x + 0.5 * f, ln_g[l, 0], ln_b[l, 0])
        z = x @ w_in[l]
        z_a = z[..., :split_a]
        z_b = z[..., split_a:split_b]
        z_c = z[..., split_b:]
        y_a = mixer_spatial_gating(z_a, sgu_ln_g[l], sgu_ln_b[l], sgu_w[l], sgu_b[l])
        y_b = mixer_short_conv(z_b, sconv_w[l])
        y_c = mixer_rglru(z_c, rg_conv_w[l], rg_conv_b[l], rg_w_a[l], rg_b_a[l],
                          rg_w_i[l], rg_b_i[l], rg_lambda[l])
        y = jnp.concatenate([y_a, y_b, y_c], axis=-1) @ w_out[l]
        x = layer_norm(ALPHA * x + y, ln_g[l, 1], ln_b[l, 1])
        f = swiglu(x, ffn_w_gate[l, 1], ffn_w_up[l, 1], ffn_w_down[l, 1])
        x = layer_norm(ALPHA * x + 0.5 * f, ln_g[l, 2], ln_b[l, 2])
    return x


_first_inputs = second_inputs


def second_inputs(seed=0):
    import zlib

    import numpy as np

    out = dict(_first_inputs(seed))
    spreads = {}
    factors = {'sgu_ln_g': 8.0,
     'sgu_ln_b': 8.0,
     'sgu_b': 8.0,
     'rg_conv_b': 2.99,
     'rg_b_a': 8.0,
     'rg_b_i': 8.0}
    for name, (base, spread) in spreads.items():
        noise = np.random.default_rng([zlib.crc32(name.encode()), seed]).standard_normal(out[name].shape)
        drawn = base * np.exp(spread * noise) if base else spread * noise
        out[name] = __import__('jax').numpy.asarray(drawn.astype(out[name].dtype))
    for name, factor in factors.items():
        out[name] = (out[name] * factor).astype(out[name].dtype)
    return out


_narrow_inputs = second_inputs


def second_inputs(seed=0):
    out = dict(_narrow_inputs(seed))
    wider = {'sgu_ln_g': 5.19, 'sgu_ln_b': 5.38, 'sgu_b': 3.69, 'rg_b_a': 12.0, 'rg_b_i': 6.35}
    for name, times in wider.items():
        mean = out[name].mean()
        out[name] = (mean + times * (out[name] - mean)).astype(out[name].dtype)
    return out


def setup_inputs(seed=0):
    out = dict(first_inputs(seed))
    for name, value in second_inputs(seed + 1).items():
        if name != "x":
            out[name + "_2"] = value
    return out


def reference(
    x, norm1, w_in, q_norm, k_norm, out_norm_a, out_norm_b, w_out, norm2, w_mlp_in, w_mlp_out,
    final_norm, ln_g_2, ln_b_2, ffn_w_gate_2, ffn_w_up_2, ffn_w_down_2, w_in_2, sgu_ln_g_2,
    sgu_ln_b_2, sgu_w_2, sgu_b_2, sconv_w_2, rg_conv_w_2, rg_conv_b_2, rg_w_a_2, rg_b_a_2,
    rg_w_i_2, rg_b_i_2, rg_lambda_2, w_out_2,
):
    x = first_block(
        x, norm1, w_in, q_norm, k_norm, out_norm_a, out_norm_b, w_out, norm2, w_mlp_in,
        w_mlp_out, final_norm,
    )
    return second_block(
        x, ln_g_2, ln_b_2, ffn_w_gate_2, ffn_w_up_2, ffn_w_down_2, w_in_2, sgu_ln_g_2,
        sgu_ln_b_2, sgu_w_2, sgu_b_2, sconv_w_2, rg_conv_w_2, rg_conv_b_2, rg_w_a_2, rg_b_a_2,
        rg_w_i_2, rg_b_i_2, rg_lambda_2, w_out_2,
    )


_drawn_inputs = setup_inputs


def setup_inputs(seed=0):
    import zlib

    import numpy as np

    out = dict(_drawn_inputs(seed))
    spreads = {}
    factors = {'q_norm': 3.995, 'k_norm': 4.423, 'out_norm_a': 2.757, 'out_norm_b': 2.938}
    for name, (base, spread) in spreads.items():
        noise = np.random.default_rng([zlib.crc32(name.encode()), seed]).standard_normal(out[name].shape)
        drawn = base * np.exp(spread * noise) if base else spread * noise
        out[name] = __import__('jax').numpy.asarray(drawn.astype(out[name].dtype))
    for name, factor in factors.items():
        out[name] = (out[name] * factor).astype(out[name].dtype)
    return out
```

```python
import math
from contextlib import ExitStack

import concourse.bass as bass
import numpy as np
from concourse import mybir

P = 128
SEQ, D, DEPTH, HD = 256, 1024, 2, 64
T = SEQ // P
KD = D // P
FF1, FF2 = 4096, 2816
NHA, NKV, NHB = 8, 2, 8
GROUP = NHA // NKV
IN_W = 2304
QKA = (NHA + NKV) * HD
VA0 = QKA
QB0 = VA0 + NKV * HD
VB0 = QB0 + 2 * NHB * HD
SCALE = HD ** -0.5
RMS_EPS, LN_EPS = 1e-6, 1e-5
ALPHA = (2.0 * DEPTH) ** 0.25
AH, CONV_B, CONV_C, CT = 4, 3, 4, 4
RG_C = 8.0

RING, CW = 3, 2048
BLK = CW // KD
NI1, NI2 = FF1 // BLK, FF2 // BLK
WIN = IN_W // BLK
OUT1 = [2, 2, 2, 2]
OUT2 = [2, 2, 1, 1, 1, 1]
MLP0 = WIN + len(OUT1)
CH1 = MLP0 + 2 * NI1
FFN = 3 * NI2
CH2 = 2 * FFN + WIN + len(OUT2)
assert CH1 % RING == 0 and CH2 % RING == 0 and FFN % RING == 0
ZORDER = [7, 8, 0, 1, 5, 6, 2, 3, 4]

C1 = 3 * KD
N2 = 6 * KD
LN0 = DEPTH * C1
M_CONV, M_CB, M_BA, M_BI, M_LAM = 0, 16, 20, 24, 28
M_SC, M_SGB = 32, 38
NM = 42
MX0 = LN0 + DEPTH * N2
FIN0 = MX0 + DEPTH * NM
NCOL = FIN0 + KD
ORD1, ORD2, ORDP = 114, 151, 12
HEADS = [0, 4, 1, 5, 2, 6, 3, 7] + list(range(8, 16))


def attention_steps(first):
    steps = []
    for k in range(10):
        steps.append([(kind, first + e) for kind, e in (("score", k), ("turn", k - 1), ("pv", k - 2)) if 0 <= e < 8])
    return steps


def plan1():
    a, b = attention_steps(0), attention_steps(8)
    plan = [("chunk", 0), ("chunk", 1), ("chunk", 2), ("ropeA", 0), ("chunk", 3), ("chunk", 4), ("tA", 0), ("chunk", 5)]
    plan += sum(a[0:3], []) + [("chunk", 6), ("ropeB", 0)] + sum(a[3:6], []) + [("chunk", 7)] + sum(a[6:], [])
    plan += [("ynorm", 0), ("chunk", 8), ("yturn", 0), ("tB", 0)] + sum(b, []) + [("ynorm", 1), ("yturn", 1)]
    return plan


PLAN1 = plan1()
ROWS = [
    [(l * C1 + at, name, (l * n, l * n + n)) for l in range(DEPTH)
     for at, name, n in ((0, "norm1", 8), (8, "norm2", 8), (16, "out_norm_a", 4), (20, "out_norm_b", 4))],
    [(l * N2 + at, name, (l * 24, l * 24 + 24)) for l in range(DEPTH) for at, name in ((0, "ln_g_rows"), (24, "ln_b_rows"))],
    [(l * NM + at, name, (l * n, l * n + n)) for l in range(DEPTH)
     for at, name, n in ((M_CONV, "rg_conv_w_2", 16), (M_CB, "rg_conv_b_2", 4), (M_BA, "rg_b_a_2", 4), (M_BI, "rg_b_i_2", 4),
                         (M_LAM, "rg_lambda_2", 4), (M_SC, "sconv_w_2", 6), (M_SGB, "sgu_b_2", 4))]
    + [(DEPTH * NM, "final_norm_rows", (0, 8))],
]
NROWS = [DEPTH * C1, DEPTH * N2, DEPTH * NM + KD]


def program(nc, ins, out):
    f32, f32r, i32 = mybir.dt.float32, mybir.dt.float32r, mybir.dt.int32
    bf16 = mybir.dt.bfloat16
    ALU, ACT, AX = mybir.AluOpType, mybir.ActivationFunctionType, mybir.AxisListType
    ds = bass.ds
    ctx = ExitStack()
    with ctx:
        def sb(name, shape, dt=f32):
            return ctx.enter_context(nc.sbuf_tensor(name, shape, dt))

        def sem(name):
            return ctx.enter_context(nc.semaphore(name))

        raw = sb("raw", [P, RING, CW])
        w_hi = sb("w_hi", [P, RING, CW], f32r)
        w_lo = sb("w_lo", [P, RING, CW], f32r)
        x_tok = sb("x_tok", [P, T, D])
        xn = sb("xn", [P, T, D])
        a_hi = sb("a_hi", [P, KD, SEQ], f32r)
        a_lo = sb("a_lo", [P, KD, SEQ], f32r)
        relu = sb("relu", [P, 2 * SEQ])
        hid = sb("hid", [P, 2 * SEQ])
        h_hi = sb("h_hi", [P, 3, 2 * SEQ], f32r)
        h_lo = sb("h_lo", [P, 3, 2 * SEQ], f32r)
        proj = sb("proj", [P, T, IN_W])
        sqs = sb("sqs", [P, T, QKA])
        rope_a = sb("rope_a", [P, T, QKA])
        rope_b = sb("rope_b", [P, T, QKA])
        qkA = rope_b
        qkTB = sb("qkTB", [P, 8, SEQ])
        cg = sb("cg", [P, T, QKA])
        sg = sb("sg", [P, T, QKA])
        qkTA = cg[:, :, :].rearrange("p a b -> p (a b)").rearrange("p (i s) -> p i s", s=SEQ)
        masked = sb("masked", [P, 2, T * SEQ])
        prob = sb("prob", [P, 2, T * SEQ])
        probT = sb("probT", [P, 2, T * SEQ])
        y_tok = sb("y_tok", [P, T, D])
        ident = sb("ident", [P, P])
        rope_ax = sb("rope_ax", [P, T, 2 * HD])
        rope_pt = sb("rope_pt", [P, T, 32])
        logc = sb("logc", [P, T, SEQ])
        qk_gain = sb("qk_gain", [P, 2 * HD])
        g_bc = masked[:, :, :].rearrange("p a b -> p (a b)")
        b_bc = prob[:, :, :].rearrange("p a b -> p (a b)")
        rows = [y_tok[:, 0, n * P:(n + 1) * P] for n in range(3)]
        cols = sb("cols", [P, NCOL])
        zero = sb("zero", [P, P], bf16)
        ss = sb("ss", [P, 8])
        stat = sb("stat", [P, T, 2, 6])
        mv = sb("mv", [P, T, 2])
        nwt = sb("nwt", [P, 4, 20])
        rstd = sb("rstd", [P, T])
        ssA = sb("ssA", [P, 20])
        rstdA = sb("rstdA", [P, 20])
        ssy = sb("ssy", [P, 4])
        rstdy = sb("rstdy", [P, 4])
        nmax = sb("nmax", [P, 16, T])
        rsum = sb("rsum", [P, 16, T])
        rinv = sb("rinv", [P, 16, T])
        sgu_gb = sb("sgu_gb", [P, 2, 256])
        bd = sb("bd", [P, 2, CT, P])
        sp = sb("sp", [P, 4, DEPTH * CT])

        def part(tensor, n, width):
            return tensor[:, :, :].rearrange("p a b -> p (a b)")[:, n * width:(n + 1) * width]

        W4 = CT * SEQ
        xr = part(proj, 0, W4)
        r_gate = part(proj, 1, W4)
        i_gate = part(proj, 2, W4)
        th = part(proj, 3, W4)
        gg = part(y_tok, 0, W4)
        root = part(qkTB, 0, W4)
        a_dec = part(qkTB, 1, W4)
        q_rec = part(y_tok, 1, W4)
        hs = part(sqs, 0, W4)
        ug = part(cg, 0, 512)
        vg = part(cg, 1, 512)
        vn = part(sg, 0, 512)
        ya = part(sg, 1, 512)
        bg = part(rope_a, 0, 512)
        cgt = part(rope_a, 1, 512)
        yb = part(proj, 8, 512)
        xrp = part(rope_b, 0, CT * (SEQ + CONV_C - 1)).rearrange("p (c s) -> p c s", c=CT)
        cxp = part(probT, 0, 2 * (SEQ + CONV_B - 1)).rearrange("p (c s) -> p c s", c=2)
        sgu_rows = part(qkTB, 0, AH * P).rearrange("p (h s) -> p h s", h=AH)
        sguT = part(logc, 0, AH * P).rearrange("p (h s) -> p h s", h=AH)
        affine = relu[:, :].rearrange("p (a s) -> p a s", a=2)
        h_hi_flat = h_hi[:, :, :].rearrange("p a b -> p (a b)")
        h_lo_flat = h_lo[:, :, :].rearrange("p a b -> p (a b)")

        def mixed(k, n=1):
            if k < 4:
                return [h[:, k * SEQ:(k + n) * SEQ] for h in (h_hi_flat, h_lo_flat)]
            return [a[:, k:k + n, :].rearrange("p a b -> p (a b)") for a in (a_hi, a_lo)]

        acc = ctx.enter_context(nc.psum_tensor("acc", [P, 4, 512], f32))
        work = ctx.enter_context(nc.psum_tensor("work", [P, 4, 512], f32))
        acc_flat = acc[:, :, :].rearrange("p a b -> p (a b)")
        work_flat = work[:, :, :].rearrange("p a b -> p (a b)")

        loaded = [sem(f"loaded{s}") for s in range(RING)]
        hi_done, lo_done, used = sem("hi_done"), sem("lo_done"), sem("used")
        x_loaded, id_loaded, tab_loaded, rows_loaded = (sem(n) for n in ("x_loaded", "id_loaded", "tab_loaded", "rows_loaded"))
        rowsT, cols_ready, zeroed, pads, conv_pads = (sem(n) for n in ("rowsT", "cols_ready", "zeroed", "pads", "conv_pads"))
        lam_abs, lam_exp, sp_ready = (sem(n) for n in ("lam_abs", "lam_exp", "sp_ready"))
        x_done, sq_sum, xn_ready, xT, aT_hi, aT_lo = (sem(n) for n in ("x_done", "sq_sum", "xn_ready", "xT", "aT_hi", "aT_lo"))
        gb_loaded, x_scaled, pool_order = (sem(n) for n in ("gb_loaded", "x_scaled", "pool_order"))
        dve_order = sem("dve_order")
        gain_loaded, rope_tab, proj_ready, qk_sq, ropeA_done, ropeB_done = (
            sem(n) for n in ("gain_loaded", "rope_tab", "proj_ready", "qk_sq", "ropeA_done", "ropeB_done"))
        qkA_ps, qkA_T, qkB_ps, qB_T, kB_T = (sem(n) for n in ("qkA_ps", "qkA_T", "qkB_ps", "qB_T", "kB_T"))
        s_ready, nmax_ready, exp_done, pT_ps, pTA, pTB, pv_done = (
            sem(n) for n in ("s_ready", "nmax_ready", "exp_done", "pT_ps", "pTA", "pTB", "pv_done"))
        y_ready, y_sq, yn_ready, yT_ps, yT_hi, yT_lo = (
            sem(n) for n in ("y_ready", "y_sq", "yn_ready", "yT_ps", "yT_hi", "yT_lo"))
        relu_done, h1_sq, h1_hi, h1_lo = (sem(n) for n in ("relu_done", "h1_sq", "h1_hi", "h1_lo"))
        silu_done, h2_f, h2_hi, h2_lo = (sem(n) for n in ("silu_done", "h2_f", "h2_hi", "h2_lo"))
        mix_w, mix_bd, sgu_masked, sgu_ps, sgu_T = (sem(n) for n in ("mix_w", "mix_bd", "sgu_masked", "sgu_ps", "sgu_T"))
        z_done, cx_done, conv_done, gate_ps, sig_done, th_done, th_pos, root_done = (
            sem(n) for n in ("z_done", "cx_done", "conv_done", "gate_ps", "sig_done", "th_done", "th_pos", "root_done"))
        v_done, mix_ps, ya_done, yaT_ps, y2_f, y2_hi, y2_lo = (
            sem(n) for n in ("v_done", "mix_ps", "ya_done", "yaT_ps", "y2_f", "y2_hi", "y2_lo"))
        out_done = sem("out_done")
        passed_sp, passed_pool, passed_dve = sem("passed_sp"), sem("passed_pool"), sem("passed_dve")

        BASE2 = DEPTH * CH1

        def g1(l, c):
            return l * CH1 + c

        def g2(l, c):
            return l * CH2 + (BASE2 + c)

        def round1(l, c):
            return l * (CH1 // RING) + (c // RING + 1)

        def round2(l, c):
            return l * (CH2 // RING) + (BASE2 // RING + c // RING + 1)

        block = ctx.enter_context(nc.Block())

        @block.sync
        def _(sp_):
            sp_.dma_start(ident[:, :], ins["c_ident"]).then_inc(id_loaded, 16)
            for t in range(T):
                sp_.dma_start(x_tok[:, t, :], ins["x"][t * P:(t + 1) * P, :]).then_inc(x_loaded, 16)
            for n, r in enumerate(ROWS):
                for at, name, src_rows in r:
                    count = src_rows[1] - src_rows[0]
                    sp_.dma_start(rows[n][at:at + count, :], ins[name][src_rows[0]:src_rows[1], :])\
                       .then_inc(rows_loaded, 16)

            def slot_free(g):
                sp_.wait_ge(lo_done, g + 1)
                sp_.sem_inc(passed_sp, 1)

            def load(g, slot, src, k):
                slot_free(g)
                sp_.dma_start(raw[:, slot, :].rearrange("p (k n) -> p k n", k=k), src).then_inc(loaded[slot], 16)

            def wide(name, l, at):
                return ins[name][ds(l, 1), :, ds(at, BLK)].rearrange("o (k p) n -> p (o k) n", p=P)

            def tall(name, l, at, k):
                return ins[name][ds(l, 1), ds(at, k * P), :].rearrange("o (k p) n -> p (o k) n", p=P)

            with sp_.Fori(0, DEPTH) as l:
                for c in range(WIN):
                    load(g1(l, c), c % RING, wide("w_in", l, c * BLK), KD)
                at = 0
                for j, k in enumerate(OUT1):
                    load(g1(l, WIN + j), (WIN + j) % RING, tall("w_out", l, at, k), k)
                    at += k * P
                load(g1(l, MLP0), MLP0 % RING, wide("w_mlp_in", l, 0), KD)
                with sp_.Fori(0, (NI1 - 1) // 3) as it:
                    for j in range(3):
                        i, c = it * 3 + (1 + j), MLP0 + 1 + 2 * j
                        load(g1(l, c) + it * 6, c % RING, wide("w_mlp_in", l, i * BLK), KD)
                        load(g1(l, c + 1) + it * 6, (c + 1) % RING, tall("w_mlp_out", l, (i - 1) * BLK, 2), 2)
                load(g1(l, CH1 - 1), (CH1 - 1) % RING, tall("w_mlp_out", l, (NI1 - 1) * BLK, 2), 2)

            def ffn(l, f, cb):
                m = l * 2 + f
                load(g2(l, cb), 0, wide("ffn_w_gate_2", m, 0), KD)
                load(g2(l, cb + 1), 1, wide("ffn_w_up_2", m, 0), KD)
                with sp_.Fori(0, NI2 - 1) as it:
                    i = it + 1
                    load(g2(l, cb + 2) + it * 3, 2, wide("ffn_w_gate_2", m, i * BLK), KD)
                    load(g2(l, cb + 3) + it * 3, 0, wide("ffn_w_up_2", m, i * BLK), KD)
                    load(g2(l, cb + 4) + it * 3, 1, tall("ffn_w_down_2", m, it * BLK, 2), 2)
                load(g2(l, cb + FFN - 1), 2, tall("ffn_w_down_2", m, (NI2 - 1) * BLK, 2), 2)

            with sp_.Fori(0, DEPTH) as l:
                ffn(l, 0, 0)
                for j, b in enumerate(ZORDER):
                    load(g2(l, FFN + j), j % RING, wide("w_in_2", l, b * BLK), KD)
                at = 0
                for j, k in enumerate(OUT2):
                    c = FFN + WIN + j
                    slot_free(g2(l, c))
                    sp_.dma_start(raw[:, c % RING, 0:k * D].rearrange("p (k n) -> p k n", k=k),
                                  tall("w_out_2", l, at, k)).then_inc(loaded[c % RING], 16)
                    at += k * P
                ffn(l, 1, FFN + WIN + len(OUT2))
            for t in range(T):
                sp_.wait_ge(x_scaled, 3 * DEPTH * T + (t + 1))
                sp_.dma_start(out[t * P:(t + 1) * P, :], xn[:, t, :]).then_inc(out_done, 16)
            sp_.wait_ge(out_done, 16 * T)

        @block.gpsimd
        def _(pool):
            n_order = [0]

            def link(ins_, base=0):
                n_order[0] += 1
                ins_.then_inc(pool_order, 1)
                pool.wait_ge(pool_order, base + n_order[0])
                pool.sem_inc(passed_pool, 1)

            nc.gpsimd.memset(bd[:, :, :, :], 0.0).then_inc(pads, 1)
            nc.gpsimd.memset(zero[:, :], 0.0).then_inc(zeroed, 1)
            pool.dma_start(rope_ax[:, :, :], ins["c_rope_ax"]).then_inc(tab_loaded, 16)
            pool.dma_start(rope_pt[:, :, :], ins["c_rope_pt"]).then_inc(tab_loaded, 16)
            pool.dma_start(logc[:, :, :], ins["c_logc"]).then_inc(tab_loaded, 16)
            pool.wait_ge(tab_loaded, 48)
            with pool.Fori(0, DEPTH) as l:
                pool.dma_start(qk_gain[:, 0:HD], ins["q_norm"][ds(l, 1), :].rearrange("o n -> (o n)").partition_broadcast(P))\
                    .then_inc(gain_loaded, 16)
                pool.dma_start(qk_gain[:, HD:], ins["k_norm"][ds(l, 1), :].rearrange("o n -> (o n)").partition_broadcast(P))\
                    .then_inc(gain_loaded, 16)
                pool.wait_ge(gain_loaded, l * 32 + 32)
                for t in range(T):
                    for h0, n, g0 in ((0, NHA, 0), (NHA, NKV, HD)):
                        span = slice(h0 * HD, (h0 + n) * HD)
                        gain = qk_gain[:, g0:g0 + HD]
                        nc.gpsimd.tensor_tensor(
                            cg[:, t, span].rearrange("p (h d) -> p h d", d=HD),
                            rope_ax[:, t, 0:HD].unsqueeze(1).broadcast_to((P, n, HD)),
                            gain.unsqueeze(1).broadcast_to((P, n, HD)), ALU.mult).then_inc(rope_tab, 1)
                        for half in range(2):
                            for ax in range(2):
                                at = 32 * ax + 16 * half
                                other = 32 * ax + 16 * (1 - half)
                                nc.gpsimd.tensor_tensor(
                                    sg[:, t, span].rearrange("p (h d) -> p h d", d=HD)[:, :, at:at + 16],
                                    rope_ax[:, t, HD + at:HD + at + 16].unsqueeze(1).broadcast_to((P, n, 16)),
                                    gain[:, other:other + 16].unsqueeze(1).broadcast_to((P, n, 16)),
                                    ALU.mult).then_inc(rope_tab, 1)
                pool.wait_ge(pv_done, l * 16 + 16)

            def affine_and_scale(norm, bias, base, n_gb):
                pool.wait_ge(gb_loaded, n_gb)
                for t in range(T):
                    pool.wait_ge(xn_ready, norm * T + (t + 1))
                    pool.wait_ge(xT, norm * T + (t + 1))
                    link(nc.gpsimd.tensor_tensor(xn[:, t, :], xn[:, t, :], g_bc[:, :], ALU.mult), base)
                    if bias:
                        link(nc.gpsimd.tensor_tensor(xn[:, t, :], xn[:, t, :], b_bc[:, :], ALU.add), base)
                    nc.gpsimd.tensor_scalar(x_tok[:, t, :], xn[:, t, :], ALPHA, None, ALU.mult).then_inc(x_scaled, 1)

            def load_gb(row):
                pool.dma_start(g_bc[:, :], ins["ln_g_2"][ds(row, 1), :].rearrange("o n -> (o n)").partition_broadcast(P))\
                    .then_inc(gb_loaded, 16)
                pool.dma_start(b_bc[:, :], ins["ln_b_2"][ds(row, 1), :].rearrange("o n -> (o n)").partition_broadcast(P))\
                    .then_inc(gb_loaded, 16)

            pool.dma_start(g_bc[:, :], ins["final_norm"].partition_broadcast(P)).then_inc(gb_loaded, 16)
            affine_and_scale(2 * DEPTH, False, 0, 16)
            base0 = n_order[0]
            with pool.Fori(0, DEPTH) as l:
                base = l * ORDP
                pool.dma_start(sgu_rows[:, :, :], ins["sgu_w_2"][ds(l, 1), :, :, :].rearrange("o h t s -> t (o h) s"))\
                    .then_inc(mix_w, 16)
                for n, name in enumerate(("sgu_ln_g_2", "sgu_ln_b_2")):
                    pool.dma_start(sgu_gb[:, n, :], ins[name][ds(l, 1), :].rearrange("o n -> (o n)").partition_broadcast(P))\
                        .then_inc(mix_w, 16)
                pool.wait_ge(pads, 1)
                for n, name in enumerate(("rg_w_a_2", "rg_w_i_2")):
                    for odd in range(2):
                        pool.dma_start(bd[64 * odd:64 * odd + 64, n, :, 64 * odd:64 * odd + 64],
                                       ins[name][ds(l, 1), odd::2, :, :].rearrange("o h d e -> d (o h) e"))\
                            .then_inc(mix_bd, 16)
                pool.wait_ge(mix_w, l * 48 + 48)
                pool.sem_inc(passed_pool, 1)
                nc.gpsimd.affine_select(out=sgu_rows[:, :, :], in_=sgu_rows[:, :, :], pattern=[[0, AH], [-1, P]],
                                        compare_op=ALU.is_ge, fill=0.0, base=0, channel_multiplier=1).then_inc(sgu_masked, 1)
                for j in range(3):
                    load_gb(l * 3 + j)
                    affine_and_scale(l * 3 + (2 * DEPTH + 1 + j), True, base, l * 96 + (16 + 32 * (j + 1)))
                assert n_order[0] - base0 == ORDP, n_order[0] - base0

        @block.scalar
        def _(act):
            def width(c, outs, at):
                return outs[c - at] * D if at <= c < at + len(outs) else CW

            def split_hi(g, rnd, slot, w=CW):
                act.wait_ge(loaded[slot], rnd * 16)
                act.wait_ge(used, g + 1)
                nc.scalar.activation(w_hi[:, slot, 0:w], raw[:, slot, 0:w], ACT.Copy).then_inc(hi_done, 1)

            def split1(l, c, it=0):
                if c < CH1:
                    split_hi(g1(l, c) + it * 6, round1(l, c) + it * 2, c % RING)

            def split2(l, c, it=0):
                if c < CH2:
                    split_hi(g2(l, c) + it * 3, round2(l, c) + it, c % RING, width(c, OUT2, FFN + WIN))

            def sum_squares(norm):
                for t in range(T):
                    act.wait_ge(x_done, norm * T + (t + 1))
                    nc.scalar.activation(xn[:, t, :], x_tok[:, t, :], ACT.Square,
                                         accum_out=ss[:, t:t + 1]).then_inc(sq_sum, 1)

            def turned(norm, gain, bias=None):
                act.wait_ge(xT, norm * T + T)
                for k in range(KD):
                    nc.scalar.activation(a_hi[:, k, :], acc_flat[:, k * SEQ:(k + 1) * SEQ], ACT.Identity,
                                         bias=0.0 if bias is None else cols[:, ds(bias + k, 1)],
                                         scale=cols[:, ds(gain + k, 1)]).then_inc(aT_hi, 1)

            def evac_proj(l, c):
                act.wait_ge(used, g1(l, c) + 4)
                nc.scalar.activation(proj[:, :, c * BLK:(c + 1) * BLK],
                                     work[:, c % 2, :].rearrange("p (t n) -> p t n", t=T), ACT.Copy).then_inc(proj_ready, 1)

            def attend(l, e):
                act.wait_ge(nmax_ready, l * 16 + (e + 1))
                if e >= 2:
                    act.wait_ge(pT_ps, l * 16 + (e - 1))
                for t in range(T):
                    src = work[:, 2 + e % 2, t * SEQ:(t + 1) * SEQ] if e < NHA else masked[:, e % 2, t * SEQ:(t + 1) * SEQ]
                    last = nc.scalar.activation(prob[:, e % 2, t * SEQ:(t + 1) * SEQ], src, ACT.Exp,
                                                bias=nmax[:, HEADS[e], t:t + 1], scale=SCALE if e < NHA else 1.0,
                                                accum_out=rsum[:, HEADS[e], t:t + 1])
                last.then_inc(exp_done, 1)

            def evac_pT(l, e):
                act.wait_ge(pT_ps, l * 16 + (e + 1))
                if e >= 2:
                    act.wait_ge(pv_done, l * 16 + (e - 1))
                nc.scalar.activation(probT[:, e % 2, :], work[:, e % 2, :], ACT.Copy).then_inc(pTB, 1)

            def y_squares(l, half):
                for t in range(T):
                    act.wait_ge(y_ready, l * 4 + (2 * half + t + 1))
                    nc.scalar.activation(sqs[:, t, 0:512], y_tok[:, t, half * 512:half * 512 + 512], ACT.Square,
                                         accum_out=ssy[:, 2 * half + t:2 * half + t + 1]).then_inc(y_sq, 1)

            def y_turned(l, half):
                act.wait_ge(yT_ps, l * 2 + (half + 1))
                src = (acc_flat[:, 1024:2048], work_flat[:, 0:1024])[half]
                for k in range(4):
                    nc.scalar.activation(a_hi[:, 4 * half + k, :], src[:, k * SEQ:(k + 1) * SEQ], ACT.Identity, bias=0.0,
                                         scale=cols[:, ds(l * C1 + (2 * KD + 4 * half + k), 1)]).then_inc(yT_hi, 1)

            act.wait_ge(cols_ready, 1)
            act.wait_ge(lam_abs, 1)
            nc.scalar.activation(sp[:, 1, :], sp[:, 0, :], ACT.Exp, scale=-1.0).then_inc(lam_exp, 1)
            with act.Fori(0, DEPTH) as l:
                for c in range(RING):
                    split1(l, c)
                sum_squares(l * 2)
                turned(l * 2, l * C1)
                for kind, n in PLAN1:
                    if kind == "chunk":
                        evac_proj(l, n)
                        split1(l, n + RING)
                    elif kind == "ropeA":
                        act.wait_ge(proj_ready, l * WIN + 3)
                        for t in range(T):
                            nc.scalar.activation(sqs[:, t, :], proj[:, t, 0:QKA], ACT.Square).then_inc(qk_sq, 1)
                    elif kind == "tA":
                        act.wait_ge(qkA_ps, l + 1)
                        nc.scalar.activation(qkTA[:, :, :].rearrange("p a b -> p (a b)"), acc_flat[:, 0:5 * SEQ], ACT.Copy)\
                            .then_inc(qkA_T, 1)
                    elif kind == "tB":
                        act.wait_ge(qkB_ps, l + 1)
                        nc.scalar.activation(qkTB[:, 0:4, :].rearrange("p a b -> p (a b)"), acc_flat[:, 0:1024], ACT.Copy)\
                            .then_inc(qB_T, 1)
                    elif kind == "score":
                        attend(l, n)
                    elif kind == "turn" and n >= NHA:
                        evac_pT(l, n)
                    elif kind == "ynorm":
                        y_squares(l, n)
                    elif kind == "yturn":
                        y_turned(l, n)
                for j in range(len(OUT1)):
                    split1(l, WIN + j + RING)
                sum_squares(l * 2 + 1)
                turned(l * 2 + 1, l * C1 + KD)

                def relu_u(l, i):
                    if not (isinstance(i, int) and i == 0):
                        act.wait_ge(h1_sq, l * NI1 + i)
                    nc.scalar.activation(relu[:, :], work[:, 0, :], ACT.Relu).then_inc(relu_done, 1)

                def hidden_hi(l, i, slot):
                    act.wait_ge(h1_sq, l * NI1 + i + 1)
                    nc.scalar.activation(h_hi[:, slot, :], hid[:, :], ACT.Copy).then_inc(h1_hi, 1)

                act.wait_ge(used, g1(l, MLP0) + 4)
                relu_u(l, 0)
                split1(l, MLP0 + 3)
                hidden_hi(l, 0, 0)

                def mlp_body(it, guard):
                    for j in range(3):
                        i, c = it * 3 + (1 + j), MLP0 + 1 + 2 * j
                        last = c + 6 * guard
                        act.wait_ge(used, g1(l, c) + it * 6 + 4)
                        relu_u(l, i)
                        if last + 3 < CH1:
                            split1(l, c + 3, it)
                        hidden_hi(l, i, (1 + j) % 3)
                        if last + 4 < CH1:
                            split1(l, c + 4, it)

                with act.Fori(0, (NI1 - 1) // 3 - 1) as it:
                    mlp_body(it, 0)
                mlp_body((NI1 - 1) // 3 - 1, (NI1 - 1) // 3 - 1)

            sum_squares(2 * DEPTH)
            turned(2 * DEPTH, FIN0)

            def ffn(l, f, cb):
                def silu(i):
                    if not (isinstance(i, int) and i == 0):
                        act.wait_ge(h2_f, (l * 2 + f) * NI2 + i)
                    nc.scalar.activation(relu[:, :], work[:, 0, :], ACT.Silu).then_inc(silu_done, 1)

                def hidden_hi(i):
                    act.wait_ge(h2_f, (l * 2 + f) * NI2 + i + 1)
                    nc.scalar.activation(h_hi[:, 0, :], hid[:, :], ACT.Copy).then_inc(h2_hi, 1)

                act.wait_ge(used, g2(l, cb) + 4)
                silu(0)
                split2(l, cb + 3)
                split2(l, cb + 4)
                hidden_hi(0)

                def body(it, last):
                    i, c = it + 1, cb + 2
                    act.wait_ge(used, g2(l, c) + it * 3 + 4)
                    silu(i)
                    for n in (3, 4, 5):
                        if n == 5:
                            act.wait_ge(used, g2(l, c) + it * 3 + 6)
                            hidden_hi(i)
                        if not last or c + 3 * (NI2 - 2) + n < CH2:
                            split2(l, c + n, it)

                with act.Fori(0, NI2 - 2) as it:
                    body(it, False)
                body(NI2 - 2, True)

            with act.Fori(0, DEPTH) as l:
                norm0 = l * 3 + (2 * DEPTH + 1)
                gains = l * N2 + LN0
                mx = l * NM + MX0
                for c in range(RING):
                    split2(l, c)
                ffn(l, 0, 0)
                turned(norm0, gains, gains + 3 * KD)
                split2(l, FFN - 1 + RING)
                for j in range(WIN):
                    c = FFN + j
                    act.wait_ge(used, g2(l, c) + 4)
                    bank = work[:, j % 2, :]
                    if j < 2:
                        act.wait_ge(conv_pads, 2)
                        nc.scalar.activation(xrp[:, 2 * j:2 * j + 2, CONV_C - 1:], bank.rearrange("p (c s) -> p c s", c=2),
                                             ACT.Copy).then_inc(z_done, 1)
                    elif j < 4:
                        nc.scalar.activation((ug, vg)[j - 2], bank, ACT.Gelu_apprx_tanh).then_inc(z_done, 1)
                    elif j < 6:
                        nc.scalar.activation(gg[:, (j - 4) * 512:(j - 3) * 512], bank, ACT.Gelu_apprx_tanh).then_inc(z_done, 1)
                    elif j < 8:
                        nc.scalar.activation((bg, cgt)[j - 6], bank, ACT.Copy).then_inc(z_done, 1)
                    split2(l, c + RING)
                    if j == 5:
                        for n in range(2):
                            act.wait_ge(gate_ps, l * 2 + (n + 1))
                            src = (work_flat[:, 1024:2048], acc_flat[:, 0:1024])[n]
                            for i in range(CT):
                                nc.scalar.activation((r_gate, i_gate)[n][:, i * SEQ:(i + 1) * SEQ], src[:, i * SEQ:(i + 1) * SEQ],
                                                     ACT.Sigmoid, bias=cols[:, ds(mx + ((M_BA, M_BI)[n] + i), 1)])\
                                    .then_inc(sig_done, 1)
                        act.wait_ge(sig_done, l * 2 * CT + CT)
                        act.wait_ge(sp_ready, 1)
                        for i in range(CT):
                            nc.scalar.activation(th[:, i * SEQ:(i + 1) * SEQ], r_gate[:, i * SEQ:(i + 1) * SEQ], ACT.Tanh,
                                                 scale=sp[:, 3, ds(l * CT + i, 1)]).then_inc(th_done, 1)
                        act.wait_ge(th_pos, l + 1)
                        nc.scalar.activation(root, th, ACT.Sqrt, scale=4.0).then_inc(root_done, 1)
                    if j == 6:
                        act.wait_ge(yaT_ps, l + 1)
                        for k in range(2):
                            nc.scalar.activation(mixed(k)[0], acc_flat[:, 1536 + k * SEQ:1536 + (k + 1) * SEQ], ACT.Copy)\
                                .then_inc(y2_hi, 1)
                act.wait_ge(y2_f, l * 2 + 1)
                nc.scalar.activation(mixed(2, 2)[0], yb, ACT.Copy).then_inc(y2_hi, 1)
                act.wait_ge(y2_f, l * 2 + 2)
                nc.scalar.activation(mixed(4, 4)[0], r_gate, ACT.Copy).then_inc(y2_hi, 1)
                for j in range(len(OUT2)):
                    split2(l, FFN + WIN + j + RING)
                turned(norm0 + 1, gains + KD, gains + 4 * KD)
                ffn(l, 1, FFN + WIN + len(OUT2))
                turned(norm0 + 2, gains + 2 * KD, gains + 5 * KD)

        @block.vector
        def _(dve):
            order = {"n": 0, "base": 0}

            def link(ins_):
                order["n"] += 1
                ins_.then_inc(dve_order, 1)
                dve.wait_ge(dve_order, order["base"] + order["n"])

            def width(c, outs, at):
                return outs[c - at] * D if at <= c < at + len(outs) else CW

            def split_lo(g, slot, w=CW):
                dve.wait_ge(hi_done, g + 1)
                nc.vector.tensor_tensor(w_lo[:, slot, 0:w], raw[:, slot, 0:w], w_hi[:, slot, 0:w].bitcast(f32), ALU.subtract)\
                    .then_inc(lo_done, 1)

            def split1(l, c, it=0):
                if c < CH1:
                    split_lo(g1(l, c) + it * 6, c % RING)

            def split2(l, c, it=0):
                if c < CH2:
                    split_lo(g2(l, c) + it * 3, c % RING, width(c, OUT2, FFN + WIN))

            def rsqrt(dst, src, n, scale, eps):
                v, y, h, b = (nwt[:, r, 0:n] for r in range(4))
                link(nc.vector.tensor_scalar(v, src, scale, eps, ALU.mult, ALU.add))
                link(nc.vector.tensor_scalar(y.bitcast(i32), v.bitcast(i32), -0.5, float(0x5f3759df), ALU.mult, ALU.add))
                link(nc.vector.tensor_scalar(h, v, -0.5, None, ALU.mult))
                for step in range(3):
                    if n == 1:
                        link(nc.vector.tensor_scalar(b, y, y, h, ALU.mult, ALU.mult))
                    else:
                        link(nc.vector.tensor_tensor(b, y, y, ALU.mult))
                        link(nc.vector.tensor_tensor(b, b, h, ALU.mult))
                    link(nc.vector.scalar_tensor_tensor(dst if step == 2 else y, b, 1.5, y, ALU.add, ALU.mult))

            def rms(norm):
                for t in range(T):
                    dve.wait_ge(sq_sum, norm * T + (t + 1))
                    rsqrt(rstd[:, t:t + 1], ss[:, t:t + 1], 1, 1.0 / D, RMS_EPS)
                    nc.vector.tensor_scalar(xn[:, t, :], x_tok[:, t, :], rstd[:, t:t + 1], None, ALU.mult).then_inc(xn_ready, 1)

            def turned(norm, gain):
                for k in range(KD):
                    dve.wait_ge(aT_hi, norm * KD + (k // 2 * 2 + 2))
                    nc.vector.scalar_tensor_tensor(a_lo[:, k, :], acc_flat[:, k * SEQ:(k + 1) * SEQ], cols[:, ds(gain + k, 1)],
                                                   a_hi[:, k, :].bitcast(f32), ALU.mult, ALU.subtract).then_inc(aT_lo, 1)

            def turned_ln(norm, gain, bias):
                for k in range(KD):
                    dve.wait_ge(aT_hi, norm * KD + (k // 2 * 2 + 2))
                    link(nc.vector.tensor_scalar(affine[:, k % 2, :], acc_flat[:, k * SEQ:(k + 1) * SEQ],
                                                 cols[:, ds(gain + k, 1)], cols[:, ds(bias + k, 1)], ALU.mult, ALU.add))
                    nc.vector.tensor_tensor(a_lo[:, k, :], affine[:, k % 2, :], a_hi[:, k, :].bitcast(f32), ALU.subtract)\
                        .then_inc(aT_lo, 1)

            def residual(g):
                dve.wait_ge(used, g + 4)
                for t in range(T):
                    nc.vector.tensor_tensor(x_tok[:, t, :], x_tok[:, t, :], acc_flat[:, t * D:(t + 1) * D], ALU.add)\
                        .then_inc(x_done, 1)

            def layer_norm(norm, g, factor):
                dve.wait_ge(used, g + 4)
                for t in range(T):
                    dve.wait_ge(x_scaled, (norm - 2 * DEPTH - 1) * T + (t + 1))
                    link(nc.vector.scalar_tensor_tensor(x_tok[:, t, :], acc_flat[:, t * D:(t + 1) * D], factor,
                                                        x_tok[:, t, :], ALU.mult, ALU.add))
                for t in range(T):
                    for n in range(2):
                        link(nc.vector.bn_stats(stat[:, t, n, :], x_tok[:, t, n * 512:(n + 1) * 512]))
                    dve.sem_inc(passed_dve, 1)
                    link(nc.vector.bn_aggr(mv[:, t, :], stat[:, t, :, :].rearrange("p a b -> p (a b)")))
                    rsqrt(rstd[:, t:t + 1], mv[:, t, 1:2], 1, 1.0, LN_EPS)
                    nc.vector.tensor_scalar(xn[:, t, :], x_tok[:, t, :], mv[:, t, 0:1], rstd[:, t:t + 1],
                                            ALU.subtract, ALU.mult).then_inc(xn_ready, 1)

            dve.sem_inc(lo_done, RING)
            dve.wait_ge(rowsT, 3)
            nc.vector.tensor_copy(cols[:, :], work[:, 0, 0:NCOL]).then_inc(cols_ready, 1)
            dve.wait_ge(cols_ready, 1)
            lam = cols[:, MX0:MX0 + DEPTH * NM].rearrange("p (l m) -> p l m", m=NM)[:, :, M_LAM:M_LAM + CT]
            sv = [sp[:, n, :].rearrange("p (l m) -> p l m", m=CT) for n in range(4)]
            nc.vector.scalar_tensor_tensor(sv[0], lam, -1.0, lam, ALU.mult, ALU.max).then_inc(lam_abs, 1)
            dve.wait_ge(lam_exp, 1)
            link(nc.vector.tensor_scalar(sp[:, 0, :], sp[:, 1, :], 2.0, None, ALU.add))
            link(nc.vector.reciprocal(sp[:, 2, :], sp[:, 0, :]))
            link(nc.vector.tensor_tensor(sp[:, 1, :], sp[:, 1, :], sp[:, 2, :], ALU.mult))
            link(nc.vector.tensor_tensor(sp[:, 0, :], sp[:, 1, :], sp[:, 1, :], ALU.mult))
            link(nc.vector.tensor_scalar(sp[:, 2, :], sp[:, 0, :], 1.0 / 17, None, ALU.mult))
            for odd in (15, 13, 11, 9, 7, 5, 3):
                link(nc.vector.scalar_tensor_tensor(sp[:, 2, :], sp[:, 2, :], 1.0 / odd, sp[:, 0, :], ALU.add, ALU.mult))
            link(nc.vector.scalar_tensor_tensor(sp[:, 2, :], sp[:, 2, :], 1.0, sp[:, 1, :], ALU.add, ALU.mult))
            link(nc.vector.tensor_scalar(sp[:, 2, :], sp[:, 2, :], RG_C, None, ALU.mult))
            link(nc.vector.tensor_scalar(sv[0], lam, -RG_C / 2, 0.0, ALU.mult, ALU.max))
            nc.vector.tensor_tensor(sp[:, 3, :], sp[:, 0, :], sp[:, 2, :], ALU.add).then_inc(sp_ready, 1)
            dve.wait_ge(x_loaded, 16 * T)
            dve.sem_inc(x_done, T)
            dve.wait_ge(tab_loaded, 48)
            setup = order["n"]

            def rope_global(l):
                for t in range(T):
                    dve.wait_ge(qk_sq, l * T + (t + 1))
                    link(nc.vector.tensor_reduce(ssA[:, t * 10:(t + 1) * 10], sqs[:, t, :].rearrange("p (h d) -> p h d", d=HD),
                                                 AX.X, ALU.add))
                rsqrt(rstdA[:, :], ssA[:, :], 20, 1.0 / HD, RMS_EPS)
                dve.wait_ge(rope_tab, l * 20 + 20)
                for t in range(T):
                    m = rope_b[:, t, :].rearrange("p (h d) -> p h d", d=HD)
                    link(nc.vector.tensor_tensor(m, proj[:, t, 0:QKA].rearrange("p (h d) -> p h d", d=HD),
                                                 rstdA[:, t * 10:(t + 1) * 10].unsqueeze(2).broadcast_to((P, NHA + NKV, HD)), ALU.mult))
                    nc.vector.tensor_tensor(rope_a[:, t, :], rope_b[:, t, :], cg[:, t, :], ALU.mult)
                    halves = [x[:, t, :].rearrange("p (a b c) -> p a b c", b=2, c=16) for x in (rope_b, sg, sqs)]
                    for b in range(2):
                        link(nc.vector.tensor_tensor(halves[2][:, :, b, :], halves[0][:, :, 1 - b, :], halves[1][:, :, b, :], ALU.mult))
                    for g in range(NKV):
                        q = slice(g * GROUP * HD, (g + 1) * GROUP * HD)
                        nc.vector.tensor_tensor(
                            qkA[:, t, 0:NHA * HD].rearrange("p (i g d) -> p g i d", g=NKV, d=HD)[:, g, :, :],
                            rope_a[:, t, q].rearrange("p (i d) -> p i d", d=HD),
                            sqs[:, t, q].rearrange("p (i d) -> p i d", d=HD), ALU.add)
                    nc.vector.tensor_tensor(qkA[:, t, NHA * HD:], rope_a[:, t, NHA * HD:], sqs[:, t, NHA * HD:], ALU.add)\
                        .then_inc(ropeA_done, 1)

            def rope_dilated(l):
                dve.wait_ge(qkA_ps, l + 1)
                dve.wait_ge(proj_ready, l * WIN + 7)
                for t in range(T):
                    x = proj[:, t, QB0:VB0].rearrange("p (h d) -> p h d", d=HD)
                    a = rope_a[:, t, 0:256].rearrange("p (h d) -> p h d", d=16)
                    b = rope_b[:, t, 0:256].rearrange("p (h d) -> p h d", d=16)
                    nc.vector.tensor_tensor(a, x[:, :, 0:16], rope_pt[:, t, 0:16].unsqueeze(1).broadcast_to((P, 2 * NHB, 16)), ALU.mult)
                    for n in range(2):
                        link(nc.vector.tensor_tensor(b[:, :, 8 * n:8 * n + 8], x[:, :, 8 - 8 * n:16 - 8 * n],
                                                     rope_pt[:, t, 16 + 8 * n:24 + 8 * n].unsqueeze(1).broadcast_to((P, 2 * NHB, 8)),
                                                     ALU.mult))
                    nc.vector.tensor_tensor(x[:, :, 0:16], a, b, ALU.add).then_inc(ropeB_done, 1)

            def row_max(l, e):
                dve.wait_ge(s_ready, l * 16 + (e + 1))
                h = HEADS[e]
                scores = work[:, 2 + e % 2, :]
                if e < NHA:
                    link(nc.vector.tensor_reduce(rinv[:, h, :], scores.rearrange("p (t s) -> p t s", t=T), AX.X, ALU.max))
                    nc.vector.tensor_scalar(nmax[:, h, :], rinv[:, h, :], -SCALE, None, ALU.mult).then_inc(nmax_ready, 1)
                else:
                    dve.wait_ge(exp_done, l * 16 + (e - 1))
                    link(nc.vector.scalar_tensor_tensor(masked[:, e % 2, :], scores, SCALE, logc_flat, ALU.mult, ALU.add))
                    nc.vector.tensor_reduce(nmax[:, h, :], masked[:, e % 2, :].rearrange("p (t s) -> p t s", t=T),
                                            AX.X, ALU.max, negate=True).then_inc(nmax_ready, 1)

            logc_flat = logc[:, :, :].rearrange("p t s -> p (t s)")

            def evac_pT(l, e):
                dve.wait_ge(pT_ps, l * 16 + (e + 1))
                if e >= 2:
                    dve.wait_ge(pv_done, l * 16 + (e - 1))
                nc.vector.tensor_copy(probT[:, e % 2, :], acc[:, e % 2, :]).then_inc(pTA, 1)

            def y_norm(l, half):
                dve.wait_ge(pv_done, l * 16 + (8 * half + 8))
                hs_ = slice(8 * half, 8 * half + 8)
                link(nc.vector.reciprocal(rinv[:, hs_, :], rsum[:, hs_, :]))
                for t in range(T):
                    y = y_tok[:, t, half * 512:half * 512 + 512].rearrange("p (h d) -> p h d", d=HD)
                    o = acc[:, (2, 0)[half] + t, :].rearrange("p (h d) -> p h d", d=HD)
                    nc.vector.tensor_tensor(y, o, rinv[:, hs_, t].unsqueeze(2).broadcast_to((P, 8, HD)), ALU.mult).then_inc(y_ready, 1)
                for t in range(T):
                    n = 2 * half + t
                    dve.wait_ge(y_sq, l * 4 + (n + 1))
                    rsqrt(rstdy[:, n:n + 1], ssy[:, n:n + 1], 1, 1.0 / 512, RMS_EPS)
                    y = y_tok[:, t, half * 512:half * 512 + 512]
                    nc.vector.tensor_scalar(y, y, rstdy[:, n:n + 1], None, ALU.mult).then_inc(yn_ready, 1)

            def y_turned(l, half):
                src = (acc_flat[:, 1024:2048], work_flat[:, 0:1024])[half]
                for k in range(4):
                    dve.wait_ge(yT_hi, l * 8 + (4 * half + k // 2 * 2 + 2))
                    nc.vector.scalar_tensor_tensor(a_lo[:, 4 * half + k, :], src[:, k * SEQ:(k + 1) * SEQ],
                                                   cols[:, ds(l * C1 + (2 * KD + 4 * half + k), 1)],
                                                   a_hi[:, 4 * half + k, :].bitcast(f32), ALU.mult, ALU.subtract).then_inc(yT_lo, 1)

            with dve.Fori(0, DEPTH) as l:
                order["n"], order["base"] = 0, l * ORD1 + setup
                for c in range(RING):
                    split1(l, c)
                rms(l * 2)
                turned(l * 2, l * C1)
                for kind, n in PLAN1:
                    if kind == "chunk":
                        split1(l, n + RING)
                    elif kind == "ropeA":
                        rope_global(l)
                    elif kind == "ropeB":
                        rope_dilated(l)
                    elif kind == "tB":
                        dve.wait_ge(qkB_ps, l + 1)
                        nc.vector.tensor_copy(qkTB[:, 4:8, :].rearrange("p a b -> p (a b)"), acc_flat[:, 1024:2048]).then_inc(kB_T, 1)
                    elif kind == "score":
                        row_max(l, n)
                    elif kind == "turn" and n < NHA:
                        evac_pT(l, n)
                    elif kind == "ynorm":
                        y_norm(l, n)
                    elif kind == "yturn":
                        y_turned(l, n)
                for j in range(len(OUT1)):
                    split1(l, WIN + j + RING)
                residual(g1(l, MLP0 - 1))
                rms(l * 2 + 1)
                turned(l * 2 + 1, l * C1 + KD)

                def square(l, i):
                    dve.wait_ge(relu_done, l * NI1 + i + 1)
                    if not (isinstance(i, int) and i == 0):
                        dve.wait_ge(h1_lo, l * NI1 + i)
                    nc.vector.tensor_tensor(hid[:, :], relu[:, :], relu[:, :], ALU.mult).then_inc(h1_sq, 1)

                def hidden_lo(l, i, slot):
                    dve.wait_ge(h1_hi, l * NI1 + i + 1)
                    nc.vector.tensor_tensor(h_lo[:, slot, :], hid[:, :], h_hi[:, slot, :].bitcast(f32), ALU.subtract).then_inc(h1_lo, 1)

                square(l, 0)
                split1(l, MLP0 + 3)
                hidden_lo(l, 0, 0)

                def mlp_body(it, guard):
                    for j in range(3):
                        i, c = it * 3 + (1 + j), MLP0 + 1 + 2 * j
                        last = c + 6 * guard
                        square(l, i)
                        if last + 3 < CH1:
                            split1(l, c + 3, it)
                        hidden_lo(l, i, (1 + j) % 3)
                        if last + 4 < CH1:
                            split1(l, c + 4, it)

                with dve.Fori(0, (NI1 - 1) // 3 - 1) as it:
                    mlp_body(it, 0)
                mlp_body((NI1 - 1) // 3 - 1, (NI1 - 1) // 3 - 1)
                residual(g1(l, CH1 - 1))
                assert order["n"] == ORD1, order["n"]

            order["n"], order["base"] = 0, setup + DEPTH * ORD1
            nc.vector.memset(xrp, 0.0).then_inc(conv_pads, 1)
            nc.vector.memset(cxp, 0.0).then_inc(conv_pads, 1)
            rms(2 * DEPTH)
            turned(2 * DEPTH, FIN0)
            before2 = setup + DEPTH * ORD1 + order["n"]

            def ffn(l, f, cb):
                def hidden(i):
                    dve.wait_ge(silu_done, (l * 2 + f) * NI2 + i + 1)
                    if not (isinstance(i, int) and i == 0):
                        dve.wait_ge(h2_lo, (l * 2 + f) * NI2 + i)
                    nc.vector.tensor_tensor(hid[:, :], relu[:, :], work[:, 1, :], ALU.mult).then_inc(h2_f, 1)

                def hidden_lo(i):
                    dve.wait_ge(h2_hi, (l * 2 + f) * NI2 + i + 1)
                    nc.vector.tensor_tensor(h_lo[:, 0, :], hid[:, :], h_hi[:, 0, :].bitcast(f32), ALU.subtract).then_inc(h2_lo, 1)

                split2(l, cb + 3)
                dve.wait_ge(used, g2(l, cb + 1) + 4)
                hidden(0)
                split2(l, cb + 4)
                hidden_lo(0)

                def body(it, last):
                    i, c = it + 1, cb + 2
                    for n in (3, 4, 5):
                        if n == 4:
                            dve.wait_ge(used, g2(l, c) + it * 3 + 5)
                            hidden(i)
                        if n == 5:
                            hidden_lo(i)
                        if not last or c + 3 * (NI2 - 2) + n < CH2:
                            split2(l, c + n, it)

                with dve.Fori(0, NI2 - 2) as it:
                    body(it, False)
                body(NI2 - 2, True)
                layer_norm_of = g2(l, cb + FFN - 1)
                return layer_norm_of

            with dve.Fori(0, DEPTH) as l:
                order["n"], order["base"] = 0, l * ORD2 + before2
                norm0 = l * 3 + (2 * DEPTH + 1)
                gains = l * N2 + LN0
                mx = l * NM + MX0
                for c in range(RING):
                    split2(l, c)
                layer_norm(norm0, ffn(l, 0, 0), 0.5)
                turned_ln(norm0, gains, gains + 3 * KD)
                split2(l, FFN - 1 + RING)
                dve.wait_ge(sgu_ps, l + 1)
                nc.vector.tensor_copy(sguT[:, :, :].rearrange("p a b -> p (a b)"), work[:, 2, :]).then_inc(sgu_T, 1)
                for j in range(WIN):
                    if j == 2:
                        dve.wait_ge(z_done, l * 8 + 2)
                        for i in range(CT):
                            for tap in range(CONV_C):
                                src, w = xrp[:, i, tap:tap + SEQ], cols[:, ds(mx + (M_CONV + tap * CT + i), 1)]
                                dst = xr[:, i * SEQ:(i + 1) * SEQ]
                                if tap == 0:
                                    link(nc.vector.tensor_scalar(dst, src, w, None, ALU.mult))
                                else:
                                    link(nc.vector.scalar_tensor_tensor(dst, src, w, dst, ALU.mult, ALU.add))
                            nc.vector.tensor_scalar(dst, dst, cols[:, ds(mx + (M_CB + i), 1)], None, ALU.add).then_inc(conv_done, 1)
                    if j == 4:
                        dve.wait_ge(z_done, l * 8 + 4)
                        for t in range(T):
                            v = vg[:, t * 256:(t + 1) * 256]
                            link(nc.vector.bn_stats(stat[:, t, 0, :], v))
                            dve.sem_inc(passed_dve, 1)
                            link(nc.vector.bn_aggr(mv[:, t, :], stat[:, t, 0, :]))
                        rsqrt(rstd[:, :], mv[:, :, 1], T, 1.0, LN_EPS)
                        dve.wait_ge(mix_w, l * 48 + 48)
                        for t in range(T):
                            v, w = vg[:, t * 256:(t + 1) * 256], vn[:, t * 256:(t + 1) * 256]
                            link(nc.vector.tensor_scalar(w, v, mv[:, t, 0:1], rstd[:, t:t + 1], ALU.subtract, ALU.mult))
                            link(nc.vector.tensor_tensor(w, w, sgu_gb[:, 0, :], ALU.mult))
                            nc.vector.tensor_tensor(w, w, sgu_gb[:, 1, :], ALU.add).then_inc(v_done, 1)
                    if j == 6:
                        dve.wait_ge(mix_ps, l + 1)
                        for h in range(AH):
                            dst, src, u = (x.rearrange("p (t c) -> p t c", t=T)[:, :, h * HD:(h + 1) * HD]
                                           for x in (ya, acc[:, 2, :], ug))
                            nc.vector.scalar_tensor_tensor(dst, src, cols[:, ds(mx + (M_SGB + h), 1)], u, ALU.add, ALU.mult)\
                                .then_inc(ya_done, 1)
                        dve.wait_ge(th_done, l * CT + CT)
                        nc.vector.tensor_scalar(th, th, 0.0, None, ALU.max).then_inc(th_pos, 1)
                        dve.wait_ge(th_pos, l + 1)
                        link(nc.vector.tensor_scalar(q_rec, th, 1.0, None, ALU.add))
                        link(nc.vector.reciprocal(q_rec, q_rec))
                        link(nc.vector.tensor_scalar(a_dec, q_rec, 2.0, -1.0, ALU.mult, ALU.add))
                        dve.wait_ge(sig_done, l * 2 * CT + 2 * CT)
                        link(nc.vector.tensor_tensor(i_gate, i_gate, xr, ALU.mult))
                    if j == 7:
                        for k in range(2):
                            dve.wait_ge(y2_hi, l * 4 + 2)
                            nc.vector.tensor_tensor(mixed(k)[1], acc_flat[:, 1536 + k * SEQ:1536 + (k + 1) * SEQ],
                                                    mixed(k)[0].bitcast(f32), ALU.subtract).then_inc(y2_lo, 1)
                        dve.wait_ge(root_done, l + 1)
                        link(nc.vector.tensor_tensor(q_rec, q_rec, root, ALU.mult))
                        link(nc.vector.tensor_tensor(q_rec, q_rec, i_gate, ALU.mult))
                        for i in range(CT):
                            span = slice(i * SEQ, (i + 1) * SEQ)
                            last = nc.vector.tensor_tensor_scan(hs[:, span], a_dec[:, span], q_rec[:, span], 0.0, ALU.mult, ALU.add)
                        link(last)
                    if j == 8:
                        dve.wait_ge(used, g2(l, FFN + 8) + 4)
                        dve.wait_ge(z_done, l * 8 + 8)
                        nc.vector.tensor_tensor(cxp[:, :, CONV_B - 1:], cgt.rearrange("p (c s) -> p c s", c=2),
                                                work[:, 0, :].rearrange("p (c s) -> p c s", c=2), ALU.mult).then_inc(cx_done, 1)
                        dve.wait_ge(cx_done, l + 1)
                        for i in range(2):
                            for tap in range(CONV_B):
                                src, w = cxp[:, i, tap:tap + SEQ], cols[:, ds(mx + (M_SC + tap * 2 + i), 1)]
                                dst = yb[:, i * SEQ:(i + 1) * SEQ]
                                if tap == 0:
                                    link(nc.vector.tensor_scalar(dst, src, w, None, ALU.mult))
                                else:
                                    link(nc.vector.scalar_tensor_tensor(dst, src, w, dst, ALU.mult, ALU.add))
                        nc.vector.tensor_tensor(yb, yb, bg, ALU.mult).then_inc(y2_f, 1)
                        nc.vector.tensor_tensor(r_gate, gg, hs, ALU.mult).then_inc(y2_f, 1)
                    split2(l, FFN + j + RING)
                dve.wait_ge(y2_hi, l * 4 + 3)
                dve.wait_ge(y2_f, l * 2 + 1)
                nc.vector.tensor_tensor(mixed(2, 2)[1], yb,
                                        mixed(2, 2)[0].bitcast(f32), ALU.subtract).then_inc(y2_lo, 1)
                dve.wait_ge(y2_hi, l * 4 + 4)
                dve.wait_ge(y2_f, l * 2 + 2)
                nc.vector.tensor_tensor(mixed(4, 4)[1], r_gate,
                                        mixed(4, 4)[0].bitcast(f32), ALU.subtract).then_inc(y2_lo, 1)
                for j in range(len(OUT2)):
                    split2(l, FFN + WIN + j + RING)
                layer_norm(norm0 + 1, g2(l, FFN + WIN + len(OUT2) - 1), 1.0)
                turned_ln(norm0 + 1, gains + KD, gains + 4 * KD)
                layer_norm(norm0 + 2, ffn(l, 1, FFN + WIN + len(OUT2)), 0.5)
                turned_ln(norm0 + 2, gains + 2 * KD, gains + 5 * KD)
                assert order["n"] == ORD2, order["n"]

        @block.tensor
        def _(pe):
            def chunk_ready(g):
                pe.wait_ge(lo_done, g + 4)

            def weights(slot, k, at, n):
                return [w[:, slot, k + at:k + at + n] for w in (w_hi, w_lo)]

            def product(dst, left, right, start, stop=False):
                (lh, ll), (rh, rl) = left, right
                nc.tensor.matmul(dst, lh, rh, start=start, stop=False, skip_group_check=True)
                nc.tensor.matmul(dst, lh, rl, start=False, stop=False, skip_group_check=True)
                return nc.tensor.matmul(dst, ll, rh, start=False, stop=stop, skip_group_check=True)

            def turn_norm(norm):
                for t in range(T):
                    pe.wait_ge(xn_ready, norm * T + (t + 1))
                    for k in range(KD):
                        at = k * SEQ + t * P
                        last = nc.tensor.transpose(acc_flat[:, at:at + P], xn[:, t, k * P:(k + 1) * P], ident[:, :])
                    last.then_inc(xT, 1)

            def by_tokens(g, slot, bank, norm=None):
                chunk_ready(g)
                for k in range(KD):
                    if norm is not None:
                        pe.wait_ge(aT_lo, norm * KD + (k + 1))
                    for t in range(T):
                        tok = slice(t * P, (t + 1) * P)
                        last = product(work[:, bank, t * BLK:(t + 1) * BLK], (a_hi[:, k, tok], a_lo[:, k, tok]),
                                       weights(slot, k * BLK, 0, BLK), start=(k == 0 and t == 0), stop=(k == KD - 1))
                last.then_inc(used, 1)

            def by_features(g, slot, bank, norm=None):
                chunk_ready(g)
                for k in range(KD):
                    if norm is not None:
                        pe.wait_ge(aT_lo, norm * KD + (k + 1))
                    for m in range(2):
                        last = product(work[:, bank, m * SEQ:(m + 1) * SEQ], weights(slot, k * BLK, m * P, P),
                                       (a_hi[:, k, :], a_lo[:, k, :]), start=(k == 0 and m == 0), stop=(k == KD - 1))
                last.then_inc(used, 1)

            def down(g, slot, left, nk, start=False, stop=False):
                chunk_ready(g)
                for k in range(nk):
                    hi, lo = left(k)
                    for t in range(T):
                        tok = slice(t * P, (t + 1) * P)
                        for n in range(2):
                            last = product(acc[:, 2 * t + n, :], (hi[:, tok], lo[:, tok]), weights(slot, k * D, n * 512, 512),
                                           start=start and k == 0, stop=stop and k == nk - 1)
                last.then_inc(used, 1)

            def open_sums():
                for b in range(4):
                    nc.tensor.matmul(acc[:, b, 0:2], zero[:, :], zero[:, 0:2], start=True, stop=False, skip_group_check=True)

            pe.sem_inc(used, RING)
            pe.wait_ge(id_loaded, 16)
            pe.wait_ge(zeroed, 1)
            pe.wait_ge(rows_loaded, 16 * sum(len(r) for r in ROWS))
            at = 0
            for n in range(3):
                nc.tensor.transpose(work[:, 0, at:at + NROWS[n]], rows[n][0:NROWS[n], :], ident[0:NROWS[n], 0:NROWS[n]])\
                    .then_inc(rowsT, 1)
                at += NROWS[n]
            pe.wait_ge(cols_ready, 1)

            def score(l, e):
                if e >= 2:
                    pe.wait_ge(exp_done, l * 16 + (e - 1))
                h = HEADS[e]
                if e < NHA:
                    g, i, qT, kT = h // GROUP, h % GROUP, qkTA, 4
                    if e == 0:
                        pe.wait_ge(qkA_T, l + 1)
                else:
                    g, i, qT = h % 2, (h - NHA) // 2, qkTB
                    kT = 4 + i
                    if e == NHA:
                        pe.wait_ge(qB_T, l + 1)
                        pe.wait_ge(kB_T, l + 1)
                rows_ = slice(HD * g, HD * g + HD)
                for t in range(T):
                    last = nc.tensor.matmul(work[:, 2 + e % 2, t * SEQ:(t + 1) * SEQ], qT[rows_, i, t * P:(t + 1) * P],
                                            qT[rows_, kT, :], start=True, stop=True)
                last.then_inc(s_ready, 1)

            def turn(l, e):
                pe.wait_ge(exp_done, l * 16 + (e + 1))
                bank = acc[:, e % 2, :] if e < NHA else work[:, e % 2, :]
                if e >= 2:
                    if e < NHA:
                        pe.wait_ge(pTA, l * 8 + (e - 1))
                    elif e >= NHA + 2:
                        pe.wait_ge(pTB, l * 8 + (e - NHA - 1))
                for kt in range(T):
                    for t in range(T):
                        last = nc.tensor.transpose(bank[:, kt * SEQ + t * P:kt * SEQ + (t + 1) * P],
                                                   prob[:, e % 2, t * SEQ + kt * P:t * SEQ + (kt + 1) * P], ident[:, :])
                last.then_inc(pT_ps, 1)

            def apply(l, e):
                h = HEADS[e]
                if e < NHA:
                    pe.wait_ge(pTA, l * 8 + (e + 1))
                    v0, b0 = VA0 + (h // GROUP) * HD, 2
                else:
                    pe.wait_ge(pTB, l * 8 + (e - NHA + 1))
                    v0, b0 = VB0 + (h - NHA) * HD, 0
                if e == 0:
                    pe.wait_ge(proj_ready, l * WIN + 3)
                if e == NHA:
                    pe.wait_ge(proj_ready, l * WIN + WIN)
                at = (h % NHA) * HD
                for t in range(T):
                    for kt in range(T):
                        last = nc.tensor.matmul(acc[:, b0 + t, at:at + HD], probT[:, e % 2, kt * SEQ + t * P:kt * SEQ + (t + 1) * P],
                                                proj[:, kt, v0:v0 + HD], start=(kt == 0), stop=(kt == T - 1))
                last.then_inc(pv_done, 1)

            with pe.Fori(0, DEPTH) as l:
                turn_norm(l * 2)
                for kind, n in PLAN1:
                    if kind == "chunk":
                        if n >= 2:
                            pe.wait_ge(proj_ready, l * WIN + (n - 1))
                        by_tokens(g1(l, n), n % RING, n % 2, l * 2 if n == 0 else None)
                    elif kind == "tA":
                        for t in range(T):
                            pe.wait_ge(ropeA_done, l * T + (t + 1))
                            for i in range(5):
                                last = nc.tensor.transpose(acc_flat[:, i * SEQ + t * P:i * SEQ + (t + 1) * P],
                                                           qkA[:, t, i * P:(i + 1) * P], ident[:, :])
                        last.then_inc(qkA_ps, 1)
                    elif kind == "tB":
                        pe.wait_ge(yT_lo, l * 8 + 4)
                        for t in range(T):
                            pe.wait_ge(ropeB_done, l * T + (t + 1))
                            for i in range(8):
                                last = nc.tensor.transpose(acc_flat[:, i * SEQ + t * P:i * SEQ + (t + 1) * P],
                                                           proj[:, t, QB0 + i * P:QB0 + (i + 1) * P], ident[:, :])
                        last.then_inc(qkB_ps, 1)
                    elif kind == "score":
                        score(l, n)
                    elif kind == "turn":
                        turn(l, n)
                    elif kind == "pv":
                        apply(l, n)
                    elif kind == "yturn":
                        dst = (acc_flat[:, 1024:2048], work_flat[:, 0:1024])[n]
                        for t in range(T):
                            pe.wait_ge(yn_ready, l * 4 + (2 * n + t + 1))
                            for k in range(4):
                                last = nc.tensor.transpose(dst[:, k * SEQ + t * P:k * SEQ + (t + 1) * P],
                                                           y_tok[:, t, n * 512 + k * P:n * 512 + (k + 1) * P], ident[:, :])
                        last.then_inc(yT_ps, 1)
                k0 = 0
                for j, nk in enumerate(OUT1):
                    pe.wait_ge(yT_lo, l * 8 + (k0 + nk))
                    down(g1(l, WIN + j), (WIN + j) % RING, lambda k, k0=k0: (a_hi[:, k0 + k, :], a_lo[:, k0 + k, :]), nk,
                         start=(j == 0), stop=(j == len(OUT1) - 1))
                    k0 += nk
                turn_norm(l * 2 + 1)

                def hidden(slot):
                    return lambda k: (h_hi[:, slot, k * SEQ:(k + 1) * SEQ], h_lo[:, slot, k * SEQ:(k + 1) * SEQ])

                by_features(g1(l, MLP0), MLP0 % RING, 0, l * 2 + 1)
                open_sums()
                with pe.Fori(0, (NI1 - 1) // 3) as it:
                    for j in range(3):
                        i, c = it * 3 + (1 + j), MLP0 + 1 + 2 * j
                        pe.wait_ge(relu_done, l * NI1 + i)
                        by_features(g1(l, c) + it * 6, c % RING, 0)
                        pe.wait_ge(h1_lo, l * NI1 + i)
                        down(g1(l, c + 1) + it * 6, (c + 1) % RING, hidden(j % 3), 2)
                pe.wait_ge(h1_lo, l * NI1 + NI1)
                down(g1(l, CH1 - 1), (CH1 - 1) % RING, hidden((NI1 - 1) % 3), 2, stop=True)

            turn_norm(2 * DEPTH)

            def ffn(l, f, cb, norm):
                def hidden(k):
                    return h_hi[:, 0, k * SEQ:(k + 1) * SEQ], h_lo[:, 0, k * SEQ:(k + 1) * SEQ]

                m = (l * 2 + f) * NI2
                by_features(g2(l, cb), 0, 0, norm)
                by_features(g2(l, cb + 1), 1, 1)
                open_sums()
                with pe.Fori(0, NI2 - 1) as it:
                    pe.wait_ge(silu_done, m + it + 1)
                    by_features(g2(l, cb + 2) + it * 3, 2, 0)
                    pe.wait_ge(h2_f, m + it + 1)
                    by_features(g2(l, cb + 3) + it * 3, 0, 1)
                    pe.wait_ge(h2_lo, m + it + 1)
                    down(g2(l, cb + 4) + it * 3, 1, hidden, 2)
                pe.wait_ge(h2_lo, m + NI2)
                down(g2(l, cb + FFN - 1), 2, hidden, 2, stop=True)

            with pe.Fori(0, DEPTH) as l:
                norm0 = l * 3 + (2 * DEPTH + 1)
                ffn(l, 0, 0, norm0 - 1)
                turn_norm(norm0)
                pe.wait_ge(sgu_masked, l + 1)
                for h in range(AH):
                    last = nc.tensor.transpose(work[:, 2, h * P:(h + 1) * P], sgu_rows[:, h, :], ident[:, :])
                last.then_inc(sgu_ps, 1)
                for j in range(WIN):
                    c = FFN + j
                    if j >= 2:
                        pe.wait_ge(z_done, l * 8 + (j - 1))
                    if j in (2, 3):
                        by_tokens(g2(l, c), c % RING, j % 2)
                    else:
                        by_features(g2(l, c), c % RING, j % 2, norm0 if j == 0 else None)
                    if j == 3:
                        pe.wait_ge(mix_bd, l * 64 + 64)
                        pe.wait_ge(conv_done, l * CT + CT)
                        pe.wait_ge(sgu_T, l + 1)
                        for n in range(2):
                            dst = (work_flat[:, 1024:2048], acc_flat[:, 0:1024])[n]
                            for i in range(CT):
                                last = nc.tensor.matmul(dst[:, i * SEQ:(i + 1) * SEQ], bd[:, n, i, :], xr[:, i * SEQ:(i + 1) * SEQ],
                                                        start=True, stop=True)
                            last.then_inc(gate_ps, 1)
                    if j == 5:
                        pe.wait_ge(v_done, l * T + T)
                        for t in range(T):
                            for h in range(AH):
                                at = t * 256 + h * HD
                                last = nc.tensor.matmul(acc[:, 2, at:at + HD], sguT[:, h, :], vn[:, at:at + HD], start=True, stop=True)
                        last.then_inc(mix_ps, 1)
                    if j == 6:
                        pe.wait_ge(ya_done, l * AH + AH)
                        for t in range(T):
                            for k in range(2):
                                last = nc.tensor.transpose(acc[:, 3, k * SEQ + t * P:k * SEQ + (t + 1) * P],
                                                           ya[:, t * 256 + k * P:t * 256 + (k + 1) * P], ident[:, :])
                        last.then_inc(yaT_ps, 1)
                k0 = 0
                for j, nk in enumerate(OUT2):
                    pe.wait_ge(y2_lo, l * 4 + (2, 3, 4, 4, 4, 4)[j])
                    if j == 0:
                        pe.wait_ge(sig_done, l * 2 * CT + 2 * CT)
                    down(g2(l, FFN + WIN + j), j % RING, lambda k, k0=k0: mixed(k0 + k), nk,
                         start=(j == 0), stop=(j == len(OUT2) - 1))
                    k0 += nk
                turn_norm(norm0 + 1)
                ffn(l, 1, FFN + WIN + len(OUT2), norm0 + 1)
                turn_norm(norm0 + 2)


def tables():
    pos = np.arange(SEQ)

    def rotation(p, half, theta):
        freqs = np.float32(theta) ** (-np.arange(half, dtype=np.float32) / np.float32(half))
        ang = p.astype(np.float32)[:, None] * freqs.astype(np.float32)[None, :]
        cos, sin = np.cos(ang.astype(np.float64)), np.sin(ang.astype(np.float64))
        return np.concatenate([cos, cos], -1), np.concatenate([-sin, sin], -1)

    def tiled(a):
        return np.ascontiguousarray(a.reshape(T, P, -1).transpose(1, 0, 2).astype(np.float32))

    (cr, sr), (cc, sc) = rotation(pos // 64, 16, 10000.0), rotation(pos % 64, 16, 10000.0)
    cp, sn = rotation(pos, 8, 500000.0)
    d = np.abs(pos[:, None] - pos[None, :])
    count = sum((d % dil == 0) & (d <= window // 2) for window, dil in ((128, 1), (512, 4), (2048, 16)))
    logc = np.where(count > 0, np.log(np.maximum(count, 1)), -1e30)
    return {"c_ident": np.eye(P, dtype=np.float32), "c_rope_ax": tiled(np.concatenate([cr, cc, sr, sc], -1)),
            "c_rope_pt": tiled(np.concatenate([cp, sn], -1)), "c_logc": tiled(logc)}


_INS = {
    "x": (SEQ, D), "norm1": (-1, P), "w_in": None, "q_norm": None, "k_norm": None, "out_norm_a": (-1, P), "out_norm_b": (-1, P),
    "w_out": None, "norm2": (-1, P), "w_mlp_in": None, "w_mlp_out": None, "final_norm": None, "ln_g_2": (-1, D), "ln_b_2": (-1, D),
    "ffn_w_gate_2": (2 * DEPTH, D, FF2), "ffn_w_up_2": (2 * DEPTH, D, FF2), "ffn_w_down_2": (2 * DEPTH, FF2, D), "w_in_2": None,
    "sgu_ln_g_2": None, "sgu_ln_b_2": None, "sgu_w_2": None, "sgu_b_2": (-1, P), "sconv_w_2": (-1, P), "rg_conv_w_2": (-1, P),
    "rg_conv_b_2": (-1, P), "rg_w_a_2": None, "rg_b_a_2": (-1, P), "rg_w_i_2": None, "rg_b_i_2": (-1, P), "rg_lambda_2": (-1, P),
    "w_out_2": None,
}


def kernel(**inputs):
    import concourse.bacc as _bacc
    from concourse.bass_utils import run_bass_kernel_spmd as _run

    nc = _bacc.Bacc("TRN2", target_bir_lowering=False, num_devices=1)
    arrays, ins = {}, {}
    for name, shape in _INS.items():
        a = np.ascontiguousarray(inputs[name])
        arrays[name] = a if shape is None else a.reshape(shape)
    arrays.update(tables())
    for name, a in arrays.items():
        ins[name] = nc.dram_tensor(name, a.shape, mybir.dt.from_np(a.dtype), kind="ExternalInput").ap()
    ins["ln_g_rows"] = ins["ln_g_2"].rearrange("r (k p) -> (r k) p", p=P)
    ins["ln_b_rows"] = ins["ln_b_2"].rearrange("r (k p) -> (r k) p", p=P)
    ins["final_norm_rows"] = ins["final_norm"].rearrange("(k p) -> k p", p=P)
    out = nc.dram_tensor("y", (SEQ, D), mybir.dt.float32, kind="ExternalOutput").ap()
    program(nc, ins, out)
    r = _run(nc, [arrays], core_ids=[0])
    return r.results[0]["y"].reshape(1, SEQ, D)
```

```python
import math
from contextlib import ExitStack

import concourse.bass as bass
import numpy as np
from concourse import mybir

P = 128
SEQ, D, DEPTH, HD = 256, 1024, 2, 64
T = SEQ // P
KD = D // P
FF1, FF2 = 4096, 2816
NHA, NKV, NHB = 8, 2, 8
GROUP = NHA // NKV
IN_W = 2304
QKA = (NHA + NKV) * HD
VA0 = QKA
QB0 = VA0 + NKV * HD
VB0 = QB0 + 2 * NHB * HD
SCALE = HD ** -0.5
RMS_EPS, LN_EPS = 1e-6, 1e-5
ALPHA = (2.0 * DEPTH) ** 0.25
AH, CONV_B, CONV_C, CT = 4, 3, 4, 4
RG_C = 8.0

RING, CW = 3, 2048
BLK = CW // KD
NI1, NI2 = FF1 // BLK, FF2 // BLK
WIN = IN_W // BLK
OUT1 = [2, 2, 2, 2]
OUT2 = [2, 1, 1, 1, 1, 2]
MLP0 = WIN + len(OUT1)
CH1 = MLP0 + 2 * NI1
FFN = 3 * NI2
CH2 = 2 * FFN + WIN + len(OUT2)
assert CH1 % RING == 0 and CH2 % RING == 0 and FFN % RING == 0
ZORDER = [7, 8, 0, 1, 5, 6, 2, 3, 4]

C1 = 3 * KD
N2 = 6 * KD
LN0 = DEPTH * C1 + N2
M_CONV, M_CB, M_BA, M_BI, M_LAM = 0, 16, 20, 24, 28
M_SC, M_SGB = 32, 38
NM = 42
MX0 = LN0 + DEPTH * N2
NCOL = MX0 + DEPTH * NM
ORD1, ORD2, ORDP = 68, 150, 6
HEADS = [0, 4, 1, 5, 2, 6, 3, 7] + list(range(8, 16))


def plan1():
    plan = [("chunk", 0), ("split", 3), ("chunk", 1), ("split", 4), ("chunk", 2), ("split", 5), ("ropeA", 0)]
    plan += [("chunk", 3), ("split", 6), ("chunk", 4), ("split", 7), ("chunk", 5), ("split", 8), ("tA", 0)]
    plan += [("chunk", 6), ("score", 0), ("score", 1), ("ropeB", 0), ("chunk", 7), ("tB", 0), ("split", 9)]
    plan += [("score", 2), ("score", 3), ("chunk", 8), ("turn", 0), ("turn", 1), ("pv", 0), ("pv", 1)]
    between = {5: ("split", 10), 7: ("split", 11), NHA + 2: ("ynorm", 0), NHA + 4: ("yturn", 0)}
    for step in range(4, NHA + NHB + 3):
        plan += [(kind, e) for kind, e, least in (("score", step, 4), ("turn", step - 2, 2), ("pv", step - 3, 2))
                 if least <= e < NHA + NHB]
        plan += [between[step]] if step in between else []
    return plan + [("ynorm", 1), ("out", 0), ("yturn", 1)]


PLAN1 = plan1()
ROWS = [
    [(name, l, n) for l in range(DEPTH) for name, n in (("norm1", 8), ("norm2", 8), ("out_norm_a", 4), ("out_norm_b", 4))],
    [(name, l, 24) for l in range(DEPTH) for name in ("ln_g_2", "ln_b_2")],
    [(name, l, n) for l in range(DEPTH) for name, n in (
        ("rg_conv_w_2", 16), ("rg_conv_b_2", 4), ("rg_b_a_2", 4), ("rg_b_i_2", 4), ("rg_lambda_2", 4), ("sconv_w_2", 6), ("sgu_b_2", 4))]
    + [("final_norm", 0, 8)],
]
NROWS = [DEPTH * C1, DEPTH * N2, DEPTH * NM + KD]
LAST_LN = LN0 - N2 + 2 * KD


def program(nc, ins, out):
    f32, f32r, i32 = mybir.dt.float32, mybir.dt.float32r, mybir.dt.int32
    bf16 = mybir.dt.bfloat16
    ALU, ACT, AX = mybir.AluOpType, mybir.ActivationFunctionType, mybir.AxisListType
    ds = bass.ds
    ctx = ExitStack()
    with ctx:
        def sb(name, shape, dt=f32):
            return ctx.enter_context(nc.sbuf_tensor(name, shape, dt))

        def sem(name):
            return ctx.enter_context(nc.semaphore(name))

        raw = sb("raw", [P, RING, CW])
        w_hi = sb("w_hi", [P, RING, CW], f32r)
        w_lo = sb("w_lo", [P, RING, CW], f32r)
        x_tok = sb("x_tok", [P, T, D])
        xn = sb("xn", [P, T, D])
        a_hi = sb("a_hi", [P, KD, SEQ], f32r)
        a_lo = sb("a_lo", [P, KD, SEQ], f32r)
        relu = sb("relu", [P, 2 * SEQ])
        hid = sb("hid", [P, 2 * SEQ])
        h_hi = sb("h_hi", [P, 3, 2 * SEQ], f32r)
        h_lo = sb("h_lo", [P, 3, 2 * SEQ], f32r)
        proj = sb("proj", [P, T, IN_W])
        sqs = sb("sqs", [P, T, QKA])
        rope_a = sb("rope_a", [P, T, QKA])
        rope_b = sb("rope_b", [P, T, QKA])
        qkA = rope_b
        qkTB = sb("qkTB", [P, 8, SEQ])
        cg = sb("cg", [P, T, QKA])
        sg = sb("sg", [P, T, QKA])
        qkTA = cg[:, :, :].rearrange("p a b -> p (a b)").rearrange("p (i s) -> p i s", s=SEQ)
        masked = sb("masked", [P, 2, T * SEQ])
        prob = sb("prob", [P, 2, T * SEQ])
        probT = sb("probT", [P, 2, T * SEQ])
        y_tok = sb("y_tok", [P, T, D])
        ident = sb("ident", [P, P])
        rope_ax = sb("rope_ax", [P, T, 2 * HD])
        rope_pt = sb("rope_pt", [P, T, 32])
        logc = sb("logc", [P, T, SEQ])
        qk_gain = sb("qk_gain", [P, 2 * HD])
        g_bc = masked[:, :, :].rearrange("p a b -> p (a b)")
        b_bc = prob[:, :, :].rearrange("p a b -> p (a b)")
        rows = [y_tok[:, 0, n * P:(n + 1) * P] for n in range(3)]
        cols = sb("cols", [P, NCOL])
        zero = sb("zero", [P, P], bf16)
        ss = sb("ss", [P, 8])
        stat = sb("stat", [P, T, 2, 6])
        mv = sb("mv", [P, T, 2])
        nwt = sb("nwt", [P, 4, 20])
        rstd = sb("rstd", [P, T])
        rms2 = sb("rms2", [P, 2, T])
        ssA = sb("ssA", [P, 20])
        rstdA = sb("rstdA", [P, 20])
        ssy = sb("ssy", [P, 4])
        rstdy = sb("rstdy", [P, 4])
        nmax = sb("nmax", [P, 16, T])
        rsum = sb("rsum", [P, 16, T])
        rinv = sb("rinv", [P, 16, T])
        sgu_gb = sb("sgu_gb", [P, 2, 256])
        bd = sb("bd", [P, 2, CT, P])
        sp = sb("sp", [P, 4, DEPTH * CT])

        def part(tensor, n, width):
            return tensor[:, :, :].rearrange("p a b -> p (a b)")[:, n * width:(n + 1) * width]

        W4 = CT * SEQ
        xr = part(proj, 0, W4)
        r_gate = part(proj, 1, W4)
        i_gate = part(proj, 2, W4)
        th = part(proj, 3, W4)
        gg = part(y_tok, 0, W4)
        root = part(qkTB, 0, W4)
        a_dec = part(qkTB, 1, W4)
        q_rec = part(y_tok, 1, W4)
        hs = part(sqs, 0, W4)
        ug = part(cg, 0, 512)
        vg = part(cg, 1, 512)
        vn = part(sg, 0, 512)
        ya = part(sg, 1, 512)
        bg = part(rope_a, 0, 512)
        cgt = part(rope_a, 1, 512)
        yb = part(proj, 8, 512)
        xrp = part(rope_b, 0, CT * (SEQ + CONV_C - 1)).rearrange("p (c s) -> p c s", c=CT)
        cxp = part(probT, 0, 2 * (SEQ + CONV_B - 1)).rearrange("p (c s) -> p c s", c=2)
        sgu_rows = part(qkTB, 0, AH * P).rearrange("p (h s) -> p h s", h=AH)
        sguT = part(logc, 0, AH * P).rearrange("p (h s) -> p h s", h=AH)
        affine = relu[:, :].rearrange("p (a s) -> p a s", a=2)
        h_hi_flat = h_hi[:, :, :].rearrange("p a b -> p (a b)")
        h_lo_flat = h_lo[:, :, :].rearrange("p a b -> p (a b)")

        def mixed(k, n=1):
            if k < 4:
                return [h[:, k * SEQ:(k + n) * SEQ] for h in (h_hi_flat, h_lo_flat)]
            return [a[:, k:k + n, :].rearrange("p a b -> p (a b)") for a in (a_hi, a_lo)]

        acc = ctx.enter_context(nc.psum_tensor("acc", [P, 4, 512], f32))
        work = ctx.enter_context(nc.psum_tensor("work", [P, 4, 512], f32))

        def turned_bank(e):
            return (acc if e < 2 else work)[:, e % 2, :]

        acc_flat = acc[:, :, :].rearrange("p a b -> p (a b)")
        work_flat = work[:, :, :].rearrange("p a b -> p (a b)")

        loaded = [sem(f"loaded{s}") for s in range(RING)]
        hi_done, lo_done, used = sem("hi_done"), sem("lo_done"), sem("used")
        x_loaded, id_loaded, tab_loaded, rows_loaded = (sem(n) for n in ("x_loaded", "id_loaded", "tab_loaded", "rows_loaded"))
        rowsT, cols_ready, zeroed, pads, conv_pads = (sem(n) for n in ("rowsT", "cols_ready", "zeroed", "pads", "conv_pads"))
        lam_abs, lam_exp, sp_ready = (sem(n) for n in ("lam_abs", "lam_exp", "sp_ready"))
        sums, x_done, sq_sum, xn_ready, xT, aT_hi, aT_lo, rstd_ready = (
            sem(n) for n in ("sums", "x_done", "sq_sum", "xn_ready", "xT", "aT_hi", "aT_lo", "rstd_ready"))
        gb_loaded, x_affine, x_scaled, pool_order = (sem(n) for n in ("gb_loaded", "x_affine", "x_scaled", "pool_order"))
        dve_order = sem("dve_order")
        gain_loaded, rope_tab, proj_ready, qk_sq, ropeA_done, ropeB_done = (
            sem(n) for n in ("gain_loaded", "rope_tab", "proj_ready", "qk_sq", "ropeA_done", "ropeB_done"))
        qkA_ps, qkA_T, qkB_ps, qB_T, kB_T = (sem(n) for n in ("qkA_ps", "qkA_T", "qkB_ps", "qB_T", "kB_T"))
        s_ready, nmax_ready, exp_done, pT_ps, pTA, pTB, pv_done = (
            sem(n) for n in ("s_ready", "nmax_ready", "exp_done", "pT_ps", "pTA", "pTB", "pv_done"))
        y_ready, y_sq, yT_ps, yT_hi, yT_lo = (sem(n) for n in ("y_ready", "y_sq", "yT_ps", "yT_hi", "yT_lo"))
        relu_done, h1_sq, h1_hi, h1_lo = (sem(n) for n in ("relu_done", "h1_sq", "h1_hi", "h1_lo"))
        silu_done, h2_f, h2_hi, h2_lo = (sem(n) for n in ("silu_done", "h2_f", "h2_hi", "h2_lo"))
        mix_w, mix_bd, sgu_masked, sgu_ps, sgu_T = (sem(n) for n in ("mix_w", "mix_bd", "sgu_masked", "sgu_ps", "sgu_T"))
        z_done, cx_done, conv_done, gate_ps, sig_done, th_done, th_pos, root_done = (
            sem(n) for n in ("z_done", "cx_done", "conv_done", "gate_ps", "sig_done", "th_done", "th_pos", "root_done"))
        v_done, mix_ps, ya_done, yaT_ps, y2_f, y2_hi, y2_lo = (
            sem(n) for n in ("v_done", "mix_ps", "ya_done", "yaT_ps", "y2_f", "y2_hi", "y2_lo"))
        out_done = sem("out_done")
        passed_sp, passed_pool, passed_dve = sem("passed_sp"), sem("passed_pool"), sem("passed_dve")

        BASE2 = DEPTH * CH1

        def g1(l, c):
            return l * CH1 + c

        def g2(l, c):
            return l * CH2 + (BASE2 + c)

        def round1(l, c):
            return l * (CH1 // RING) + (c // RING + 1)

        def round2(l, c):
            return l * (CH2 // RING) + (BASE2 // RING + c // RING + 1)

        block = ctx.enter_context(nc.Block())

        @block.sync
        def _(sp_):
            for t in range(T):
                sp_.dma_start(x_tok[:, t, :], ins["x"][t * P:(t + 1) * P, :]).then_inc(x_loaded, 16)

            def slot_free(g):
                sp_.wait_ge(lo_done, g + 1)
                sp_.sem_inc(passed_sp, 1)

            def load(g, slot, src, k):
                slot_free(g)
                sp_.dma_start(raw[:, slot, :].rearrange("p (k n) -> p k n", k=k), src).then_inc(loaded[slot], 16)

            def wide(name, l, at):
                return ins[name][ds(l, 1), :, ds(at, BLK)].rearrange("o (k p) n -> p (o k) n", p=P)

            def tall(name, l, at, k):
                return ins[name][ds(l, 1), ds(at, k * P), :].rearrange("o (k p) n -> p (o k) n", p=P)

            with sp_.Fori(0, DEPTH) as l:
                for c in range(WIN):
                    load(g1(l, c), c % RING, wide("w_in", l, c * BLK), KD)
                at = 0
                for j, k in enumerate(OUT1):
                    load(g1(l, WIN + j), (WIN + j) % RING, tall("w_out", l, at, k), k)
                    at += k * P
                load(g1(l, MLP0), MLP0 % RING, wide("w_mlp_in", l, 0), KD)
                with sp_.Fori(0, (NI1 - 1) // 3) as it:
                    for j in range(3):
                        i, c = it * 3 + (1 + j), MLP0 + 1 + 2 * j
                        load(g1(l, c) + it * 6, c % RING, wide("w_mlp_in", l, i * BLK), KD)
                        load(g1(l, c + 1) + it * 6, (c + 1) % RING, tall("w_mlp_out", l, (i - 1) * BLK, 2), 2)
                load(g1(l, CH1 - 1), (CH1 - 1) % RING, tall("w_mlp_out", l, (NI1 - 1) * BLK, 2), 2)

            def ffn(l, f, cb):
                m = l * 2 + f
                load(g2(l, cb), 0, wide("ffn_w_gate_2", m, 0), KD)
                load(g2(l, cb + 1), 1, wide("ffn_w_up_2", m, 0), KD)
                with sp_.Fori(0, NI2 - 1) as it:
                    i = it + 1
                    load(g2(l, cb + 2) + it * 3, 2, wide("ffn_w_gate_2", m, i * BLK), KD)
                    load(g2(l, cb + 3) + it * 3, 0, wide("ffn_w_up_2", m, i * BLK), KD)
                    load(g2(l, cb + 4) + it * 3, 1, tall("ffn_w_down_2", m, it * BLK, 2), 2)
                load(g2(l, cb + FFN - 1), 2, tall("ffn_w_down_2", m, (NI2 - 1) * BLK, 2), 2)

            with sp_.Fori(0, DEPTH) as l:
                ffn(l, 0, 0)
                for j, b in enumerate(ZORDER):
                    load(g2(l, FFN + j), j % RING, wide("w_in_2", l, b * BLK), KD)
                at = 0
                for j, k in enumerate(OUT2):
                    c = FFN + WIN + j
                    slot_free(g2(l, c))
                    sp_.dma_start(raw[:, c % RING, 0:k * D].rearrange("p (k n) -> p k n", k=k),
                                  tall("w_out_2", l, at, k)).then_inc(loaded[c % RING], 16)
                    at += k * P
                ffn(l, 1, FFN + WIN + len(OUT2))
            for c in range(2):
                slot_free(BASE2 + DEPTH * CH2 + c)
                sp_.sem_inc(loaded[c], 16)
            for t in range(T):
                sp_.wait_ge(x_affine, 3 * DEPTH * T + (t + 1))
                sp_.dma_start(out[t * P:(t + 1) * P, :], xn[:, t, :]).then_inc(out_done, 16)
            sp_.wait_ge(out_done, 16 * T)

        @block.gpsimd
        def _(pool):
            n_order = [0]

            def link(ins_, base=0):
                n_order[0] += 1
                ins_.then_inc(pool_order, 1)
                pool.wait_ge(pool_order, base + n_order[0])
                pool.sem_inc(passed_pool, 1)

            nc.gpsimd.memset(bd[:, :, :, :], 0.0).then_inc(pads, 1)
            nc.gpsimd.memset(zero[:, :], 0.0).then_inc(zeroed, 1)
            pool.dma_start(rope_ax[:, :, :], ins["c_rope_ax"]).then_inc(tab_loaded, 16)
            pool.dma_start(rope_pt[:, :, :], ins["c_rope_pt"]).then_inc(tab_loaded, 16)
            pool.dma_start(logc[:, :, :], ins["c_logc"]).then_inc(tab_loaded, 16)
            pool.wait_ge(tab_loaded, 48)
            with pool.Fori(0, DEPTH) as l:
                pool.dma_start(qk_gain[:, 0:HD], ins["q_norm"][ds(l, 1), :].rearrange("o n -> (o n)").partition_broadcast(P))\
                    .then_inc(gain_loaded, 16)
                pool.dma_start(qk_gain[:, HD:], ins["k_norm"][ds(l, 1), :].rearrange("o n -> (o n)").partition_broadcast(P))\
                    .then_inc(gain_loaded, 16)
                pool.wait_ge(gain_loaded, l * 32 + 32)
                for t in range(T):
                    for h0, n, g0 in ((0, NHA, 0), (NHA, NKV, HD)):
                        span = slice(h0 * HD, (h0 + n) * HD)
                        gain = qk_gain[:, g0:g0 + HD]
                        nc.gpsimd.tensor_tensor(
                            cg[:, t, span].rearrange("p (h d) -> p h d", d=HD),
                            rope_ax[:, t, 0:HD].unsqueeze(1).broadcast_to((P, n, HD)),
                            gain.unsqueeze(1).broadcast_to((P, n, HD)), ALU.mult).then_inc(rope_tab, 1)
                        for half in range(2):
                            for ax in range(2):
                                at = 32 * ax + 16 * half
                                other = 32 * ax + 16 * (1 - half)
                                nc.gpsimd.tensor_tensor(
                                    sg[:, t, span].rearrange("p (h d) -> p h d", d=HD)[:, :, at:at + 16],
                                    rope_ax[:, t, HD + at:HD + at + 16].unsqueeze(1).broadcast_to((P, n, 16)),
                                    gain[:, other:other + 16].unsqueeze(1).broadcast_to((P, n, 16)),
                                    ALU.mult).then_inc(rope_tab, 1)
                for c in range(WIN, WIN + RING):
                    pool.wait_ge(hi_done, g1(l, c) + 1)
                    pool.wait_ge(lo_done, g1(l, c) + 3)
                    nc.gpsimd.tensor_tensor(w_lo[:, c % RING, :], raw[:, c % RING, :], w_hi[:, c % RING, :].bitcast(f32),
                                            ALU.subtract).then_inc(lo_done, 1)
                pool.wait_ge(pv_done, l * 16 + 16)

            def affine_and_scale(norm, bias, base, n_gb):
                pool.wait_ge(gb_loaded, n_gb)
                for t in range(T):
                    pool.wait_ge(xn_ready, (norm - 2 * DEPTH) * 4 + (2 * t + 2))
                    pool.wait_ge(xT, norm * 8 + 4 * (t + 1))
                    last = nc.gpsimd.tensor_tensor(xn[:, t, :], xn[:, t, :], g_bc[:, :], ALU.mult)
                    if bias:
                        link(last, base)
                        last = nc.gpsimd.tensor_tensor(xn[:, t, :], xn[:, t, :], b_bc[:, :], ALU.add)
                    last.then_inc(x_affine, 1)
                    pool.wait_ge(x_affine, (norm - 2 * DEPTH) * T + (t + 1))
                    pool.sem_inc(passed_pool, 1)
                    nc.gpsimd.tensor_scalar(x_tok[:, t, :], xn[:, t, :], ALPHA, None, ALU.mult).then_inc(x_scaled, 1)

            def load_gb(row):
                pool.dma_start(g_bc[:, :], ins["ln_g_2"][ds(row, 1), :].rearrange("o n -> (o n)").partition_broadcast(P))\
                    .then_inc(gb_loaded, 16)
                pool.dma_start(b_bc[:, :], ins["ln_b_2"][ds(row, 1), :].rearrange("o n -> (o n)").partition_broadcast(P))\
                    .then_inc(gb_loaded, 16)

            pool.dma_start(g_bc[:, :], ins["final_norm"].partition_broadcast(P)).then_inc(gb_loaded, 16)
            affine_and_scale(2 * DEPTH, False, 0, 16)
            base0 = n_order[0]
            with pool.Fori(0, DEPTH) as l:
                base = l * ORDP
                pool.dma_start(sgu_rows[:, :, :], ins["sgu_w_2"][ds(l, 1), :, :, :].rearrange("o h t s -> t (o h) s"))\
                    .then_inc(mix_w, 16)
                for n, name in enumerate(("sgu_ln_g_2", "sgu_ln_b_2")):
                    pool.dma_start(sgu_gb[:, n, :], ins[name][ds(l, 1), :].rearrange("o n -> (o n)").partition_broadcast(P))\
                        .then_inc(mix_w, 16)
                pool.wait_ge(pads, 1)
                for n, name in enumerate(("rg_w_a_2", "rg_w_i_2")):
                    for odd in range(2):
                        pool.dma_start(bd[64 * odd:64 * odd + 64, n, :, 64 * odd:64 * odd + 64],
                                       ins[name][ds(l, 1), odd::2, :, :].rearrange("o h d e -> d (o h) e"))\
                            .then_inc(mix_bd, 16)
                pool.wait_ge(mix_w, l * 48 + 48)
                pool.sem_inc(passed_pool, 1)
                nc.gpsimd.affine_select(out=sgu_rows[:, :, :], in_=sgu_rows[:, :, :], pattern=[[0, AH], [-1, P]],
                                        compare_op=ALU.is_ge, fill=0.0, base=0, channel_multiplier=1).then_inc(sgu_masked, 1)
                for j in range(3):
                    load_gb(l * 3 + j)
                    affine_and_scale(l * 3 + (2 * DEPTH + 1 + j), True, base, l * 96 + (16 + 32 * (j + 1)))
                assert n_order[0] - base0 == ORDP, n_order[0] - base0

        @block.scalar
        def _(act):
            def width(c, outs, at):
                return outs[c - at] * D if at <= c < at + len(outs) else CW

            def split_hi(g, rnd, slot, w=CW):
                act.wait_ge(loaded[slot], rnd * 16)
                act.wait_ge(used, g + 1)
                nc.scalar.activation(w_hi[:, slot, 0:w], raw[:, slot, 0:w], ACT.Copy).then_inc(hi_done, 1)

            def split1(l, c, it=0):
                if c < CH1 + 2:
                    split_hi(g1(l, c) + it * 6, round1(l, c) + it * 2, c % RING)

            def split2(l, c, it=0):
                if c < CH2 + 2:
                    split_hi(g2(l, c) + it * 3, round2(l, c) + it, c % RING, width(c, OUT2, FFN + WIN))

            def sum_squares(norm):
                for t in range(T):
                    act.wait_ge(x_done, norm * 4 + (2 * t + 2))
                    nc.scalar.activation(xn[:, t, :], x_tok[:, t, :], ACT.Square,
                                         accum_out=ss[:, t:t + 1]).then_inc(sq_sum, 1)

            def turned(norm, gain, bias=None):
                for k in range(KD):
                    if k % 2 == 0:
                        act.wait_ge(xT, norm * 8 + (4 + k // 2 + 1))
                    nc.scalar.activation(a_hi[:, k, :], work_flat[:, k * SEQ:(k + 1) * SEQ], ACT.Identity,
                                         bias=0.0 if bias is None else cols[:, ds(bias + k, 1)],
                                         scale=cols[:, ds(gain + k, 1)]).then_inc(aT_hi, 1)

            def evac_proj(l, c):
                act.wait_ge(used, g1(l, c) + 4)
                if c == 0:
                    act.wait_ge(rstd_ready, l + 1)
                for t in range(T):
                    last = nc.scalar.activation(proj[:, t, c * BLK:(c + 1) * BLK], work[:, c % 2, t * BLK:(t + 1) * BLK],
                                                ACT.Identity, bias=0.0, scale=rstd[:, t:t + 1])
                last.then_inc(proj_ready, 1)

            def attend(l, e):
                act.wait_ge(nmax_ready, l * 16 + (e + 1))
                if e >= 2:
                    act.wait_ge(pT_ps, l * 16 + (e - 1))
                for t in range(T):
                    src = work[:, 2 + e % 2, t * SEQ:(t + 1) * SEQ] if e < NHA else masked[:, e % 2, t * SEQ:(t + 1) * SEQ]
                    last = nc.scalar.activation(prob[:, e % 2, t * SEQ:(t + 1) * SEQ], src, ACT.Exp,
                                                bias=nmax[:, HEADS[e], t:t + 1], scale=SCALE if e < NHA else 1.0,
                                                accum_out=rsum[:, HEADS[e], t:t + 1])
                last.then_inc(exp_done, 1)

            def evac_pT(l, e):
                act.wait_ge(pT_ps, l * 16 + (e + 1))
                if e >= 2:
                    act.wait_ge(pv_done, l * 16 + (e - 1))
                nc.scalar.activation(probT[:, e % 2, :], turned_bank(e), ACT.Copy).then_inc(pTB, 1)

            def y_squares(l, half):
                for t in range(T):
                    act.wait_ge(y_ready, l * 4 + (2 * half + t + 1))
                    nc.scalar.activation((sqs, rope_a)[half][:, t, 0:512], y_tok[:, t, half * 512:half * 512 + 512], ACT.Square,
                                         accum_out=ssy[:, 2 * half + t:2 * half + t + 1]).then_inc(y_sq, 1)

            def y_turned(l, half):
                act.wait_ge(yT_ps, l * 2 + (half + 1))
                src = acc_flat[:, 1024:2048]
                for k in range(4):
                    nc.scalar.activation(a_hi[:, 4 * half + k, :], src[:, k * SEQ:(k + 1) * SEQ], ACT.Identity, bias=0.0,
                                         scale=cols[:, ds(l * C1 + (2 * KD + 4 * half + k), 1)]).then_inc(yT_hi, 1)

            act.dma_start(ident[:, :], ins["c_ident"]).then_inc(id_loaded, 16)
            for n in range(3):
                act.dma_start(rows[n][0:NROWS[n], :], ins["rows"][sum(NROWS[:n]):sum(NROWS[:n + 1]), :]).then_inc(rows_loaded, 16)
            split1(0, 0)
            act.wait_ge(cols_ready, 4)
            split1(0, 1)
            with act.Fori(0, DEPTH) as l:
                sum_squares(l * 2)
                turned(l * 2, l * C1)
                split1(l, 2)
                for kind, n in PLAN1:
                    if kind == "chunk":
                        evac_proj(l, n)
                    elif kind == "split":
                        split1(l, n)
                    elif kind == "ropeA":
                        act.wait_ge(proj_ready, l * WIN + 3)
                        for t in range(T):
                            nc.scalar.activation(sqs[:, t, :], proj[:, t, 0:QKA], ACT.Square).then_inc(qk_sq, 1)
                    elif kind == "tA":
                        act.wait_ge(qkA_ps, l + 1)
                        nc.scalar.activation(qkTA[:, :, :].rearrange("p a b -> p (a b)"), acc_flat[:, 0:5 * SEQ], ACT.Copy)\
                            .then_inc(qkA_T, 1)
                    elif kind == "tB":
                        act.wait_ge(qkB_ps, l + 1)
                        nc.scalar.activation(qkTB[:, 0:4, :].rearrange("p a b -> p (a b)"), acc_flat[:, 0:1024], ACT.Copy)\
                            .then_inc(qB_T, 1)
                    elif kind == "score":
                        attend(l, n)
                    elif kind == "turn" and n >= NHA:
                        evac_pT(l, n)
                    elif kind == "yturn":
                        y_turned(l, n)
                        if n == 1:
                            split1(l, WIN + RING)
                            y_squares(l, 0)
                            y_squares(l, 1)
                split1(l, WIN + 1 + RING)
                split1(l, WIN + 2 + RING)
                sum_squares(l * 2 + 1)
                turned(l * 2 + 1, l * C1 + KD)
                split1(l, WIN + 3 + RING)

                def relu_u(l, i):
                    if not (isinstance(i, int) and i == 0):
                        act.wait_ge(h1_sq, l * NI1 + i)
                    nc.scalar.activation(relu[:, :], work[:, 0, :], ACT.Relu).then_inc(relu_done, 1)

                def hidden_hi(l, i, slot):
                    act.wait_ge(h1_sq, l * NI1 + i + 1)
                    nc.scalar.activation(h_hi[:, slot, :], hid[:, :], ACT.Copy).then_inc(h1_hi, 1)

                act.wait_ge(used, g1(l, MLP0) + 4)
                relu_u(l, 0)
                split1(l, MLP0 + 3)
                hidden_hi(l, 0, 0)

                def mlp_body(it, guard):
                    for j in range(3):
                        i, c = it * 3 + (1 + j), MLP0 + 1 + 2 * j
                        last = c + 6 * guard
                        act.wait_ge(used, g1(l, c) + it * 6 + 4)
                        relu_u(l, i)
                        split1(l, c + 3, it)
                        hidden_hi(l, i, (1 + j) % 3)
                        if last + 4 < CH1 + 2:
                            split1(l, c + 4, it)

                with act.Fori(0, (NI1 - 1) // 3 - 1) as it:
                    mlp_body(it, 0)
                mlp_body((NI1 - 1) // 3 - 1, (NI1 - 1) // 3 - 1)

            sum_squares(2 * DEPTH)
            act.wait_ge(lam_abs, 1)
            nc.scalar.activation(sp[:, 1, :], sp[:, 0, :], ACT.Exp, scale=-1.0).then_inc(lam_exp, 1)

            def ffn(l, f, cb):
                def silu(i):
                    if not (isinstance(i, int) and i == 0):
                        act.wait_ge(h2_f, (l * 2 + f) * NI2 + i)
                    nc.scalar.activation(relu[:, :], work[:, 0, :], ACT.Silu).then_inc(silu_done, 1)

                def hidden_hi(i, slot):
                    act.wait_ge(h2_f, (l * 2 + f) * NI2 + i + 1)
                    nc.scalar.activation(h_hi[:, slot, :], hid[:, :], ACT.Copy).then_inc(h2_hi, 1)

                act.wait_ge(used, g2(l, cb) + 4)
                silu(0)
                split2(l, cb + 3)
                split2(l, cb + 4)
                hidden_hi(0, 0)

                def body(it, last):
                    i, c = it + 1, cb + 2
                    act.wait_ge(used, g2(l, c) + it * 3 + 4)
                    silu(i)
                    for n in (3, 4, 5):
                        if n == 5:
                            if not last:
                                act.wait_ge(used, g2(l, c) + it * 3 + 6)
                            hidden_hi(i, int(last))
                        if not last or c + 3 * (NI2 - 2) + n < cb + FFN + 2:
                            split2(l, c + n, it)

                with act.Fori(0, NI2 - 2) as it:
                    body(it, False)
                body(NI2 - 2, True)

            with act.Fori(0, DEPTH) as l:
                norm0 = l * 3 + (2 * DEPTH + 1)
                gains = l * N2 + LN0
                mx = l * NM + MX0
                turned(norm0 - 1, l * N2 + LAST_LN, l * N2 + (LAST_LN + 3 * KD))
                split2(l, 2)
                ffn(l, 0, 0)
                turned(norm0, gains, gains + 3 * KD)
                split2(l, FFN + 2)
                for j in range(WIN):
                    c = FFN + j
                    act.wait_ge(used, g2(l, c) + 4)
                    bank = work[:, j % 2, :]
                    if j < 2:
                        act.wait_ge(conv_pads, 2)
                        nc.scalar.activation(xrp[:, 2 * j:2 * j + 2, CONV_C - 1:], bank.rearrange("p (c s) -> p c s", c=2),
                                             ACT.Copy).then_inc(z_done, 1)
                    elif j < 4:
                        nc.scalar.activation((ug, vg)[j - 2], bank, ACT.Gelu_apprx_tanh).then_inc(z_done, 1)
                    elif j < 6:
                        nc.scalar.activation(gg[:, (j - 4) * 512:(j - 3) * 512], bank, ACT.Gelu_apprx_tanh).then_inc(z_done, 1)
                    elif j < 8:
                        nc.scalar.activation((bg, cgt)[j - 6], bank, ACT.Copy).then_inc(z_done, 1)
                    split2(l, c + RING)
                    if j == 5:
                        for n in range(2):
                            act.wait_ge(gate_ps, l * 2 + (n + 1))
                            src = (work_flat[:, 1024:2048], acc_flat[:, 0:1024])[n]
                            for i in range(CT):
                                nc.scalar.activation((r_gate, i_gate)[n][:, i * SEQ:(i + 1) * SEQ], src[:, i * SEQ:(i + 1) * SEQ],
                                                     ACT.Sigmoid, bias=cols[:, ds(mx + ((M_BA, M_BI)[n] + i), 1)])\
                                    .then_inc(sig_done, 1)
                        act.wait_ge(sig_done, l * 2 * CT + CT)
                        act.wait_ge(sp_ready, 1)
                        for i in range(CT):
                            nc.scalar.activation(th[:, i * SEQ:(i + 1) * SEQ], r_gate[:, i * SEQ:(i + 1) * SEQ], ACT.Tanh,
                                                 scale=sp[:, 3, ds(l * CT + i, 1)]).then_inc(th_done, 1)
                        act.wait_ge(th_pos, l + 1)
                        nc.scalar.activation(root, th, ACT.Sqrt, scale=4.0).then_inc(root_done, 1)
                    if j == 6:
                        act.wait_ge(yaT_ps, l + 1)
                        for k in range(2):
                            nc.scalar.activation(mixed(k)[0], acc_flat[:, 1536 + k * SEQ:1536 + (k + 1) * SEQ], ACT.Copy)\
                                .then_inc(y2_hi, 1)
                act.wait_ge(y2_f, l * 2 + 1)
                nc.scalar.activation(mixed(2, 2)[0], yb, ACT.Copy).then_inc(y2_hi, 1)
                act.wait_ge(y2_f, l * 2 + 2)
                nc.scalar.activation(mixed(4, 4)[0], r_gate, ACT.Copy).then_inc(y2_hi, 1)
                for j in range(len(OUT2) - 1):
                    split2(l, FFN + WIN + j + RING)
                turned(norm0 + 1, gains + KD, gains + 4 * KD)
                split2(l, FFN + WIN + len(OUT2) + 2)
                ffn(l, 1, FFN + WIN + len(OUT2))

        @block.vector
        def _(dve):
            order = {"n": 0, "base": 0}

            def step(ins_):
                order["n"] += 1
                ins_.then_inc(dve_order, 1)
                return order["n"]

            def after(n):
                dve.wait_ge(dve_order, order["base"] + n)

            def link(ins_):
                after(step(ins_))

            def width(c, outs, at):
                return outs[c - at] * D if at <= c < at + len(outs) else CW

            def split_lo(g, slot, w=CW):
                dve.wait_ge(hi_done, g + 1)
                nc.vector.tensor_tensor(w_lo[:, slot, 0:w], raw[:, slot, 0:w], w_hi[:, slot, 0:w].bitcast(f32), ALU.subtract)\
                    .then_inc(lo_done, 1)

            def split1(l, c, it=0):
                split_lo(g1(l, c) + it * 6, c % RING)

            def split2(l, c, it=0):
                split_lo(g2(l, c) + it * 3, c % RING, width(c, OUT2, FFN + WIN))

            def rsqrt(dst, src, n, scale, eps):
                v, y, h, b = (nwt[:, r, 0:n] for r in range(4))
                link(nc.vector.tensor_scalar(v, src, scale, eps, ALU.mult, ALU.add))
                nc.vector.tensor_scalar(y.bitcast(i32), v.bitcast(i32), -0.5, float(0x5f3759df), ALU.mult, ALU.add)
                link(nc.vector.tensor_scalar(h, v, -0.5, None, ALU.mult))
                for turn in range(3):
                    link(nc.vector.tensor_tensor(b, y, y, ALU.mult))
                    link(nc.vector.tensor_tensor(b, b, h, ALU.mult))
                    last = nc.vector.scalar_tensor_tensor(dst if turn == 2 else y, b, 1.5, y, ALU.add, ALU.mult)
                    if turn < 2:
                        link(last)
                return last

            def turned(norm, gain):
                for k in range(KD):
                    dve.wait_ge(aT_hi, norm * KD + (k // 2 * 2 + 2))
                    nc.vector.scalar_tensor_tensor(a_lo[:, k, :], work_flat[:, k * SEQ:(k + 1) * SEQ], cols[:, ds(gain + k, 1)],
                                                   a_hi[:, k, :].bitcast(f32), ALU.mult, ALU.subtract).then_inc(aT_lo, 1)

            def turned_ln(norm, gain, bias):
                for k in range(KD):
                    dve.wait_ge(aT_hi, norm * KD + (k // 2 * 2 + 2))
                    link(nc.vector.tensor_scalar(affine[:, k % 2, :], work_flat[:, k * SEQ:(k + 1) * SEQ],
                                                 cols[:, ds(gain + k, 1)], cols[:, ds(bias + k, 1)], ALU.mult, ALU.add))
                    nc.vector.tensor_tensor(a_lo[:, k, :], affine[:, k % 2, :], a_hi[:, k, :].bitcast(f32), ALU.subtract)\
                        .then_inc(aT_lo, 1)

            def quarter_ready(norm, g, q):
                if q < 3:
                    dve.wait_ge(sums, (norm - 1) * 3 + (q + 1))
                else:
                    dve.wait_ge(used, g + 4)

            def residual(norm, g, factor):
                for q in range(4):
                    t, n = q // 2, q % 2
                    x = x_tok[:, t, n * 512:(n + 1) * 512]
                    quarter_ready(norm, g, q)
                    nc.vector.scalar_tensor_tensor(x, acc[:, q, :], factor[:, t:t + 1], x, ALU.mult, ALU.add).then_inc(x_done, 1)

            def layer_norm(norm, g, factor):
                latest = [0, 0]

                def newton(t, i):
                    v, y, h, b = (nwt[:, r, t:t + 1] for r in range(4))
                    after(latest[t])
                    if i == 0:
                        ins_ = nc.vector.tensor_scalar(v, mv[:, t, 1:2], 1.0, LN_EPS, ALU.mult, ALU.add)
                    elif i == 1:
                        nc.vector.tensor_scalar(y.bitcast(i32), v.bitcast(i32), -0.5, float(0x5f3759df), ALU.mult, ALU.add)
                        ins_ = nc.vector.tensor_scalar(h, v, -0.5, None, ALU.mult)
                    elif i % 2 == 0:
                        ins_ = nc.vector.tensor_scalar(b, y, y, h, ALU.mult, ALU.mult)
                    else:
                        ins_ = nc.vector.scalar_tensor_tensor(rstd[:, t:t + 1] if i == 7 else y, b, 1.5, y, ALU.add, ALU.mult)
                    latest[t] = step(ins_)

                def normalise(t):
                    after(latest[t])
                    for n in range(2):
                        half = slice(n * 512, (n + 1) * 512)
                        nc.vector.tensor_scalar(xn[:, t, half], x_tok[:, t, half], mv[:, t, 0:1], rstd[:, t:t + 1],
                                                ALU.subtract, ALU.mult).then_inc(xn_ready, 1)

                for q in range(4):
                    t, n = q // 2, q % 2
                    x = x_tok[:, t, n * 512:(n + 1) * 512]
                    quarter_ready(norm, g, q)
                    if n == 0:
                        dve.wait_ge(x_scaled, (norm - 2 * DEPTH - 1) * T + (t + 1))
                    summed = step(nc.vector.scalar_tensor_tensor(x, acc[:, q, :], factor, x, ALU.mult, ALU.add))
                    if t == 1:
                        newton(0, 2 * n)
                    after(summed)
                    stats = step(nc.vector.bn_stats(stat[:, t, n, :], x))
                    if t == 1:
                        newton(0, 2 * n + 1)
                    if n == 1:
                        after(stats)
                        dve.sem_inc(passed_dve, 1)
                        latest[t] = step(nc.vector.bn_aggr(mv[:, t, :], stat[:, t, :, :].rearrange("p a b -> p (a b)")))
                for i in range(4):
                    newton(0, i + 4)
                    newton(1, i)
                normalise(0)
                for i in range(4, 8):
                    newton(1, i)
                normalise(1)

            dve.sem_inc(lo_done, RING)
            dve.wait_ge(x_loaded, 16 * T)
            dve.sem_inc(x_done, 4)
            split1(0, 0)
            nc.vector.memset(cols[:, DEPTH * C1:LN0], 0.0).then_inc(cols_ready, 1)
            dve.wait_ge(rowsT, 3)
            tabs = acc[:, 0, :]
            nc.vector.tensor_copy(cols[:, 0:DEPTH * C1], tabs[:, 0:DEPTH * C1]).then_inc(cols_ready, 1)
            nc.vector.tensor_copy(cols[:, LN0:NCOL], tabs[:, DEPTH * C1:DEPTH * C1 + NCOL - LN0]).then_inc(cols_ready, 1)
            dve.wait_ge(cols_ready, 3)
            at = DEPTH * C1 + NCOL - LN0
            nc.vector.tensor_copy(cols[:, LAST_LN:LAST_LN + KD], tabs[:, at:at + KD]).then_inc(cols_ready, 1)
            lam = cols[:, MX0:MX0 + DEPTH * NM].rearrange("p (l m) -> p l m", m=NM)[:, :, M_LAM:M_LAM + CT]
            sv = [sp[:, n, :].rearrange("p (l m) -> p l m", m=CT) for n in range(4)]
            setup = 0

            def rope_global(l):
                for t in range(T):
                    dve.wait_ge(qk_sq, l * T + (t + 1))
                    link(nc.vector.tensor_reduce(ssA[:, t * 10:(t + 1) * 10], sqs[:, t, :].rearrange("p (h d) -> p h d", d=HD),
                                                 AX.X, ALU.add))
                link(rsqrt(rstdA[:, :], ssA[:, :], 20, 1.0 / HD, RMS_EPS))
                dve.wait_ge(rope_tab, l * 20 + 20)
                for t in range(T):
                    m = rope_b[:, t, :].rearrange("p (h d) -> p h d", d=HD)
                    link(nc.vector.tensor_tensor(m, proj[:, t, 0:QKA].rearrange("p (h d) -> p h d", d=HD),
                                                 rstdA[:, t * 10:(t + 1) * 10].unsqueeze(2).broadcast_to((P, NHA + NKV, HD)), ALU.mult))
                    nc.vector.tensor_tensor(rope_a[:, t, :], rope_b[:, t, :], cg[:, t, :], ALU.mult)
                    halves = [x[:, t, :].rearrange("p (a b c) -> p a b c", b=2, c=16) for x in (rope_b, sg, sqs)]
                    for b in range(2):
                        link(nc.vector.tensor_tensor(halves[2][:, :, b, :], halves[0][:, :, 1 - b, :], halves[1][:, :, b, :], ALU.mult))
                    for g in range(NKV):
                        q = slice(g * GROUP * HD, (g + 1) * GROUP * HD)
                        nc.vector.tensor_tensor(
                            qkA[:, t, 0:NHA * HD].rearrange("p (i g d) -> p g i d", g=NKV, d=HD)[:, g, :, :],
                            rope_a[:, t, q].rearrange("p (i d) -> p i d", d=HD),
                            sqs[:, t, q].rearrange("p (i d) -> p i d", d=HD), ALU.add)
                    nc.vector.tensor_tensor(qkA[:, t, NHA * HD:], rope_a[:, t, NHA * HD:], sqs[:, t, NHA * HD:], ALU.add)\
                        .then_inc(ropeA_done, 1)

            def rope_dilated(l):
                dve.wait_ge(tab_loaded, 48)
                dve.wait_ge(qkA_ps, l + 1)
                dve.wait_ge(proj_ready, l * WIN + 7)
                for t in range(T):
                    x = proj[:, t, QB0:VB0].rearrange("p (h d) -> p h d", d=HD)
                    a = rope_a[:, t, 0:256].rearrange("p (h d) -> p h d", d=16)
                    b = rope_b[:, t, 0:256].rearrange("p (h d) -> p h d", d=16)
                    nc.vector.tensor_tensor(a, x[:, :, 0:16], rope_pt[:, t, 0:16].unsqueeze(1).broadcast_to((P, 2 * NHB, 16)), ALU.mult)
                    for n in range(2):
                        link(nc.vector.tensor_tensor(b[:, :, 8 * n:8 * n + 8], x[:, :, 8 - 8 * n:16 - 8 * n],
                                                     rope_pt[:, t, 16 + 8 * n:24 + 8 * n].unsqueeze(1).broadcast_to((P, 2 * NHB, 8)),
                                                     ALU.mult))
                    nc.vector.tensor_tensor(x[:, :, 0:16], a, b, ALU.add).then_inc(ropeB_done, 1)

            def row_max(l, e):
                dve.wait_ge(s_ready, l * 16 + (e + 1))
                h = HEADS[e]
                scores = work[:, 2 + e % 2, :]
                if e < NHA:
                    link(nc.vector.tensor_reduce(rinv[:, h, :], scores.rearrange("p (t s) -> p t s", t=T), AX.X, ALU.max))
                    nc.vector.tensor_scalar(nmax[:, h, :], rinv[:, h, :], -SCALE, None, ALU.mult).then_inc(nmax_ready, 1)
                else:
                    dve.wait_ge(exp_done, l * 16 + (e - 1))
                    link(nc.vector.scalar_tensor_tensor(masked[:, e % 2, :], scores, SCALE, logc_flat, ALU.mult, ALU.add))
                    nc.vector.tensor_reduce(nmax[:, h, :], masked[:, e % 2, :].rearrange("p (t s) -> p t s", t=T),
                                            AX.X, ALU.max, negate=True).then_inc(nmax_ready, 1)

            logc_flat = logc[:, :, :].rearrange("p t s -> p (t s)")

            def evac_pT(l, e):
                dve.wait_ge(pT_ps, l * 16 + (e + 1))
                if e >= 2:
                    dve.wait_ge(pv_done, l * 16 + (e - 1))
                nc.vector.tensor_copy(probT[:, e % 2, :], turned_bank(e)).then_inc(pTA, 1)

            def y_norm(l, half):
                dve.wait_ge(pv_done, l * 16 + (8 * half + 8))
                hs_ = slice(8 * half, 8 * half + 8)
                link(nc.vector.reciprocal(rinv[:, hs_, :], rsum[:, hs_, :]))
                for t in range(T):
                    y = y_tok[:, t, half * 512:half * 512 + 512].rearrange("p (h d) -> p h d", d=HD)
                    o = acc[:, (2, 0)[half] + t, :].rearrange("p (h d) -> p h d", d=HD)
                    nc.vector.tensor_tensor(y, o, rinv[:, hs_, t].unsqueeze(2).broadcast_to((P, 8, HD)), ALU.mult).then_inc(y_ready, 1)

            def y_turned(l, half):
                src = acc_flat[:, 1024:2048]
                for k in range(4):
                    dve.wait_ge(yT_hi, l * 8 + (4 * half + k // 2 * 2 + 2))
                    nc.vector.scalar_tensor_tensor(a_lo[:, 4 * half + k, :], src[:, k * SEQ:(k + 1) * SEQ],
                                                   cols[:, ds(l * C1 + (2 * KD + 4 * half + k), 1)],
                                                   a_hi[:, 4 * half + k, :].bitcast(f32), ALU.mult, ALU.subtract).then_inc(yT_lo, 1)

            with dve.Fori(0, DEPTH) as l:
                order["n"], order["base"] = 0, l * ORD1 + setup
                turned(l * 2, l * C1)
                split1(l, 1)
                dve.wait_ge(sq_sum, l * 2 * T + T)
                rsqrt(rstd[:, :], ss[:, 0:T], T, 1.0 / D, RMS_EPS).then_inc(rstd_ready, 1)
                split1(l, 2)
                for kind, n in PLAN1:
                    if kind == "split" and n < WIN:
                        split1(l, n)
                    elif kind == "ropeA":
                        rope_global(l)
                    elif kind == "ropeB":
                        rope_dilated(l)
                    elif kind == "tB":
                        dve.wait_ge(qkB_ps, l + 1)
                        nc.vector.tensor_copy(qkTB[:, 4:8, :].rearrange("p a b -> p (a b)"), acc_flat[:, 1024:2048]).then_inc(kB_T, 1)
                    elif kind == "score":
                        row_max(l, n)
                    elif kind == "turn" and n < NHA:
                        evac_pT(l, n)
                    elif kind == "ynorm":
                        y_norm(l, n)
                    elif kind == "yturn":
                        y_turned(l, n)
                dve.wait_ge(lo_done, g1(l, WIN + RING) + 3)
                split1(l, WIN + RING)
                dve.wait_ge(y_sq, l * 4 + 4)
                link(rsqrt(rstdy[:, :], ssy[:, :], 4, 1.0 / 512, RMS_EPS))
                split1(l, WIN + 1 + RING)
                dve.wait_ge(used, g1(l, WIN + 1) + 4)
                for t in range(T):
                    for n in range(2):
                        x = x_tok[:, t, n * 512:(n + 1) * 512]
                        link(nc.vector.scalar_tensor_tensor(x, work[:, 2 * t + n, :], rstdy[:, t:t + 1], x, ALU.mult, ALU.add))
                residual(l * 2 + 1, g1(l, MLP0 - 1), rstdy[:, T:])
                turned(l * 2 + 1, l * C1 + KD)
                split1(l, WIN + 2 + RING)
                dve.wait_ge(sq_sum, (l * 2 + 2) * T)
                link(nc.vector.tensor_scalar(rms2[:, 0, :], ss[:, 0:T], 1.0 / D, RMS_EPS, ALU.mult, ALU.add))
                link(nc.vector.reciprocal(rms2[:, 1, :], rms2[:, 0, :]))
                split1(l, WIN + 3 + RING)

                def square(l, i):
                    dve.wait_ge(relu_done, l * NI1 + i + 1)
                    if not (isinstance(i, int) and i == 0):
                        dve.wait_ge(h1_lo, l * NI1 + i)
                    nc.vector.tensor_tensor(hid[:, :], relu[:, :], relu[:, :], ALU.mult).then_inc(h1_sq, 1)

                def hidden_lo(l, i, slot):
                    dve.wait_ge(h1_hi, l * NI1 + i + 1)
                    nc.vector.tensor_tensor(h_lo[:, slot, :], hid[:, :], h_hi[:, slot, :].bitcast(f32), ALU.subtract).then_inc(h1_lo, 1)

                square(l, 0)
                split1(l, MLP0 + 3)
                hidden_lo(l, 0, 0)

                def mlp_body(it, guard):
                    for j in range(3):
                        i, c = it * 3 + (1 + j), MLP0 + 1 + 2 * j
                        last = c + 6 * guard
                        square(l, i)
                        split1(l, c + 3, it)
                        hidden_lo(l, i, (1 + j) % 3)
                        if last + 4 < CH1 + 1:
                            split1(l, c + 4, it)

                with dve.Fori(0, (NI1 - 1) // 3 - 1) as it:
                    mlp_body(it, 0)
                mlp_body((NI1 - 1) // 3 - 1, (NI1 - 1) // 3 - 1)
                residual(l * 2 + 2, g1(l, CH1 - 1), rms2[:, 1, :])
                assert order["n"] == ORD1, order["n"]

            order["n"], order["base"] = 0, setup + DEPTH * ORD1
            nc.vector.memset(xrp, 0.0).then_inc(conv_pads, 1)
            nc.vector.memset(cxp, 0.0).then_inc(conv_pads, 1)
            dve.wait_ge(sq_sum, (2 * DEPTH + 1) * T)
            link(rsqrt(rstd[:, :], ss[:, 0:T], T, 1.0 / D, RMS_EPS))
            for t in range(T):
                for n in range(2):
                    half = slice(n * 512, (n + 1) * 512)
                    nc.vector.tensor_scalar(xn[:, t, half], x_tok[:, t, half], rstd[:, t:t + 1], None, ALU.mult).then_inc(xn_ready, 1)
            nc.vector.scalar_tensor_tensor(sv[0], lam, -1.0, lam, ALU.mult, ALU.max).then_inc(lam_abs, 1)
            dve.wait_ge(lam_exp, 1)
            link(nc.vector.tensor_scalar(sp[:, 0, :], sp[:, 1, :], 2.0, None, ALU.add))
            link(nc.vector.reciprocal(sp[:, 2, :], sp[:, 0, :]))
            link(nc.vector.tensor_tensor(sp[:, 1, :], sp[:, 1, :], sp[:, 2, :], ALU.mult))
            link(nc.vector.tensor_tensor(sp[:, 0, :], sp[:, 1, :], sp[:, 1, :], ALU.mult))
            link(nc.vector.tensor_scalar(sp[:, 2, :], sp[:, 0, :], 1.0 / 17, None, ALU.mult))
            for odd in (15, 13, 11, 9, 7, 5, 3):
                link(nc.vector.scalar_tensor_tensor(sp[:, 2, :], sp[:, 2, :], 1.0 / odd, sp[:, 0, :], ALU.add, ALU.mult))
            link(nc.vector.scalar_tensor_tensor(sp[:, 2, :], sp[:, 2, :], 1.0, sp[:, 1, :], ALU.add, ALU.mult))
            link(nc.vector.tensor_scalar(sp[:, 2, :], sp[:, 2, :], RG_C, None, ALU.mult))
            link(nc.vector.tensor_scalar(sv[0], lam, -RG_C / 2, 0.0, ALU.mult, ALU.max))
            nc.vector.tensor_tensor(sp[:, 3, :], sp[:, 0, :], sp[:, 2, :], ALU.add).then_inc(sp_ready, 1)
            before2 = setup + DEPTH * ORD1 + order["n"]

            def ffn(l, f, cb):
                def hidden(i):
                    dve.wait_ge(silu_done, (l * 2 + f) * NI2 + i + 1)
                    if not (isinstance(i, int) and i == 0):
                        dve.wait_ge(h2_lo, (l * 2 + f) * NI2 + i)
                    nc.vector.tensor_tensor(hid[:, :], relu[:, :], work[:, 1, :], ALU.mult).then_inc(h2_f, 1)

                def hidden_lo(i, slot):
                    dve.wait_ge(h2_hi, (l * 2 + f) * NI2 + i + 1)
                    nc.vector.tensor_tensor(h_lo[:, slot, :], hid[:, :], h_hi[:, slot, :].bitcast(f32), ALU.subtract).then_inc(h2_lo, 1)

                split2(l, cb + 3)
                dve.wait_ge(used, g2(l, cb + 1) + 4)
                hidden(0)
                split2(l, cb + 4)
                hidden_lo(0, 0)

                def body(it, last):
                    i, c = it + 1, cb + 2
                    for n in (3, 4, 5):
                        if n == 4:
                            dve.wait_ge(used, g2(l, c) + it * 3 + 5)
                            hidden(i)
                        if n == 5:
                            hidden_lo(i, int(last))
                        if not last or c + 3 * (NI2 - 2) + n < cb + FFN + 1:
                            split2(l, c + n, it)

                with dve.Fori(0, NI2 - 2) as it:
                    body(it, False)
                body(NI2 - 2, True)

            with dve.Fori(0, DEPTH) as l:
                order["n"], order["base"] = 0, l * ORD2 + before2
                norm0 = l * 3 + (2 * DEPTH + 1)
                gains = l * N2 + LN0
                mx = l * NM + MX0
                turned_ln(norm0 - 1, l * N2 + LAST_LN, l * N2 + (LAST_LN + 3 * KD))
                split2(l, 1)
                split2(l, 2)
                ffn(l, 0, 0)
                layer_norm(norm0, g2(l, FFN - 1), 0.5)
                turned_ln(norm0, gains, gains + 3 * KD)
                split2(l, FFN + 1)
                split2(l, FFN + 2)
                dve.wait_ge(sgu_ps, l + 1)
                nc.vector.tensor_copy(sguT[:, :, :].rearrange("p a b -> p (a b)"), acc[:, 2, :]).then_inc(sgu_T, 1)
                for j in range(WIN):
                    if j == 2:
                        dve.wait_ge(z_done, l * 8 + 2)
                        for i in range(CT):
                            for tap in range(CONV_C):
                                src, w = xrp[:, i, tap:tap + SEQ], cols[:, ds(mx + (M_CONV + tap * CT + i), 1)]
                                dst = xr[:, i * SEQ:(i + 1) * SEQ]
                                if tap == 0:
                                    link(nc.vector.tensor_scalar(dst, src, w, None, ALU.mult))
                                else:
                                    link(nc.vector.scalar_tensor_tensor(dst, src, w, dst, ALU.mult, ALU.add))
                            nc.vector.tensor_scalar(dst, dst, cols[:, ds(mx + (M_CB + i), 1)], None, ALU.add).then_inc(conv_done, 1)
                    if j == 4:
                        dve.wait_ge(z_done, l * 8 + 4)
                        for t in range(T):
                            v = vg[:, t * 256:(t + 1) * 256]
                            link(nc.vector.bn_stats(stat[:, t, 0, :], v))
                            dve.sem_inc(passed_dve, 1)
                            link(nc.vector.bn_aggr(mv[:, t, :], stat[:, t, 0, :]))
                        link(rsqrt(rstd[:, :], mv[:, :, 1], T, 1.0, LN_EPS))
                        dve.wait_ge(mix_w, l * 48 + 48)
                        for t in range(T):
                            v, w = vg[:, t * 256:(t + 1) * 256], vn[:, t * 256:(t + 1) * 256]
                            link(nc.vector.tensor_scalar(w, v, mv[:, t, 0:1], rstd[:, t:t + 1], ALU.subtract, ALU.mult))
                            link(nc.vector.tensor_tensor(w, w, sgu_gb[:, 0, :], ALU.mult))
                            nc.vector.tensor_tensor(w, w, sgu_gb[:, 1, :], ALU.add).then_inc(v_done, 1)
                    if j == 6:
                        dve.wait_ge(mix_ps, l + 1)
                        for h in range(AH):
                            dst, src, u = (x.rearrange("p (t c) -> p t c", t=T)[:, :, h * HD:(h + 1) * HD]
                                           for x in (ya, acc[:, 2, :], ug))
                            nc.vector.scalar_tensor_tensor(dst, src, cols[:, ds(mx + (M_SGB + h), 1)], u, ALU.add, ALU.mult)\
                                .then_inc(ya_done, 1)
                        dve.wait_ge(th_done, l * CT + CT)
                        nc.vector.tensor_scalar(th, th, 0.0, None, ALU.max).then_inc(th_pos, 1)
                        dve.wait_ge(th_pos, l + 1)
                        link(nc.vector.tensor_scalar(q_rec, th, 1.0, None, ALU.add))
                        link(nc.vector.reciprocal(q_rec, q_rec))
                        link(nc.vector.tensor_scalar(a_dec, q_rec, 2.0, -1.0, ALU.mult, ALU.add))
                        dve.wait_ge(sig_done, l * 2 * CT + 2 * CT)
                        link(nc.vector.tensor_tensor(i_gate, i_gate, xr, ALU.mult))
                    if j == 7:
                        for k in range(2):
                            dve.wait_ge(y2_hi, l * 4 + 2)
                            nc.vector.tensor_tensor(mixed(k)[1], acc_flat[:, 1536 + k * SEQ:1536 + (k + 1) * SEQ],
                                                    mixed(k)[0].bitcast(f32), ALU.subtract).then_inc(y2_lo, 1)
                        dve.wait_ge(root_done, l + 1)
                        link(nc.vector.tensor_tensor(q_rec, q_rec, root, ALU.mult))
                        link(nc.vector.tensor_tensor(q_rec, q_rec, i_gate, ALU.mult))
                        for i in range(CT):
                            span = slice(i * SEQ, (i + 1) * SEQ)
                            last = nc.vector.tensor_tensor_scan(hs[:, span], a_dec[:, span], q_rec[:, span], 0.0, ALU.mult, ALU.add)
                        link(last)
                    if j == 8:
                        dve.wait_ge(used, g2(l, FFN + 8) + 4)
                        dve.wait_ge(z_done, l * 8 + 8)
                        nc.vector.tensor_tensor(cxp[:, :, CONV_B - 1:], cgt.rearrange("p (c s) -> p c s", c=2),
                                                work[:, 0, :].rearrange("p (c s) -> p c s", c=2), ALU.mult).then_inc(cx_done, 1)
                        dve.wait_ge(cx_done, l + 1)
                        for i in range(2):
                            for tap in range(CONV_B):
                                src, w = cxp[:, i, tap:tap + SEQ], cols[:, ds(mx + (M_SC + tap * 2 + i), 1)]
                                dst = yb[:, i * SEQ:(i + 1) * SEQ]
                                if tap == 0:
                                    link(nc.vector.tensor_scalar(dst, src, w, None, ALU.mult))
                                else:
                                    link(nc.vector.scalar_tensor_tensor(dst, src, w, dst, ALU.mult, ALU.add))
                        nc.vector.tensor_tensor(yb, yb, bg, ALU.mult).then_inc(y2_f, 1)
                        nc.vector.tensor_tensor(r_gate, gg, hs, ALU.mult).then_inc(y2_f, 1)
                    split2(l, FFN + j + RING)
                dve.wait_ge(y2_hi, l * 4 + 3)
                dve.wait_ge(y2_f, l * 2 + 1)
                nc.vector.tensor_tensor(mixed(2, 2)[1], yb,
                                        mixed(2, 2)[0].bitcast(f32), ALU.subtract).then_inc(y2_lo, 1)
                dve.wait_ge(y2_hi, l * 4 + 4)
                dve.wait_ge(y2_f, l * 2 + 2)
                nc.vector.tensor_tensor(mixed(4, 4)[1], r_gate,
                                        mixed(4, 4)[0].bitcast(f32), ALU.subtract).then_inc(y2_lo, 1)
                for j in range(len(OUT2) - 2):
                    split2(l, FFN + WIN + j + RING)
                layer_norm(norm0 + 1, g2(l, FFN + WIN + len(OUT2) - 1), 1.0)
                turned_ln(norm0 + 1, gains + KD, gains + 4 * KD)
                for c in (1, 2):
                    split2(l, FFN + WIN + len(OUT2) + c)
                ffn(l, 1, FFN + WIN + len(OUT2))
                layer_norm(norm0 + 2, g2(l, CH2 - 1), 0.5)
                assert order["n"] == ORD2, order["n"]

        @block.tensor
        def _(pe):
            def chunk_ready(g):
                pe.wait_ge(lo_done, g + 4)

            def weights(slot, k, at, n):
                return [w[:, slot, k + at:k + at + n] for w in (w_hi, w_lo)]

            def product(dst, left, right, start, stop=False):
                (lh, ll), (rh, rl) = left, right
                nc.tensor.matmul(dst, lh, rh, start=start, stop=False, skip_group_check=True)
                nc.tensor.matmul(dst, lh, rl, start=False, stop=False, skip_group_check=True)
                return nc.tensor.matmul(dst, ll, rh, start=False, stop=stop, skip_group_check=True)

            def turn_norm(norm, src, ready, at0):
                for t in range(T):
                    for k in range(KD):
                        if k % 4 == 0:
                            pe.wait_ge(ready, at0 + (2 * t + k // 4 + 1))
                        at = k * SEQ + t * P
                        last = nc.tensor.transpose(work_flat[:, at:at + P], src[:, t, k * P:(k + 1) * P], ident[:, :])
                        if k % 2 == 1:
                            last.then_inc(xT, 1)

            def by_tokens(g, slot, bank, norm=None):
                chunk_ready(g)
                for k in range(KD):
                    if norm is not None and k % 2 == 0:
                        pe.wait_ge(aT_lo, norm * KD + (k + 2))
                    for t in range(T):
                        tok = slice(t * P, (t + 1) * P)
                        last = product(work[:, bank, t * BLK:(t + 1) * BLK], (a_hi[:, k, tok], a_lo[:, k, tok]),
                                       weights(slot, k * BLK, 0, BLK), start=(k == 0 and t == 0), stop=(k == KD - 1))
                last.then_inc(used, 1)

            def by_features(g, slot, bank, norm=None):
                chunk_ready(g)
                for k in range(KD):
                    if norm is not None and k % 2 == 0:
                        pe.wait_ge(aT_lo, norm * KD + (k + 2))
                    for m in range(2):
                        last = product(work[:, bank, m * SEQ:(m + 1) * SEQ], weights(slot, k * BLK, m * P, P),
                                       (a_hi[:, k, :], a_lo[:, k, :]), start=(k == 0 and m == 0), stop=(k == KD - 1))
                last.then_inc(used, 1)

            def down(g, slot, left, nk, dst=acc, start=False, stop=False, quarters=False):
                chunk_ready(g)

                def part_of(k, t, n):
                    hi, lo = left(k)
                    tok = slice(t * P, (t + 1) * P)
                    return product(dst[:, 2 * t + n, :], (hi[:, tok], lo[:, tok]), weights(slot, k * D, n * 512, 512),
                                   start=start and k == 0, stop=stop and k == nk - 1)

                if quarters:
                    for t in range(T):
                        for n in range(2):
                            for k in range(nk):
                                last = part_of(k, t, n)
                            last.then_inc(used if t == T - 1 and n == 1 else sums, 1)
                else:
                    for k in range(nk):
                        for t in range(T):
                            for n in range(2):
                                last = part_of(k, t, n)
                    last.then_inc(used, 1)

            def open_sums():
                for b in range(4):
                    nc.tensor.matmul(acc[:, b, 0:2], zero[:, :], zero[:, 0:2], start=True, stop=False, skip_group_check=True)

            pe.sem_inc(used, RING)
            def score(l, e):
                if e >= 2:
                    pe.wait_ge(exp_done, l * 16 + (e - 1))
                h = HEADS[e]
                if e < NHA:
                    g, i, qT, kT = h // GROUP, h % GROUP, qkTA, 4
                    if e == 0:
                        pe.wait_ge(qkA_T, l + 1)
                else:
                    g, i, qT = h % 2, (h - NHA) // 2, qkTB
                    kT = 4 + i
                    if e == NHA:
                        pe.wait_ge(qB_T, l + 1)
                        pe.wait_ge(kB_T, l + 1)
                rows_ = slice(HD * g, HD * g + HD)
                for t in range(T):
                    last = nc.tensor.matmul(work[:, 2 + e % 2, t * SEQ:(t + 1) * SEQ], qT[rows_, i, t * P:(t + 1) * P],
                                            qT[rows_, kT, :], start=True, stop=True)
                last.then_inc(s_ready, 1)

            def turn(l, e):
                pe.wait_ge(exp_done, l * 16 + (e + 1))
                bank = turned_bank(e)
                if e < 2:
                    pe.wait_ge(qB_T, l + 1)
                    pe.wait_ge(kB_T, l + 1)
                elif e < 4:
                    pe.wait_ge(proj_ready, l * WIN + WIN)
                elif e < NHA + 2:
                    pe.wait_ge(pTA, l * 8 + (e - 1))
                else:
                    pe.wait_ge(pTB, l * 8 + (e - NHA - 1))
                for kt in range(T):
                    for t in range(T):
                        last = nc.tensor.transpose(bank[:, kt * SEQ + t * P:kt * SEQ + (t + 1) * P],
                                                   prob[:, e % 2, t * SEQ + kt * P:t * SEQ + (kt + 1) * P], ident[:, :])
                last.then_inc(pT_ps, 1)

            def apply(l, e):
                h = HEADS[e]
                if e < NHA:
                    pe.wait_ge(pTA, l * 8 + (e + 1))
                    v0, b0 = VA0 + (h // GROUP) * HD, 2
                else:
                    pe.wait_ge(pTB, l * 8 + (e - NHA + 1))
                    v0, b0 = VB0 + (h - NHA) * HD, 0
                at = (h % NHA) * HD
                for t in range(T):
                    for kt in range(T):
                        last = nc.tensor.matmul(acc[:, b0 + t, at:at + HD], probT[:, e % 2, kt * SEQ + t * P:kt * SEQ + (t + 1) * P],
                                                proj[:, kt, v0:v0 + HD], start=(kt == 0), stop=(kt == T - 1))
                last.then_inc(pv_done, 1)

            def out(l, j):
                k0, nk, group = sum(OUT1[:j]), OUT1[j], j // 2
                pe.wait_ge(yT_lo, l * 8 + 4 * (group + 1))
                down(g1(l, WIN + j), (WIN + j) % RING, lambda k: (a_hi[:, k0 + k, :], a_lo[:, k0 + k, :]), nk,
                     (work, acc)[group], start=(j % 2 == 0), stop=(j % 2 == 1), quarters=(j == len(OUT1) - 1))

            pe.wait_ge(id_loaded, 16)
            pe.wait_ge(zeroed, 1)
            pe.wait_ge(rows_loaded, 16 * 3)
            at = 0
            for n in range(3):
                nc.tensor.transpose(acc[:, 0, at:at + NROWS[n]], rows[n][0:NROWS[n], :], ident[0:NROWS[n], 0:NROWS[n]])\
                    .then_inc(rowsT, 1)
                at += NROWS[n]
            pe.wait_ge(cols_ready, 4)

            with pe.Fori(0, DEPTH) as l:
                turn_norm(l * 2, x_tok, x_done, l * 8)
                for kind, n in PLAN1:
                    if kind == "chunk":
                        if n >= 2:
                            pe.wait_ge(proj_ready, l * WIN + (n - 1))
                        by_tokens(g1(l, n), n % RING, n % 2, l * 2 if n == 0 else None)
                    elif kind == "tA":
                        for t in range(T):
                            pe.wait_ge(ropeA_done, l * T + (t + 1))
                            for i in range(5):
                                last = nc.tensor.transpose(acc_flat[:, i * SEQ + t * P:i * SEQ + (t + 1) * P],
                                                           qkA[:, t, i * P:(i + 1) * P], ident[:, :])
                        last.then_inc(qkA_ps, 1)
                    elif kind == "tB":
                        pe.wait_ge(qkA_T, l + 1)
                        for t in range(T):
                            pe.wait_ge(ropeB_done, l * T + (t + 1))
                            for i in range(8):
                                last = nc.tensor.transpose(acc_flat[:, i * SEQ + t * P:i * SEQ + (t + 1) * P],
                                                           proj[:, t, QB0 + i * P:QB0 + (i + 1) * P], ident[:, :])
                        last.then_inc(qkB_ps, 1)
                    elif kind == "score":
                        score(l, n)
                    elif kind == "turn":
                        turn(l, n)
                    elif kind == "pv":
                        apply(l, n)
                    elif kind == "out":
                        out(l, n)
                    elif kind == "yturn":
                        dst = acc_flat[:, 1024:2048]
                        pe.wait_ge(y_ready, l * 4 + (2 * n + T))
                        for t in range(T):
                            for k in range(4):
                                last = nc.tensor.transpose(dst[:, k * SEQ + t * P:k * SEQ + (t + 1) * P],
                                                           y_tok[:, t, n * 512 + k * P:n * 512 + (k + 1) * P], ident[:, :])
                        last.then_inc(yT_ps, 1)
                out(l, 1)
                out(l, 2)
                out(l, 3)
                turn_norm(l * 2 + 1, x_tok, x_done, l * 8 + 4)

                def hidden(slot):
                    return lambda k: (h_hi[:, slot, k * SEQ:(k + 1) * SEQ], h_lo[:, slot, k * SEQ:(k + 1) * SEQ])

                by_features(g1(l, MLP0), MLP0 % RING, 0, l * 2 + 1)
                open_sums()
                with pe.Fori(0, (NI1 - 1) // 3) as it:
                    for j in range(3):
                        i, c = it * 3 + (1 + j), MLP0 + 1 + 2 * j
                        pe.wait_ge(relu_done, l * NI1 + i)
                        by_features(g1(l, c) + it * 6, c % RING, 0)
                        pe.wait_ge(h1_lo, l * NI1 + i)
                        down(g1(l, c + 1) + it * 6, (c + 1) % RING, hidden(j % 3), 2)
                pe.wait_ge(h1_lo, l * NI1 + NI1)
                down(g1(l, CH1 - 1), (CH1 - 1) % RING, hidden((NI1 - 1) % 3), 2, stop=True, quarters=True)


            def ffn(l, f, cb, norm):
                def hidden(slot):
                    return lambda k: (h_hi[:, slot, k * SEQ:(k + 1) * SEQ], h_lo[:, slot, k * SEQ:(k + 1) * SEQ])

                m = (l * 2 + f) * NI2
                by_features(g2(l, cb), 0, 0, norm)
                by_features(g2(l, cb + 1), 1, 1)
                open_sums()
                with pe.Fori(0, NI2 - 1) as it:
                    pe.wait_ge(silu_done, m + it + 1)
                    by_features(g2(l, cb + 2) + it * 3, 2, 0)
                    pe.wait_ge(h2_f, m + it + 1)
                    by_features(g2(l, cb + 3) + it * 3, 0, 1)
                    pe.wait_ge(h2_lo, m + it + 1)
                    down(g2(l, cb + 4) + it * 3, 1, hidden(0), 2)
                pe.wait_ge(h2_lo, m + NI2)
                down(g2(l, cb + FFN - 1), 2, hidden(1), 2, stop=True, quarters=True)

            with pe.Fori(0, DEPTH) as l:
                norm0 = l * 3 + (2 * DEPTH + 1)
                turn_norm(norm0 - 1, xn, xn_ready, l * 12)
                ffn(l, 0, 0, norm0 - 1)
                turn_norm(norm0, xn, xn_ready, l * 12 + 4)
                pe.wait_ge(sgu_masked, l + 1)
                for h in range(AH):
                    last = nc.tensor.transpose(acc[:, 2, h * P:(h + 1) * P], sgu_rows[:, h, :], ident[:, :])
                last.then_inc(sgu_ps, 1)
                for j in range(WIN):
                    c = FFN + j
                    if j >= 2:
                        pe.wait_ge(z_done, l * 8 + (j - 1))
                    if j in (2, 3):
                        by_tokens(g2(l, c), c % RING, j % 2)
                    else:
                        by_features(g2(l, c), c % RING, j % 2, norm0 if j == 0 else None)
                    if j == 3:
                        pe.wait_ge(mix_bd, l * 64 + 64)
                        pe.wait_ge(conv_done, l * CT + CT)
                        pe.wait_ge(sgu_T, l + 1)
                        for n in range(2):
                            dst = (work_flat[:, 1024:2048], acc_flat[:, 0:1024])[n]
                            for i in range(CT):
                                last = nc.tensor.matmul(dst[:, i * SEQ:(i + 1) * SEQ], bd[:, n, i, :], xr[:, i * SEQ:(i + 1) * SEQ],
                                                        start=True, stop=True)
                            last.then_inc(gate_ps, 1)
                    if j == 5:
                        pe.wait_ge(v_done, l * T + T)
                        for t in range(T):
                            for h in range(AH):
                                at = t * 256 + h * HD
                                last = nc.tensor.matmul(acc[:, 2, at:at + HD], sguT[:, h, :], vn[:, at:at + HD], start=True, stop=True)
                        last.then_inc(mix_ps, 1)
                    if j == 6:
                        pe.wait_ge(ya_done, l * AH + AH)
                        for t in range(T):
                            for k in range(2):
                                last = nc.tensor.transpose(acc[:, 3, k * SEQ + t * P:k * SEQ + (t + 1) * P],
                                                           ya[:, t * 256 + k * P:t * 256 + (k + 1) * P], ident[:, :])
                        last.then_inc(yaT_ps, 1)
                k0 = 0
                for j, nk in enumerate(OUT2):
                    pe.wait_ge(y2_lo, l * 4 + (2, 3, 3, 4, 4, 4)[j])
                    if j == 0:
                        pe.wait_ge(sig_done, l * 2 * CT + 2 * CT)
                    down(g2(l, FFN + WIN + j), j % RING, lambda k, k0=k0: mixed(k0 + k), nk,
                         start=(j == 0), stop=(j == len(OUT2) - 1), quarters=(j == len(OUT2) - 1))
                    k0 += nk
                turn_norm(norm0 + 1, xn, xn_ready, l * 12 + 8)
                ffn(l, 1, FFN + WIN + len(OUT2), norm0 + 1)
            pe.sem_inc(xT, 8)


def tables():
    pos = np.arange(SEQ)

    def rotation(p, half, theta):
        freqs = np.float32(theta) ** (-np.arange(half, dtype=np.float32) / np.float32(half))
        ang = p.astype(np.float32)[:, None] * freqs.astype(np.float32)[None, :]
        cos, sin = np.cos(ang.astype(np.float64)), np.sin(ang.astype(np.float64))
        return np.concatenate([cos, cos], -1), np.concatenate([-sin, sin], -1)

    def tiled(a):
        return np.ascontiguousarray(a.reshape(T, P, -1).transpose(1, 0, 2).astype(np.float32))

    (cr, sr), (cc, sc) = rotation(pos // 64, 16, 10000.0), rotation(pos % 64, 16, 10000.0)
    cp, sn = rotation(pos, 8, 500000.0)
    d = np.abs(pos[:, None] - pos[None, :])
    count = sum((d % dil == 0) & (d <= window // 2) for window, dil in ((128, 1), (512, 4), (2048, 16)))
    logc = np.where(count > 0, np.log(np.maximum(count, 1)), -1e30)
    return {"c_ident": np.eye(P, dtype=np.float32), "c_rope_ax": tiled(np.concatenate([cr, cc, sr, sc], -1)),
            "c_rope_pt": tiled(np.concatenate([cp, sn], -1)), "c_logc": tiled(logc)}


_INS = {
    "x": (SEQ, D), "w_in": None, "q_norm": None, "k_norm": None, "w_out": None, "w_mlp_in": None, "w_mlp_out": None,
    "final_norm": None, "ln_g_2": (-1, D), "ln_b_2": (-1, D), "ffn_w_gate_2": (2 * DEPTH, D, FF2), "ffn_w_up_2": (2 * DEPTH, D, FF2),
    "ffn_w_down_2": (2 * DEPTH, FF2, D), "w_in_2": None, "sgu_ln_g_2": None, "sgu_ln_b_2": None, "sgu_w_2": None,
    "rg_w_a_2": None, "rg_w_i_2": None, "w_out_2": None,
}


def kernel(**inputs):
    import concourse.bacc as _bacc
    from concourse.bass_utils import run_bass_kernel_spmd as _run

    nc = _bacc.Bacc("TRN2", target_bir_lowering=False, num_devices=1)
    arrays, ins = {}, {}
    for name, shape in _INS.items():
        a = np.ascontiguousarray(inputs[name])
        arrays[name] = a if shape is None else a.reshape(shape)
    arrays.update(tables())
    arrays["rows"] = np.concatenate([np.asarray(inputs[name]).reshape(-1, P)[l * n:(l + 1) * n]
                                     for group in ROWS for name, l, n in group])
    for name, a in arrays.items():
        ins[name] = nc.dram_tensor(name, a.shape, mybir.dt.from_np(a.dtype), kind="ExternalInput").ap()
    out = nc.dram_tensor("y", (SEQ, D), mybir.dt.float32, kind="ExternalOutput").ap()
    program(nc, ins, out)
    r = _run(nc, [arrays], core_ids=[0])
    return r.results[0]["y"].reshape(1, SEQ, D)
```

```python
import math
from contextlib import ExitStack

import concourse.bass as bass
import numpy as np
from concourse import mybir

P = 128
SEQ, D, DEPTH, HD = 256, 1024, 2, 64
T = SEQ // P
KD = D // P
FF1, FF2 = 4096, 2816
NHA, NKV, NHB = 8, 2, 8
GROUP = NHA // NKV
IN_W = 2304
QKA = (NHA + NKV) * HD
VA0 = QKA
QB0 = VA0 + NKV * HD
VB0 = QB0 + 2 * NHB * HD
SCALE = HD ** -0.5
RMS_EPS, LN_EPS = 1e-6, 1e-5
ALPHA = (2.0 * DEPTH) ** 0.25
AH, CONV_B, CONV_C, CT = 4, 3, 4, 4
RG_C = 8.0

RING, CW = 3, 2048
BLK = CW // KD
NI1, NI2 = FF1 // BLK, FF2 // BLK
WIN = IN_W // BLK
OUT1 = [2, 2, 2, 2]
OUT2 = [2, 1, 1, 1, 1, 2]
MLP0 = WIN + len(OUT1)
CH1 = MLP0 + 2 * NI1
FFN = 3 * NI2
CH2 = 2 * FFN + WIN + len(OUT2)
assert CH1 % RING == 0 and CH2 % RING == 0 and FFN % RING == 0
KORDER2 = [0, 1, 4, 5, 6, 7, 2, 3]
POOL1 = range(6, WIN + RING)
POOL2 = range(5, WIN)
ZORDER = [7, 8, 0, 1, 5, 6, 2, 3, 4]

C1 = 3 * KD
N2 = 6 * KD
LN0 = DEPTH * C1 + N2
M_CONV, M_CB, M_BA, M_BI, M_LAM = 0, 16, 20, 24, 28
M_SC, M_SGB = 32, 38
NM = 42
MX0 = LN0 + DEPTH * N2
NCOL = MX0 + DEPTH * NM
WARM = 16
ORD1, ORD2, ORDP = 68, 101, 6
HEADS = [0, 4, 1, 5, 2, 6, 3, 7] + list(range(8, 16))


def plan1():
    plan = [("chunk", 0), ("split", 3), ("chunk", 1), ("split", 4), ("chunk", 2), ("split", 5), ("ropeA", 0)]
    plan += [("chunk", 3), ("split", 6), ("chunk", 4), ("split", 7), ("chunk", 5), ("split", 8), ("tA", 0)]
    plan += [("chunk", 6), ("score", 0), ("score", 1), ("ropeB", 0), ("chunk", 7), ("tB", 0), ("split", 9)]
    plan += [("score", 2), ("score", 3), ("chunk", 8), ("turn", 0), ("turn", 1), ("pv", 0), ("pv", 1)]
    between = {5: [("split", 10)], 7: [("split", 11)], 10: [("yscale", 0)], 11: [("yscale", 1)], 12: [("yturn", 0)],
               13: [("yhi", 0)], 14: [("yhi", 1)], 15: [("yhi", 2), ("ylo", 0)], 16: [("yhi", 3), ("ylo", 1)],
               17: [("ylo", 2)], 18: [("ylo", 3)]}
    for step in range(4, NHA + NHB + 3):
        plan += [(kind, e) for kind, e, least in (("score", step, 4), ("turn", step - 2, 2), ("pv", step - 3, 2))
                 if least <= e < NHA + NHB]
        plan += between.get(step, [])
    return plan + [("yscale", 2), ("yscale", 3), ("out", 0), ("yturn", 1)] + [("yhi", k) for k in range(4, 8)] \
        + [("ylo", k) for k in range(4, 8)]


PLAN1 = plan1()
ROWS = [
    [(name, l, n) for l in range(DEPTH) for name, n in (("norm1", 8), ("norm2", 8), ("out_norm_a", 4), ("out_norm_b", 4))],
    [(name, l, 24) for l in range(DEPTH) for name in ("ln_g_2", "ln_b_2")],
    [(name, l, n) for l in range(DEPTH) for name, n in (
        ("rg_conv_w_2", 16), ("rg_conv_b_2", 4), ("rg_b_a_2", 4), ("rg_b_i_2", 4), ("rg_lambda_2", 4), ("sconv_w_2", 6), ("sgu_b_2", 4))]
    + [("final_norm", 0, 8)],
]
NROWS = [DEPTH * C1, DEPTH * N2, DEPTH * NM + KD]
LAST_LN = LN0 - N2 + 2 * KD


def program(nc, ins, out):
    f32, f32r, i32 = mybir.dt.float32, mybir.dt.float32r, mybir.dt.int32
    bf16 = mybir.dt.bfloat16
    ALU, ACT, AX = mybir.AluOpType, mybir.ActivationFunctionType, mybir.AxisListType
    ds = bass.ds
    ctx = ExitStack()
    with ctx:
        def sb(name, shape, dt=f32):
            return ctx.enter_context(nc.sbuf_tensor(name, shape, dt))

        def sem(name):
            return ctx.enter_context(nc.semaphore(name))

        raw = sb("raw", [P, RING, CW])
        w_hi = sb("w_hi", [P, RING, CW], f32r)
        w_lo = sb("w_lo", [P, RING, CW], f32r)
        x_tok = sb("x_tok", [P, T, D])
        xn = sb("xn", [P, T, D])
        a_hi = sb("a_hi", [P, KD, SEQ], f32r)
        a_lo = sb("a_lo", [P, KD, SEQ], f32r)
        relu = sb("relu", [P, 2 * SEQ])
        hid = sb("hid", [P, 2 * SEQ])
        h_hi = sb("h_hi", [P, 3, 2 * SEQ], f32r)
        h_lo = sb("h_lo", [P, 3, 2 * SEQ], f32r)
        proj = sb("proj", [P, T, IN_W])
        sqs = sb("sqs", [P, T, QKA])
        rope_a = sb("rope_a", [P, T, QKA])
        rope_b = sb("rope_b", [P, T, QKA])
        qkA = rope_b
        qkTB = sb("qkTB", [P, 8, SEQ])
        cg = sb("cg", [P, T, QKA])
        sg = sb("sg", [P, T, QKA])
        qkTA = cg[:, :, :].rearrange("p a b -> p (a b)").rearrange("p (i s) -> p i s", s=SEQ)
        masked = sb("masked", [P, 2, T * SEQ])
        prob = sb("prob", [P, 2, T * SEQ])
        probT = sb("probT", [P, 2, T * SEQ])
        y_tok = sb("y_tok", [P, T, D])
        ident = sb("ident", [P, P])
        rope_ax = sb("rope_ax", [P, T, 2 * HD])
        rope_pt = sb("rope_pt", [P, T, 32])
        logc = sb("logc", [P, T, SEQ])
        qk_gain = sb("qk_gain", [P, 2 * HD])
        g_bc = masked[:, :, :].rearrange("p a b -> p (a b)")
        b_bc = prob[:, :, :].rearrange("p a b -> p (a b)")
        rows = [y_tok[:, 0, n * P:(n + 1) * P] for n in range(3)]
        cols = sb("cols", [P, NCOL])
        zero = sb("zero", [P, 512], bf16)
        ss = sb("ss", [P, 8])
        stat = sb("stat", [P, T, 2, 6])
        mv = sb("mv", [P, T, 2])
        nwt = sb("nwt", [P, 4, 20])
        rstd = sb("rstd", [P, T])
        shift = sb("shift", [P, 4])
        rms2 = sb("rms2", [P, 2, T])
        ssA = sb("ssA", [P, 20])
        rstdA = sb("rstdA", [P, 20])
        ssy = sb("ssy", [P, 4])
        rstdy = sb("rstdy", [P, 4])
        nmax = sb("nmax", [P, 16, T])
        rsum = sb("rsum", [P, 16, T])
        rinv = sb("rinv", [P, 16, T])
        sgu_gb = sb("sgu_gb", [P, 2, 256])
        bd = sb("bd", [P, 2, CT, P])
        sp = sb("sp", [P, 4, DEPTH * CT])

        def part(tensor, n, width):
            return tensor[:, :, :].rearrange("p a b -> p (a b)")[:, n * width:(n + 1) * width]

        W4 = CT * SEQ
        xr = part(proj, 0, W4)
        r_gate = part(proj, 1, W4)
        i_gate = part(proj, 2, W4)
        th = part(proj, 3, W4)
        gg = part(y_tok, 0, W4)
        root = part(qkTB, 0, W4)
        a_dec = part(qkTB, 1, W4)
        q_rec = part(y_tok, 1, W4)
        hs = part(sqs, 0, W4)
        ug = part(cg, 0, 512)
        vg = part(cg, 1, 512)
        vn = part(sg, 0, 512)
        ya = part(sg, 1, 512)
        bg = part(rope_a, 0, 512)
        cgt = part(rope_a, 1, 512)
        yb = part(proj, 8, 512)
        xrp = part(rope_b, 0, CT * (SEQ + CONV_C - 1)).rearrange("p (c s) -> p c s", c=CT)
        cxp = part(probT, 0, 2 * (SEQ + CONV_B - 1)).rearrange("p (c s) -> p c s", c=2)
        sgu_rows = part(qkTB, 0, AH * P).rearrange("p (h s) -> p h s", h=AH)
        sguT = part(logc, 0, AH * P).rearrange("p (h s) -> p h s", h=AH)
        affine = [x[:, n * SEQ:(n + 1) * SEQ] for x in (relu, hid) for n in range(2)]
        h_hi_flat = h_hi[:, :, :].rearrange("p a b -> p (a b)")
        h_lo_flat = h_lo[:, :, :].rearrange("p a b -> p (a b)")

        def mixed(at, n=1):
            if at < 6:
                return [h[:, at * SEQ:(at + n) * SEQ] for h in (h_hi_flat, h_lo_flat)]
            return [a[:, at - 6:at - 6 + n, :].rearrange("p a b -> p (a b)") for a in (a_hi, a_lo)]

        acc = ctx.enter_context(nc.psum_tensor("acc", [P, 4, 512], f32))
        work = ctx.enter_context(nc.psum_tensor("work", [P, 4, 512], f32))

        def turned_bank(e):
            return (acc if e < 2 else work)[:, e % 2, :]

        acc_flat = acc[:, :, :].rearrange("p a b -> p (a b)")
        work_flat = work[:, :, :].rearrange("p a b -> p (a b)")

        loaded = [sem(f"loaded{s}") for s in range(RING)]
        hi_done, lo_done, used = sem("hi_done"), sem("lo_done"), sem("used")
        x_loaded, id_loaded, tab_loaded, rows_loaded = (sem(n) for n in ("x_loaded", "id_loaded", "tab_loaded", "rows_loaded"))
        rowsT, cols_ready, zeroed, pads, conv_pads = (sem(n) for n in ("rowsT", "cols_ready", "zeroed", "pads", "conv_pads"))
        lam_abs, lam_exp, sp_ready = (sem(n) for n in ("lam_abs", "lam_exp", "sp_ready"))
        shift_ready, affine_done, tile0_sums, tile0_stat, mean_ready = (
            sem(n) for n in ("shift_ready", "affine_done", "tile0_sums", "tile0_stat", "mean_ready"))
        xn_ready = [sem(f"xn_ready{t}") for t in range(T)]
        sums, x_done, sq_sum, xT, aT_hi, aT_lo, rstd_ready = (
            sem(n) for n in ("sums", "x_done", "sq_sum", "xT", "aT_hi", "aT_lo", "rstd_ready"))
        gb_loaded, x_affine, x_scaled, pool_order = (sem(n) for n in ("gb_loaded", "x_affine", "x_scaled", "pool_order"))
        dve_order = sem("dve_order")
        gain_loaded, rope_tab, proj_ready, qk_sq, ropeA_done, ropeB_done = (
            sem(n) for n in ("gain_loaded", "rope_tab", "proj_ready", "qk_sq", "ropeA_done", "ropeB_done"))
        qkA_ps, qkA_T, qkB_ps, qB_T, kB_T = (sem(n) for n in ("qkA_ps", "qkA_T", "qkB_ps", "qB_T", "kB_T"))
        s_ready, nmax_ready, exp_done, pT_ps, pTA, pTB, pv_done = (
            sem(n) for n in ("s_ready", "nmax_ready", "exp_done", "pT_ps", "pTA", "pTB", "pv_done"))
        y_ready, y_sq, yT_ps, yT_hi, yT_lo = (sem(n) for n in ("y_ready", "y_sq", "yT_ps", "yT_hi", "yT_lo"))
        relu_done, h1_sq, h1_hi, h1_lo = (sem(n) for n in ("relu_done", "h1_sq", "h1_hi", "h1_lo"))
        silu_done, h2_f, h2_hi, h2_lo = (sem(n) for n in ("silu_done", "h2_f", "h2_hi", "h2_lo"))
        mix_w, mix_bd, sgu_masked, sgu_ps, sgu_T = (sem(n) for n in ("mix_w", "mix_bd", "sgu_masked", "sgu_ps", "sgu_T"))
        tap0_done = sem("tap0_done")
        z_done, cx_done, conv_done, gate_ps, sig_done, th_done, th_pos, root_done = (
            sem(n) for n in ("z_done", "cx_done", "conv_done", "gate_ps", "sig_done", "th_done", "th_pos", "root_done"))
        v_done, mix_ps, ya_done, yaT_ps, y2_f, y2_hi, y2_lo = (
            sem(n) for n in ("v_done", "mix_ps", "ya_done", "yaT_ps", "y2_f", "y2_hi", "y2_lo"))
        tile1_out, out_done = sem("tile1_out"), sem("out_done")
        passed_sp, passed_pool, passed_dve = sem("passed_sp"), sem("passed_pool"), sem("passed_dve")

        def turned_value(norm, bank):
            return norm * 8 + (3, 4, 7, 8)[bank]

        BASE2 = DEPTH * CH1

        def g1(l, c):
            return l * CH1 + c

        def g2(l, c):
            return l * CH2 + (BASE2 + c)

        def round1(l, c):
            return l * (CH1 // RING) + (c // RING + 1)

        def round2(l, c):
            return l * (CH2 // RING) + (BASE2 // RING + c // RING + 1)

        block = ctx.enter_context(nc.Block())

        @block.sync
        def _(sp_):
            sp_.dma_start(ident[:, :], ins["c_ident"]).then_inc(id_loaded, 16)
            for n in range(3):
                sp_.dma_start(rows[n][0:NROWS[n], :], ins["rows"][sum(NROWS[:n]):sum(NROWS[:n + 1]), :]).then_inc(rows_loaded, 16)
            for t in range(T):
                sp_.dma_start(x_tok[:, t, :], ins["x"][t * P:(t + 1) * P, :]).then_inc(x_loaded, 16)

            def slot_free(g):
                sp_.wait_ge(lo_done, g + 1)
                sp_.sem_inc(passed_sp, 1)

            def load(g, slot, src, k):
                slot_free(g)
                sp_.dma_start(raw[:, slot, :].rearrange("p (k n) -> p k n", k=k), src).then_inc(loaded[slot], 16)

            def wide(name, l, at):
                return ins[name][ds(l, 1), :, ds(at, BLK)].rearrange("o (k p) n -> p (o k) n", p=P)

            def tall(name, l, at, k):
                return ins[name][ds(l, 1), ds(at, k * P), :].rearrange("o (k p) n -> p (o k) n", p=P)

            with sp_.Fori(0, DEPTH) as l:
                for c in range(WIN):
                    load(g1(l, c), c % RING, wide("w_in", l, c * BLK), KD)
                at = 0
                for j, k in enumerate(OUT1):
                    load(g1(l, WIN + j), (WIN + j) % RING, tall("w_out", l, at, k), k)
                    at += k * P
                load(g1(l, MLP0), MLP0 % RING, wide("w_mlp_in", l, 0), KD)
                with sp_.Fori(0, (NI1 - 1) // 3) as it:
                    for j in range(3):
                        i, c = it * 3 + (1 + j), MLP0 + 1 + 2 * j
                        load(g1(l, c) + it * 6, c % RING, wide("w_mlp_in", l, i * BLK), KD)
                        load(g1(l, c + 1) + it * 6, (c + 1) % RING, tall("w_mlp_out", l, (i - 1) * BLK, 2), 2)
                load(g1(l, CH1 - 1), (CH1 - 1) % RING, tall("w_mlp_out", l, (NI1 - 1) * BLK, 2), 2)

            def ffn(l, f, cb):
                m = l * 2 + f
                load(g2(l, cb), 0, wide("ffn_w_gate_2", m, 0), KD)
                load(g2(l, cb + 1), 1, wide("ffn_w_up_2", m, 0), KD)
                with sp_.Fori(0, NI2 - 1) as it:
                    i = it + 1
                    load(g2(l, cb + 2) + it * 3, 2, wide("ffn_w_gate_2", m, i * BLK), KD)
                    load(g2(l, cb + 3) + it * 3, 0, wide("ffn_w_up_2", m, i * BLK), KD)
                    load(g2(l, cb + 4) + it * 3, 1, tall("ffn_w_down_2", m, it * BLK, 2), 2)
                load(g2(l, cb + FFN - 1), 2, tall("ffn_w_down_2", m, (NI2 - 1) * BLK, 2), 2)

            with sp_.Fori(0, DEPTH) as l:
                ffn(l, 0, 0)
                for j, b in enumerate(ZORDER):
                    load(g2(l, FFN + j), j % RING, wide("w_in_2", l, b * BLK), KD)
                for j, k in enumerate(OUT2):
                    c = FFN + WIN + j
                    slot_free(g2(l, c))
                    sp_.dma_start(raw[:, c % RING, 0:k * D].rearrange("p (k n) -> p k n", k=k),
                                  tall("w_out_2", l, KORDER2[sum(OUT2[:j])] * P, k)).then_inc(loaded[c % RING], 16)
                ffn(l, 1, FFN + WIN + len(OUT2))
            for c in range(2):
                slot_free(BASE2 + DEPTH * CH2 + c)
                sp_.sem_inc(loaded[c], 16)
            for t in range(T):
                if t == 0:
                    sp_.wait_ge(x_affine, 3 * DEPTH * T + 1)
                else:
                    sp_.wait_ge(tile1_out, 1)
                sp_.dma_start(out[t * P:(t + 1) * P, :], xn[:, t, :]).then_inc(out_done, 16)
            sp_.wait_ge(out_done, 16 * T)

        @block.gpsimd
        def _(pool):
            n_order = [0]

            def link(ins_, base=0):
                n_order[0] += 1
                ins_.then_inc(pool_order, 1)
                pool.wait_ge(pool_order, base + n_order[0])
                pool.sem_inc(passed_pool, 1)

            def lo_part(g, slot):
                pool.wait_ge(hi_done, g + 1)
                pool.wait_ge(lo_done, g + 3)
                nc.gpsimd.tensor_tensor(w_lo[:, slot, :], raw[:, slot, :], w_hi[:, slot, :].bitcast(f32), ALU.subtract)\
                    .then_inc(lo_done, 1)

            nc.gpsimd.memset(bd[:, :, :, :], 0.0).then_inc(pads, 1)
            nc.gpsimd.memset(zero[:, :], 0.0).then_inc(zeroed, 1)
            pool.wait_ge(x_loaded, 16 * T)
            pool.dma_start(rope_ax[:, :, :], ins["c_rope_ax"]).then_inc(tab_loaded, 16)
            pool.dma_start(rope_pt[:, :, :], ins["c_rope_pt"]).then_inc(tab_loaded, 16)
            pool.dma_start(logc[:, :, :], ins["c_logc"]).then_inc(tab_loaded, 16)
            pool.wait_ge(tab_loaded, 48)
            with pool.Fori(0, DEPTH) as l:
                pool.dma_start(qk_gain[:, 0:HD], ins["q_norm"][ds(l, 1), :].rearrange("o n -> (o n)").partition_broadcast(P))\
                    .then_inc(gain_loaded, 16)
                pool.dma_start(qk_gain[:, HD:], ins["k_norm"][ds(l, 1), :].rearrange("o n -> (o n)").partition_broadcast(P))\
                    .then_inc(gain_loaded, 16)
                pool.wait_ge(gain_loaded, l * 32 + 32)
                for t in range(T):
                    for h0, n, g0 in ((0, NHA, 0), (NHA, NKV, HD)):
                        span = slice(h0 * HD, (h0 + n) * HD)
                        gain = qk_gain[:, g0:g0 + HD]
                        nc.gpsimd.tensor_tensor(
                            cg[:, t, span].rearrange("p (h d) -> p h d", d=HD),
                            rope_ax[:, t, 0:HD].unsqueeze(1).broadcast_to((P, n, HD)),
                            gain.unsqueeze(1).broadcast_to((P, n, HD)), ALU.mult).then_inc(rope_tab, 1)
                        for half in range(2):
                            for ax in range(2):
                                at = 32 * ax + 16 * half
                                other = 32 * ax + 16 * (1 - half)
                                nc.gpsimd.tensor_tensor(
                                    sg[:, t, span].rearrange("p (h d) -> p h d", d=HD)[:, :, at:at + 16],
                                    rope_ax[:, t, HD + at:HD + at + 16].unsqueeze(1).broadcast_to((P, n, 16)),
                                    gain[:, other:other + 16].unsqueeze(1).broadcast_to((P, n, 16)),
                                    ALU.mult).then_inc(rope_tab, 1)
                for c in POOL1:
                    lo_part(g1(l, c), c % RING)
                pool.wait_ge(pv_done, l * 16 + 16)

            def lower(norm):
                for k in range(KD):
                    pool.wait_ge(aT_hi, norm * KD + (k + 1))
                    nc.gpsimd.tensor_tensor(a_lo[:, k, :], affine[k % 4], a_hi[:, k, :].bitcast(f32), ALU.subtract)\
                        .then_inc(aT_lo, 1)

            def affine_rows(norm, t, base, n_gb):
                pool.wait_ge(gb_loaded, n_gb)
                pool.wait_ge(xn_ready[t], (norm - 2 * DEPTH) * 2 + 2)
                link(nc.gpsimd.tensor_tensor(xn[:, t, :], xn[:, t, :], g_bc[:, :], ALU.mult), base)
                nc.gpsimd.tensor_tensor(xn[:, t, :], xn[:, t, :], b_bc[:, :], ALU.add).then_inc(x_affine, 1)

            def affine_and_scale(norm, base, n_gb):
                for t in range(T):
                    pool.wait_ge(xT, norm * 8 + (6 + 2 * t))
                    affine_rows(norm, t, base, n_gb)
                    pool.wait_ge(x_affine, (norm - 2 * DEPTH) * T + (t + 1))
                    pool.sem_inc(passed_pool, 1)
                    nc.gpsimd.tensor_scalar(x_tok[:, t, :], xn[:, t, :], ALPHA, None, ALU.mult).then_inc(x_scaled, 1)

            def load_gb(row):
                pool.dma_start(g_bc[:, :], ins["ln_g_2"][ds(row, 1), :].rearrange("o n -> (o n)").partition_broadcast(P))\
                    .then_inc(gb_loaded, 16)
                pool.dma_start(b_bc[:, :], ins["ln_b_2"][ds(row, 1), :].rearrange("o n -> (o n)").partition_broadcast(P))\
                    .then_inc(gb_loaded, 16)

            pool.dma_start(g_bc[:, :], ins["final_norm"].partition_broadcast(P)).then_inc(gb_loaded, 16)
            link(nc.gpsimd.memset(b_bc[:, :], 0.0))
            base0 = n_order[0]
            with pool.Fori(0, DEPTH) as l:
                base, norm0, gb = l * ORDP, l * 3 + (2 * DEPTH + 1), l * 96 + 16
                lower(norm0 - 1)
                affine_and_scale(norm0 - 1, base, gb)
                load_gb(l * 3)
                pool.dma_start(sgu_rows[:, :, :], ins["sgu_w_2"][ds(l, 1), :, :, :].rearrange("o h t s -> t (o h) s"))\
                    .then_inc(mix_w, 16)
                for n, name in enumerate(("sgu_ln_g_2", "sgu_ln_b_2")):
                    pool.dma_start(sgu_gb[:, n, :], ins[name][ds(l, 1), :].rearrange("o n -> (o n)").partition_broadcast(P))\
                        .then_inc(mix_w, 16)
                pool.wait_ge(pads, 1)
                for n, name in enumerate(("rg_w_a_2", "rg_w_i_2")):
                    for odd in range(2):
                        pool.dma_start(bd[64 * odd:64 * odd + 64, n, :, 64 * odd:64 * odd + 64],
                                       ins[name][ds(l, 1), odd::2, :, :].rearrange("o h d e -> d (o h) e"))\
                            .then_inc(mix_bd, 16)
                pool.wait_ge(mix_w, l * 48 + 48)
                pool.sem_inc(passed_pool, 1)
                nc.gpsimd.affine_select(out=sgu_rows[:, :, :], in_=sgu_rows[:, :, :], pattern=[[0, AH], [-1, P]],
                                        compare_op=ALU.is_ge, fill=0.0, base=0, channel_multiplier=1).then_inc(sgu_masked, 1)
                lower(norm0)
                affine_and_scale(norm0, base, gb + 32)
                load_gb(l * 3 + 1)
                for j in POOL2:
                    lo_part(l * CH2 + (BASE2 + FFN + j), j % RING)
                lower(norm0 + 1)
                affine_and_scale(norm0 + 1, base, gb + 64)
                load_gb(l * 3 + 2)
                assert n_order[0] - base0 == ORDP, n_order[0] - base0
            affine_rows(5 * DEPTH, 0, (DEPTH - 1) * ORDP, DEPTH * 96 + 16)

        @block.scalar
        def _(act):
            def width(c, outs, at):
                return outs[c - at] * D if at <= c < at + len(outs) else CW

            def split_hi(g, rnd, slot, w=CW):
                act.wait_ge(loaded[slot], rnd * 16)
                act.wait_ge(used, g + 1)
                nc.scalar.activation(w_hi[:, slot, 0:w], raw[:, slot, 0:w], ACT.Copy).then_inc(hi_done, 1)

            def split1(l, c, it=0):
                split_hi(g1(l, c) + it * 6, round1(l, c) + it * 2, c % RING)

            def split2(l, c, it=0):
                split_hi(g2(l, c) + it * 3, round2(l, c) + it, c % RING, width(c, OUT2, FFN + WIN))

            def sum_squares(norm):
                for t in range(T):
                    act.wait_ge(x_done, norm * 4 + (2 * t + 2))
                    nc.scalar.activation(xn[:, t, :], x_tok[:, t, :], ACT.Square,
                                         accum_out=ss[:, t:t + 1]).then_inc(sq_sum, 1)

            def turned_ln(norm):
                for k in range(KD):
                    act.wait_ge(affine_done, (norm - 2 * DEPTH) * KD + (k + 1))
                    nc.scalar.activation(a_hi[:, k, :], affine[k % 4], ACT.Copy).then_inc(aT_hi, 1)

            def normalise0(norm):
                act.wait_ge(tile0_sums, (norm - 2 * DEPTH) * 2)
                nc.scalar.activation(xn[:, 0, :], x_tok[:, 0, :], ACT.Identity, bias=0.0, scale=1.0,
                                     accum_out=shift[:, 2:3]).then_inc(tile0_stat, 1)
                act.wait_ge(mean_ready, norm - 2 * DEPTH)
                nc.scalar.activation(xn[:, 0, :], x_tok[:, 0, :], ACT.Square, bias=shift[:, 1:2],
                                     accum_out=shift[:, 3:4]).then_inc(tile0_stat, 1)
                act.wait_ge(shift_ready, norm - 2 * DEPTH)
                for n in range(2):
                    half = slice(n * 512, (n + 1) * 512)
                    nc.scalar.activation(xn[:, 0, half], x_tok[:, 0, half], ACT.Identity, bias=shift[:, 0:1], scale=rstd[:, 0:1])\
                        .then_inc(xn_ready[0], 1)

            def turned(norm, gain):
                for k in range(KD):
                    if k % 2 == 0:
                        act.wait_ge(xT, turned_value(norm, k // 2))
                    nc.scalar.activation(a_hi[:, k, :], work_flat[:, k * SEQ:(k + 1) * SEQ], ACT.Identity, bias=0.0,
                                         scale=cols[:, ds(gain + k, 1)]).then_inc(aT_hi, 1)

            def evac_proj(l, c):
                act.wait_ge(used, g1(l, c) + 4)
                if c == 0:
                    act.wait_ge(rstd_ready, l + 1)
                for t in range(T):
                    last = nc.scalar.activation(proj[:, t, c * BLK:(c + 1) * BLK], work[:, c % 2, t * BLK:(t + 1) * BLK],
                                                ACT.Identity, bias=0.0, scale=rstd[:, t:t + 1])
                last.then_inc(proj_ready, 1)

            def attend(l, e):
                act.wait_ge(nmax_ready, l * 16 + (e + 1))
                if e >= 2:
                    act.wait_ge(pT_ps, l * 16 + (e - 1))
                for t in range(T):
                    src = work[:, 2 + e % 2, t * SEQ:(t + 1) * SEQ] if e < NHA else masked[:, e % 2, t * SEQ:(t + 1) * SEQ]
                    last = nc.scalar.activation(prob[:, e % 2, t * SEQ:(t + 1) * SEQ], src, ACT.Exp,
                                                bias=nmax[:, HEADS[e], t:t + 1], scale=SCALE if e < NHA else 1.0,
                                                accum_out=rsum[:, HEADS[e], t:t + 1])
                last.then_inc(exp_done, 1)

            def evac_pT(l, e):
                act.wait_ge(pT_ps, l * 16 + (e + 1))
                if e >= 2:
                    act.wait_ge(pv_done, l * 16 + (e - 1))
                nc.scalar.activation(probT[:, e % 2, :], turned_bank(e), ACT.Copy).then_inc(pTB, 1)

            def y_squares(l, half):
                for t in range(T):
                    act.wait_ge(y_ready, l * 4 + (2 * half + t + 1))
                    nc.scalar.activation((sqs, rope_a)[half][:, t, 0:512], y_tok[:, t, half * 512:half * 512 + 512], ACT.Square,
                                         accum_out=ssy[:, 2 * half + t:2 * half + t + 1]).then_inc(y_sq, 1)

            def y_hi(l, k):
                act.wait_ge(yT_ps, l * 2 + (k // 4 + 1))
                nc.scalar.activation(a_hi[:, k, :], acc_flat[:, (4 + k % 4) * SEQ:(5 + k % 4) * SEQ], ACT.Identity, bias=0.0,
                                     scale=cols[:, ds(l * C1 + (2 * KD + k), 1)]).then_inc(yT_hi, 1)

            split1(0, 0)
            act.wait_ge(cols_ready, 4)
            split1(0, 1)
            with act.Fori(0, DEPTH) as l:
                turned(l * 2, l * C1)
                sum_squares(l * 2)
                split1(l, 2)
                for kind, n in PLAN1:
                    if kind == "chunk":
                        evac_proj(l, n)
                    elif kind == "split":
                        split1(l, n)
                    elif kind == "ropeA":
                        act.wait_ge(proj_ready, l * WIN + 3)
                        for t in range(T):
                            nc.scalar.activation(sqs[:, t, :], proj[:, t, 0:QKA], ACT.Square).then_inc(qk_sq, 1)
                    elif kind == "tA":
                        act.wait_ge(qkA_ps, l + 1)
                        nc.scalar.activation(qkTA[:, :, :].rearrange("p a b -> p (a b)"), acc_flat[:, 0:5 * SEQ], ACT.Copy)\
                            .then_inc(qkA_T, 1)
                    elif kind == "tB":
                        act.wait_ge(qkB_ps, l + 1)
                        nc.scalar.activation(qkTB[:, 0:4, :].rearrange("p a b -> p (a b)"), acc_flat[:, 0:1024], ACT.Copy)\
                            .then_inc(qB_T, 1)
                    elif kind == "score":
                        if n >= NHA + 2:
                            evac_pT(l, n - 2)
                        attend(l, n)
                    elif kind == "turn" and n >= NHA + NHB - 2:
                        evac_pT(l, n)
                    elif kind == "yhi":
                        y_hi(l, n)
                split1(l, WIN + RING)
                y_squares(l, 0)
                y_squares(l, 1)
                split1(l, WIN + 1 + RING)
                split1(l, WIN + 2 + RING)
                sum_squares(l * 2 + 1)
                turned(l * 2 + 1, l * C1 + KD)
                split1(l, WIN + 3 + RING)

                def relu_u(l, i, first=False):
                    if not first:
                        act.wait_ge(h1_sq, l * NI1 + i)
                    nc.scalar.activation(relu[:, :], work[:, 0, :], ACT.Relu).then_inc(relu_done, 1)

                def hidden_hi(l, i, slot):
                    act.wait_ge(h1_sq, l * NI1 + i + 1)
                    nc.scalar.activation(h_hi[:, slot, :], hid[:, :], ACT.Copy).then_inc(h1_hi, 1)

                act.wait_ge(used, g1(l, MLP0) + 4)
                relu_u(l, 0, first=True)
                split1(l, MLP0 + 3)
                hidden_hi(l, 0, 0)

                def mlp_round(it):
                    for j in range(3):
                        i, c = it * 3 + (1 + j), MLP0 + 1 + 2 * j
                        act.wait_ge(used, g1(l, c) + it * 6 + 4)
                        relu_u(l, i)
                        split1(l, c + 3, it)
                        hidden_hi(l, i, (1 + j) % 3)
                        split1(l, c + 4, it)

                with act.Fori(0, (NI1 - 1) // 3) as it:
                    mlp_round(it)

            sum_squares(2 * DEPTH)
            act.wait_ge(lam_abs, 1)
            nc.scalar.activation(sp[:, 1, :], sp[:, 0, :], ACT.Exp, scale=-1.0).then_inc(lam_exp, 1)

            def ffn(l, f, cb):
                def silu(i, first=False):
                    if not first:
                        act.wait_ge(h2_f, (l * 2 + f) * NI2 + i)
                    nc.scalar.activation(relu[:, :], work[:, 0, :], ACT.Silu).then_inc(silu_done, 1)

                def hidden_hi(i, slot):
                    act.wait_ge(h2_f, (l * 2 + f) * NI2 + i + 1)
                    nc.scalar.activation(h_hi[:, slot, :], hid[:, :], ACT.Copy).then_inc(h2_hi, 1)

                act.wait_ge(used, g2(l, cb) + 4)
                silu(0, first=True)
                split2(l, cb + 3)
                split2(l, cb + 4)
                hidden_hi(0, 0)

                def body(it, last):
                    i, c = it + 1, cb + 2
                    act.wait_ge(used, g2(l, c) + it * 3 + 4)
                    silu(i)
                    for n in (3, 4, 5):
                        if n == 5:
                            if not last:
                                act.wait_ge(used, g2(l, c) + it * 3 + 6)
                            hidden_hi(i, int(last))
                        split2(l, c + n, it)

                with act.Fori(0, NI2 - 2) as it:
                    body(it, False)
                body(NI2 - 2, True)

            with act.Fori(0, DEPTH) as l:
                norm0 = l * 3 + (2 * DEPTH + 1)
                mx = l * NM + MX0
                turned_ln(norm0 - 1)
                split2(l, 2)
                ffn(l, 0, 0)
                normalise0(norm0)
                turned_ln(norm0)
                split2(l, FFN + 2)
                for j in range(WIN):
                    c = FFN + j
                    act.wait_ge(used, g2(l, c) + 4)
                    bank = work[:, j % 2, :]
                    if j < 2:
                        act.wait_ge(conv_pads, 2)
                        nc.scalar.activation(xrp[:, 2 * j:2 * j + 2, CONV_C - 1:], bank.rearrange("p (c s) -> p c s", c=2),
                                             ACT.Copy).then_inc(z_done, 1)
                        act.wait_ge(z_done, l * 8 + (j + 1))
                        for i in (2 * j, 2 * j + 1):
                            nc.scalar.activation(xr[:, i * SEQ:(i + 1) * SEQ], xrp[:, i, 0:SEQ], ACT.Identity,
                                                 bias=cols[:, ds(mx + (M_CB + i), 1)], scale=cols[:, ds(mx + (M_CONV + i), 1)])\
                                .then_inc(tap0_done, 1)
                    elif j < 4:
                        nc.scalar.activation((ug, vg)[j - 2], bank, ACT.Gelu_apprx_tanh).then_inc(z_done, 1)
                    elif j < 6:
                        nc.scalar.activation(gg[:, (j - 4) * 512:(j - 3) * 512], bank, ACT.Gelu_apprx_tanh).then_inc(z_done, 1)
                    elif j < 8:
                        nc.scalar.activation((bg, cgt)[j - 6], bank, ACT.Copy).then_inc(z_done, 1)
                    split2(l, c + RING)
                    if j == 2:
                        for n in range(2):
                            act.wait_ge(gate_ps, l * 2 + (n + 1))
                            src = (work_flat[:, 1024:2048], acc_flat[:, 0:1024])[n]
                            for i in range(CT):
                                nc.scalar.activation((r_gate, i_gate)[n][:, i * SEQ:(i + 1) * SEQ], src[:, i * SEQ:(i + 1) * SEQ],
                                                     ACT.Sigmoid, bias=cols[:, ds(mx + ((M_BA, M_BI)[n] + i), 1)])\
                                    .then_inc(sig_done, 1)
                        act.wait_ge(sig_done, l * 2 * CT + CT)
                        act.wait_ge(sp_ready, 1)
                        for i in range(CT):
                            nc.scalar.activation(th[:, i * SEQ:(i + 1) * SEQ], r_gate[:, i * SEQ:(i + 1) * SEQ], ACT.Tanh,
                                                 scale=sp[:, 3, ds(l * CT + i, 1)]).then_inc(th_done, 1)
                    if j == 4:
                        act.wait_ge(th_pos, l + 1)
                        nc.scalar.activation(root, th, ACT.Sqrt, scale=4.0).then_inc(root_done, 1)
                    if j == 6:
                        act.wait_ge(yaT_ps, l + 1)
                        for k in range(2):
                            nc.scalar.activation(mixed(k)[0], acc_flat[:, 1536 + k * SEQ:1536 + (k + 1) * SEQ], ACT.Copy)\
                                .then_inc(y2_hi, 1)
                    if j == 7:
                        act.wait_ge(y2_f, l * 2 + 1)
                        nc.scalar.activation(mixed(2, 4)[0], r_gate, ACT.Copy).then_inc(y2_hi, 1)
                act.wait_ge(y2_f, l * 2 + 2)
                nc.scalar.activation(mixed(6, 2)[0], yb, ACT.Copy).then_inc(y2_hi, 1)
                for j in range(len(OUT2) - 1):
                    split2(l, FFN + WIN + j + RING)
                normalise0(norm0 + 1)
                turned_ln(norm0 + 1)
                split2(l, FFN + WIN + len(OUT2) + 2)
                ffn(l, 1, FFN + WIN + len(OUT2))
                normalise0(norm0 + 2)

        @block.vector
        def _(dve):
            order = {"n": 0, "base": 0}

            def step(ins_):
                order["n"] += 1
                ins_.then_inc(dve_order, 1)
                return order["n"]

            def after(n):
                dve.wait_ge(dve_order, order["base"] + n)

            def link(ins_):
                after(step(ins_))

            def width(c, outs, at):
                return outs[c - at] * D if at <= c < at + len(outs) else CW

            def split_lo(g, slot, w=CW):
                dve.wait_ge(hi_done, g + 1)
                nc.vector.tensor_tensor(w_lo[:, slot, 0:w], raw[:, slot, 0:w], w_hi[:, slot, 0:w].bitcast(f32), ALU.subtract)\
                    .then_inc(lo_done, 1)

            def split1(l, c, it=0):
                split_lo(g1(l, c) + it * 6, c % RING)

            def split2(l, c, it=0):
                split_lo(g2(l, c) + it * 3, c % RING, width(c, OUT2, FFN + WIN))

            def rsqrt(dst, src, n, scale, eps):
                v, y, h, b = (nwt[:, r, 0:n] for r in range(4))
                link(nc.vector.tensor_scalar(v, src, scale, eps, ALU.mult, ALU.add))
                nc.vector.tensor_scalar(y.bitcast(i32), v.bitcast(i32), -0.5, float(0x5f3759df), ALU.mult, ALU.add)
                link(nc.vector.tensor_scalar(h, v, -0.5, None, ALU.mult))
                for turn in range(3):
                    link(nc.vector.tensor_tensor(b, y, y, ALU.mult))
                    link(nc.vector.tensor_tensor(b, b, h, ALU.mult))
                    last = nc.vector.scalar_tensor_tensor(dst if turn == 2 else y, b, 1.5, y, ALU.add, ALU.mult)
                    if turn < 2:
                        link(last)
                return last

            def turned(norm, gain):
                for k in range(KD):
                    dve.wait_ge(aT_hi, norm * KD + (k // 2 * 2 + 2))
                    nc.vector.scalar_tensor_tensor(a_lo[:, k, :], work_flat[:, k * SEQ:(k + 1) * SEQ], cols[:, ds(gain + k, 1)],
                                                   a_hi[:, k, :].bitcast(f32), ALU.mult, ALU.subtract).then_inc(aT_lo, 1)

            def turned_ln(norm, gain, bias):
                for k in range(KD):
                    if k % 2 == 0:
                        dve.wait_ge(xT, turned_value(norm, k // 2))
                    if k >= 4:
                        dve.wait_ge(aT_lo, norm * KD + (k - 3))
                    nc.vector.tensor_scalar(affine[k % 4], work_flat[:, k * SEQ:(k + 1) * SEQ], cols[:, ds(gain + k, 1)],
                                            cols[:, ds(bias + k, 1)], ALU.mult, ALU.add).then_inc(affine_done, 1)

            def quarter_ready(norm, g, q):
                if q < 3:
                    dve.wait_ge(sums, (norm - 1) * 3 + (q + 1))
                else:
                    dve.wait_ge(used, g + 4)

            def residual(norm, g, factor):
                for q in range(4):
                    t, n = q // 2, q % 2
                    x = x_tok[:, t, n * 512:(n + 1) * 512]
                    quarter_ready(norm, g, q)
                    nc.vector.scalar_tensor_tensor(x, acc[:, q, :], factor[:, t:t + 1], x, ALU.mult, ALU.add).then_inc(x_done, 1)

            def layer_norm(norm, g, factor):
                latest = [0, 0]

                def newton(t, i):
                    v, y, h, b = (nwt[:, r, t:t + 1] for r in range(4))
                    if i > 0:
                        after(latest[t])
                    if i == 0 and t == 0:
                        dve.wait_ge(tile0_stat, (norm - 2 * DEPTH) * 2)
                        ins_ = nc.vector.tensor_scalar(v, shift[:, 3:4], 1.0 / D, LN_EPS, ALU.mult, ALU.add)
                    elif i == 0:
                        after(latest[t])
                        ins_ = nc.vector.tensor_scalar(v, mv[:, t, 1:2], 1.0, LN_EPS, ALU.mult, ALU.add)
                    elif i == 1:
                        nc.vector.tensor_scalar(y.bitcast(i32), v.bitcast(i32), -0.5, float(0x5f3759df), ALU.mult, ALU.add)
                        ins_ = nc.vector.tensor_scalar(h, v, -0.5, None, ALU.mult)
                    elif i % 2 == 0:
                        ins_ = nc.vector.tensor_scalar(b, y, y, h, ALU.mult, ALU.mult)
                    else:
                        ins_ = nc.vector.scalar_tensor_tensor(rstd[:, t:t + 1] if i == 7 else y, b, 1.5, y, ALU.add, ALU.mult)
                    latest[t] = step(ins_)

                for q in range(4):
                    t, n = q // 2, q % 2
                    x = x_tok[:, t, n * 512:(n + 1) * 512]
                    quarter_ready(norm, g, q)
                    if n == 0:
                        dve.wait_ge(x_scaled, (norm - 2 * DEPTH - 1) * T + (t + 1))
                    ins_ = nc.vector.scalar_tensor_tensor(x, acc[:, q, :], factor, x, ALU.mult, ALU.add)
                    if t == 0:
                        ins_.then_inc(tile0_sums, 1)
                        continue
                    summed = step(ins_)
                    if n == 0:
                        dve.wait_ge(tile0_stat, (norm - 2 * DEPTH) * 2 - 1)
                        nc.vector.tensor_scalar(shift[:, 1:2], shift[:, 2:3], -1.0 / D, None, ALU.mult).then_inc(mean_ready, 1)
                    after(summed)
                    stats = step(nc.vector.bn_stats(stat[:, t, n, :], x))
                newton(0, 0)
                after(stats)
                dve.sem_inc(passed_dve, 1)
                latest[1] = step(nc.vector.bn_aggr(mv[:, 1, :], stat[:, 1, :, :].rearrange("p a b -> p (a b)")))
                for i in range(8):
                    if i < 7:
                        newton(0, i + 1)
                    else:
                        after(latest[0])
                        dve.wait_ge(mean_ready, norm - 2 * DEPTH)
                        nc.vector.tensor_scalar(shift[:, 0:1], shift[:, 1:2], rstd[:, 0:1], None, ALU.mult)\
                            .then_inc(shift_ready, 1)
                    newton(1, i)
                after(latest[1])
                for n in range(2):
                    half = slice(n * 512, (n + 1) * 512)
                    nc.vector.tensor_scalar(xn[:, 1, half], x_tok[:, 1, half], mv[:, 1, 0:1], rstd[:, 1:2],
                                            ALU.subtract, ALU.mult).then_inc(xn_ready[1], 1)

            dve.sem_inc(lo_done, RING)
            nc.vector.memset(cols[:, DEPTH * C1:LN0], 0.0).then_inc(cols_ready, 1)
            dve.wait_ge(rowsT, 3)
            tabs = acc[:, 0, :]
            nc.vector.tensor_copy(cols[:, 0:DEPTH * C1], tabs[:, 0:DEPTH * C1]).then_inc(cols_ready, 1)
            nc.vector.tensor_copy(cols[:, LN0:NCOL], tabs[:, DEPTH * C1:DEPTH * C1 + NCOL - LN0]).then_inc(cols_ready, 1)
            dve.wait_ge(cols_ready, 3)
            at = DEPTH * C1 + NCOL - LN0
            nc.vector.tensor_copy(cols[:, LAST_LN:LAST_LN + KD], tabs[:, at:at + KD]).then_inc(cols_ready, 1)
            lam = cols[:, MX0:MX0 + DEPTH * NM].rearrange("p (l m) -> p l m", m=NM)[:, :, M_LAM:M_LAM + CT]
            sv = [sp[:, n, :].rearrange("p (l m) -> p l m", m=CT) for n in range(4)]
            dve.wait_ge(x_loaded, 16 * T)
            dve.sem_inc(x_done, 4)
            split1(0, 0)

            def rope_global(l):
                for t in range(T):
                    dve.wait_ge(qk_sq, l * T + (t + 1))
                    link(nc.vector.tensor_reduce(ssA[:, t * 10:(t + 1) * 10], sqs[:, t, :].rearrange("p (h d) -> p h d", d=HD),
                                                 AX.X, ALU.add))
                link(rsqrt(rstdA[:, :], ssA[:, :], 20, 1.0 / HD, RMS_EPS))
                dve.wait_ge(rope_tab, l * 20 + 20)
                for t in range(T):
                    m = rope_b[:, t, :].rearrange("p (h d) -> p h d", d=HD)
                    link(nc.vector.tensor_tensor(m, proj[:, t, 0:QKA].rearrange("p (h d) -> p h d", d=HD),
                                                 rstdA[:, t * 10:(t + 1) * 10].unsqueeze(2).broadcast_to((P, NHA + NKV, HD)), ALU.mult))
                    nc.vector.tensor_tensor(rope_a[:, t, :], rope_b[:, t, :], cg[:, t, :], ALU.mult)
                    halves = [x[:, t, :].rearrange("p (a b c) -> p a b c", b=2, c=16) for x in (rope_b, sg, sqs)]
                    for b in range(2):
                        link(nc.vector.tensor_tensor(halves[2][:, :, b, :], halves[0][:, :, 1 - b, :], halves[1][:, :, b, :], ALU.mult))
                    for g in range(NKV):
                        q = slice(g * GROUP * HD, (g + 1) * GROUP * HD)
                        nc.vector.tensor_tensor(
                            qkA[:, t, 0:NHA * HD].rearrange("p (i g d) -> p g i d", g=NKV, d=HD)[:, g, :, :],
                            rope_a[:, t, q].rearrange("p (i d) -> p i d", d=HD),
                            sqs[:, t, q].rearrange("p (i d) -> p i d", d=HD), ALU.add)
                    nc.vector.tensor_tensor(qkA[:, t, NHA * HD:], rope_a[:, t, NHA * HD:], sqs[:, t, NHA * HD:], ALU.add)\
                        .then_inc(ropeA_done, 1)

            def rope_dilated(l):
                dve.wait_ge(tab_loaded, 48)
                dve.wait_ge(qkA_ps, l + 1)
                dve.wait_ge(proj_ready, l * WIN + 7)
                for t in range(T):
                    x = proj[:, t, QB0:VB0].rearrange("p (h d) -> p h d", d=HD)
                    a = rope_a[:, t, 0:256].rearrange("p (h d) -> p h d", d=16)
                    b = rope_b[:, t, 0:256].rearrange("p (h d) -> p h d", d=16)
                    nc.vector.tensor_tensor(a, x[:, :, 0:16], rope_pt[:, t, 0:16].unsqueeze(1).broadcast_to((P, 2 * NHB, 16)), ALU.mult)
                    for n in range(2):
                        link(nc.vector.tensor_tensor(b[:, :, 8 * n:8 * n + 8], x[:, :, 8 - 8 * n:16 - 8 * n],
                                                     rope_pt[:, t, 16 + 8 * n:24 + 8 * n].unsqueeze(1).broadcast_to((P, 2 * NHB, 8)),
                                                     ALU.mult))
                    nc.vector.tensor_tensor(x[:, :, 0:16], a, b, ALU.add).then_inc(ropeB_done, 1)

            def row_max(l, e):
                dve.wait_ge(s_ready, l * 16 + (e + 1))
                h = HEADS[e]
                scores = work[:, 2 + e % 2, :]
                if e < NHA:
                    link(nc.vector.tensor_reduce(rinv[:, h, :], scores.rearrange("p (t s) -> p t s", t=T), AX.X, ALU.max))
                    nc.vector.tensor_scalar(nmax[:, h, :], rinv[:, h, :], -SCALE, None, ALU.mult).then_inc(nmax_ready, 1)
                else:
                    dve.wait_ge(exp_done, l * 16 + (e - 1))
                    link(nc.vector.scalar_tensor_tensor(masked[:, e % 2, :], scores, SCALE, logc_flat, ALU.mult, ALU.add))
                    nc.vector.tensor_reduce(nmax[:, h, :], masked[:, e % 2, :].rearrange("p (t s) -> p t s", t=T),
                                            AX.X, ALU.max, negate=True).then_inc(nmax_ready, 1)

            logc_flat = logc[:, :, :].rearrange("p t s -> p (t s)")

            def evac_pT(l, e):
                dve.wait_ge(pT_ps, l * 16 + (e + 1))
                if e >= 2:
                    dve.wait_ge(pv_done, l * 16 + (e - 1))
                nc.vector.tensor_copy(probT[:, e % 2, :], turned_bank(e)).then_inc(pTA, 1)

            def y_scale(l, n):
                half, t = n // 2, n % 2
                hs_ = slice(8 * half, 8 * half + 8)
                if t == 0:
                    dve.wait_ge(pv_done, l * 16 + (8 * half + 8))
                    link(nc.vector.reciprocal(rinv[:, hs_, :], rsum[:, hs_, :]))
                y = y_tok[:, t, half * 512:half * 512 + 512].rearrange("p (h d) -> p h d", d=HD)
                o = acc[:, (2, 0)[half] + t, :].rearrange("p (h d) -> p h d", d=HD)
                nc.vector.tensor_tensor(y, o, rinv[:, hs_, t].unsqueeze(2).broadcast_to((P, 8, HD)), ALU.mult).then_inc(y_ready, 1)

            def y_lo(l, k):
                dve.wait_ge(yT_hi, l * 8 + (k // 2 * 2 + 2))
                nc.vector.scalar_tensor_tensor(a_lo[:, k, :], acc_flat[:, (4 + k % 4) * SEQ:(5 + k % 4) * SEQ],
                                               cols[:, ds(l * C1 + (2 * KD + k), 1)],
                                               a_hi[:, k, :].bitcast(f32), ALU.mult, ALU.subtract).then_inc(yT_lo, 1)

            with dve.Fori(0, DEPTH) as l:
                order["n"], order["base"] = 0, l * ORD1
                turned(l * 2, l * C1)
                split1(l, 1)
                dve.wait_ge(sq_sum, l * 2 * T + T)
                rsqrt(rstd[:, :], ss[:, 0:T], T, 1.0 / D, RMS_EPS).then_inc(rstd_ready, 1)
                split1(l, 2)
                for kind, n in PLAN1:
                    if kind == "split" and n not in POOL1:
                        split1(l, n)
                    elif kind == "ropeA":
                        rope_global(l)
                    elif kind == "ropeB":
                        rope_dilated(l)
                    elif kind == "tB":
                        dve.wait_ge(qkB_ps, l + 1)
                        nc.vector.tensor_copy(qkTB[:, 4:8, :].rearrange("p a b -> p (a b)"), acc_flat[:, 1024:2048]).then_inc(kB_T, 1)
                    elif kind == "score":
                        row_max(l, n)
                    elif kind == "turn" and n < NHA:
                        evac_pT(l, n)
                    elif kind == "yscale":
                        y_scale(l, n)
                    elif kind == "ylo":
                        y_lo(l, n)
                dve.wait_ge(lo_done, g1(l, WIN + RING) + 3)
                split1(l, WIN + RING)
                dve.wait_ge(y_sq, l * 4 + 4)
                link(rsqrt(rstdy[:, :], ssy[:, :], 4, 1.0 / 512, RMS_EPS))
                split1(l, WIN + 1 + RING)
                dve.wait_ge(used, g1(l, WIN + 1) + 4)
                for t in range(T):
                    for n in range(2):
                        x = x_tok[:, t, n * 512:(n + 1) * 512]
                        link(nc.vector.scalar_tensor_tensor(x, work[:, 2 * t + n, :], rstdy[:, t:t + 1], x, ALU.mult, ALU.add))
                residual(l * 2 + 1, g1(l, MLP0 - 1), rstdy[:, T:])
                turned(l * 2 + 1, l * C1 + KD)
                split1(l, WIN + 2 + RING)
                dve.wait_ge(sq_sum, (l * 2 + 2) * T)
                link(nc.vector.tensor_scalar(rms2[:, 0, :], ss[:, 0:T], 1.0 / D, RMS_EPS, ALU.mult, ALU.add))
                link(nc.vector.reciprocal(rms2[:, 1, :], rms2[:, 0, :]))
                split1(l, WIN + 3 + RING)

                def square(l, i, first=False):
                    dve.wait_ge(relu_done, l * NI1 + i + 1)
                    if not first:
                        dve.wait_ge(h1_lo, l * NI1 + i)
                    nc.vector.tensor_tensor(hid[:, :], relu[:, :], relu[:, :], ALU.mult).then_inc(h1_sq, 1)

                def hidden_lo(l, i, slot):
                    dve.wait_ge(h1_hi, l * NI1 + i + 1)
                    nc.vector.tensor_tensor(h_lo[:, slot, :], hid[:, :], h_hi[:, slot, :].bitcast(f32), ALU.subtract).then_inc(h1_lo, 1)

                square(l, 0, first=True)
                split1(l, MLP0 + 3)
                hidden_lo(l, 0, 0)

                def mlp_round(it, last=False):
                    for j in range(3):
                        i, c = it * 3 + (1 + j), MLP0 + 1 + 2 * j
                        square(l, i)
                        split1(l, c + 3, it)
                        hidden_lo(l, i, (1 + j) % 3)
                        if not (last and j == 2):
                            split1(l, c + 4, it)

                with dve.Fori(0, (NI1 - 1) // 3 - 1) as it:
                    mlp_round(it)
                mlp_round((NI1 - 1) // 3 - 1, last=True)
                residual(l * 2 + 2, g1(l, CH1 - 1), rms2[:, 1, :])
                assert order["n"] == ORD1, order["n"]

            order["n"], order["base"] = 0, DEPTH * ORD1
            nc.vector.memset(xrp, 0.0).then_inc(conv_pads, 1)
            nc.vector.memset(cxp, 0.0).then_inc(conv_pads, 1)
            dve.wait_ge(sq_sum, (2 * DEPTH + 1) * T)
            link(rsqrt(rstd[:, :], ss[:, 0:T], T, 1.0 / D, RMS_EPS))
            for t in range(T):
                for n in range(2):
                    half = slice(n * 512, (n + 1) * 512)
                    nc.vector.tensor_scalar(xn[:, t, half], x_tok[:, t, half], rstd[:, t:t + 1], None, ALU.mult)\
                        .then_inc(xn_ready[t], 1)
            nc.vector.scalar_tensor_tensor(sv[0], lam, -1.0, lam, ALU.mult, ALU.max).then_inc(lam_abs, 1)
            dve.wait_ge(lam_exp, 1)
            link(nc.vector.tensor_scalar(sp[:, 0, :], sp[:, 1, :], 2.0, None, ALU.add))
            link(nc.vector.reciprocal(sp[:, 2, :], sp[:, 0, :]))
            link(nc.vector.tensor_tensor(sp[:, 1, :], sp[:, 1, :], sp[:, 2, :], ALU.mult))
            link(nc.vector.tensor_tensor(sp[:, 0, :], sp[:, 1, :], sp[:, 1, :], ALU.mult))
            link(nc.vector.tensor_scalar(sp[:, 2, :], sp[:, 0, :], 1.0 / 17, None, ALU.mult))
            for odd in (15, 13, 11, 9, 7, 5, 3):
                link(nc.vector.scalar_tensor_tensor(sp[:, 2, :], sp[:, 2, :], 1.0 / odd, sp[:, 0, :], ALU.add, ALU.mult))
            link(nc.vector.scalar_tensor_tensor(sp[:, 2, :], sp[:, 2, :], 1.0, sp[:, 1, :], ALU.add, ALU.mult))
            link(nc.vector.tensor_scalar(sp[:, 2, :], sp[:, 2, :], RG_C, None, ALU.mult))
            link(nc.vector.tensor_scalar(sv[0], lam, -RG_C / 2, 0.0, ALU.mult, ALU.max))
            nc.vector.tensor_tensor(sp[:, 3, :], sp[:, 0, :], sp[:, 2, :], ALU.add).then_inc(sp_ready, 1)
            before2 = DEPTH * ORD1 + order["n"]

            def ffn(l, f, cb):
                def hidden(i, first=False):
                    dve.wait_ge(silu_done, (l * 2 + f) * NI2 + i + 1)
                    if not first:
                        dve.wait_ge(h2_lo, (l * 2 + f) * NI2 + i)
                    nc.vector.tensor_tensor(hid[:, :], relu[:, :], work[:, 1, :], ALU.mult).then_inc(h2_f, 1)

                def hidden_lo(i, slot):
                    dve.wait_ge(h2_hi, (l * 2 + f) * NI2 + i + 1)
                    nc.vector.tensor_tensor(h_lo[:, slot, :], hid[:, :], h_hi[:, slot, :].bitcast(f32), ALU.subtract).then_inc(h2_lo, 1)

                split2(l, cb + 3)
                dve.wait_ge(used, g2(l, cb + 1) + 4)
                hidden(0, first=True)
                split2(l, cb + 4)
                hidden_lo(0, 0)

                def body(it, last):
                    i, c = it + 1, cb + 2
                    for n in (3, 4, 5):
                        if n == 4:
                            dve.wait_ge(used, g2(l, c) + it * 3 + 5)
                            hidden(i)
                        if n == 5:
                            hidden_lo(i, int(last))
                        if not last or n < 5:
                            split2(l, c + n, it)

                with dve.Fori(0, NI2 - 2) as it:
                    body(it, False)
                body(NI2 - 2, True)

            with dve.Fori(0, DEPTH) as l:
                order["n"], order["base"] = 0, l * ORD2 + before2
                norm0 = l * 3 + (2 * DEPTH + 1)
                gains = l * N2 + LN0
                mx = l * NM + MX0
                turned_ln(norm0 - 1, l * N2 + LAST_LN, l * N2 + (LAST_LN + 3 * KD))
                split2(l, 1)
                split2(l, 2)
                ffn(l, 0, 0)
                layer_norm(norm0, g2(l, FFN - 1), 0.5)
                turned_ln(norm0, gains, gains + 3 * KD)
                split2(l, FFN + 1)
                split2(l, FFN + 2)

                def causal_conv(j):
                    dve.wait_ge(tap0_done, l * CT + (2 * j + 2))
                    for tap in range(1, CONV_C):
                        for i in (2 * j, 2 * j + 1):
                            dst = xr[:, i * SEQ:(i + 1) * SEQ]
                            ins_ = nc.vector.scalar_tensor_tensor(dst, xrp[:, i, tap:tap + SEQ], cols[:, ds(mx + (M_CONV + tap * CT + i), 1)],
                                                                  dst, ALU.mult, ALU.add)
                            if tap == CONV_C - 1:
                                ins_.then_inc(conv_done, 1)
                            elif i % 2 == 0:
                                step(ins_)
                            else:
                                link(ins_)

                causal_conv(0)
                split2(l, FFN + 3)
                causal_conv(1)
                split2(l, FFN + 4)
                dve.wait_ge(sgu_ps, l + 1)
                nc.vector.tensor_copy(sguT[:, :, :].rearrange("p a b -> p (a b)"), acc[:, 2, :]).then_inc(sgu_T, 1)
                dve.wait_ge(th_done, l * CT + CT)
                nc.vector.tensor_scalar(th, th, 0.0, None, ALU.max).then_inc(th_pos, 1)
                dve.wait_ge(z_done, l * 8 + 4)
                for t in range(T):
                    v = vg[:, t * 256:(t + 1) * 256]
                    link(nc.vector.bn_stats(stat[:, t, 0, :], v))
                    dve.sem_inc(passed_dve, 1)
                    link(nc.vector.bn_aggr(mv[:, t, :], stat[:, t, 0, :]))
                link(rsqrt(rstd[:, :], mv[:, :, 1], T, 1.0, LN_EPS))
                dve.wait_ge(mix_w, l * 48 + 48)
                v, w = [[x[:, t * 256:(t + 1) * 256] for t in range(T)] for x in (vg, vn)]
                for t in range(T):
                    last = step(nc.vector.tensor_scalar(w[t], v[t], mv[:, t, 0:1], rstd[:, t:t + 1], ALU.subtract, ALU.mult))
                after(last)
                for t in range(T):
                    last = step(nc.vector.tensor_tensor(w[t], w[t], sgu_gb[:, 0, :], ALU.mult))
                after(last)
                for t in range(T):
                    nc.vector.tensor_tensor(w[t], w[t], sgu_gb[:, 1, :], ALU.add).then_inc(v_done, 1)
                dve.wait_ge(th_pos, l + 1)
                link(nc.vector.tensor_scalar(q_rec, th, 1.0, None, ALU.add))
                link(nc.vector.reciprocal(q_rec, q_rec))
                dve.wait_ge(mix_ps, l + 1)
                for h in range(AH):
                    dst, src, u = (x.rearrange("p (t c) -> p t c", t=T)[:, :, h * HD:(h + 1) * HD]
                                   for x in (ya, acc[:, 2, :], ug))
                    nc.vector.scalar_tensor_tensor(dst, src, cols[:, ds(mx + (M_SGB + h), 1)], u, ALU.add, ALU.mult)\
                        .then_inc(ya_done, 1)
                nc.vector.tensor_scalar(a_dec, q_rec, 2.0, -1.0, ALU.mult, ALU.add)
                dve.wait_ge(sig_done, l * 2 * CT + 2 * CT)
                nc.vector.tensor_tensor(i_gate, i_gate, xr, ALU.mult)
                dve.wait_ge(root_done, l + 1)
                link(nc.vector.tensor_tensor(q_rec, q_rec, root, ALU.mult))
                link(nc.vector.tensor_tensor(q_rec, q_rec, i_gate, ALU.mult))
                for i in range(CT):
                    span = slice(i * SEQ, (i + 1) * SEQ)
                    last = nc.vector.tensor_tensor_scan(hs[:, span], a_dec[:, span], q_rec[:, span], 0.0, ALU.mult, ALU.add)
                link(last)
                dve.wait_ge(z_done, l * 8 + 6)
                nc.vector.tensor_tensor(r_gate, gg, hs, ALU.mult).then_inc(y2_f, 1)
                dve.wait_ge(lo_done, g2(l, FFN + WIN) + 3)
                split2(l, FFN + WIN)
                for k in range(2):
                    dve.wait_ge(y2_hi, l * 4 + 2)
                    nc.vector.tensor_tensor(mixed(k)[1], acc_flat[:, 1536 + k * SEQ:1536 + (k + 1) * SEQ],
                                            mixed(k)[0].bitcast(f32), ALU.subtract).then_inc(y2_lo, 1)
                split2(l, FFN + WIN + 1)
                dve.wait_ge(y2_hi, l * 4 + 3)
                dve.wait_ge(y2_f, l * 2 + 1)
                nc.vector.tensor_tensor(mixed(2, 4)[1], r_gate, mixed(2, 4)[0].bitcast(f32), ALU.subtract).then_inc(y2_lo, 1)
                dve.wait_ge(used, g2(l, FFN + 8) + 4)
                dve.wait_ge(z_done, l * 8 + 8)
                nc.vector.tensor_tensor(cxp[:, :, CONV_B - 1:], cgt.rearrange("p (c s) -> p c s", c=2),
                                        work[:, 0, :].rearrange("p (c s) -> p c s", c=2), ALU.mult).then_inc(cx_done, 1)
                split2(l, FFN + WIN + 2)
                dve.wait_ge(cx_done, l + 1)
                for tap in range(CONV_B):
                    for i in range(2):
                        src, w = cxp[:, i, tap:tap + SEQ], cols[:, ds(mx + (M_SC + tap * 2 + i), 1)]
                        dst = yb[:, i * SEQ:(i + 1) * SEQ]
                        if tap == 0:
                            ins_ = nc.vector.tensor_scalar(dst, src, w, None, ALU.mult)
                        else:
                            ins_ = nc.vector.scalar_tensor_tensor(dst, src, w, dst, ALU.mult, ALU.add)
                        last = step(ins_)
                    after(last)
                nc.vector.tensor_tensor(yb, yb, bg, ALU.mult).then_inc(y2_f, 1)
                split2(l, FFN + WIN + RING)
                dve.wait_ge(y2_hi, l * 4 + 4)
                dve.wait_ge(y2_f, l * 2 + 2)
                nc.vector.tensor_tensor(mixed(6, 2)[1], yb, mixed(6, 2)[0].bitcast(f32), ALU.subtract).then_inc(y2_lo, 1)
                for j in range(1, len(OUT2) - 2):
                    split2(l, FFN + WIN + j + RING)
                layer_norm(norm0 + 1, g2(l, FFN + WIN + len(OUT2) - 1), 1.0)
                turned_ln(norm0 + 1, gains + KD, gains + 4 * KD)
                for c in (1, 2):
                    split2(l, FFN + WIN + len(OUT2) + c)
                ffn(l, 1, FFN + WIN + len(OUT2))
                layer_norm(norm0 + 2, g2(l, CH2 - 1), 0.5)
                assert order["n"] == ORD2, order["n"]
            order["n"], order["base"] = 0, DEPTH * ORD2 + before2
            dve.wait_ge(gb_loaded, DEPTH * 96 + 16)
            dve.wait_ge(xn_ready[1], (3 * DEPTH + 1) * 2)
            link(nc.vector.tensor_tensor(xn[:, 1, :], xn[:, 1, :], g_bc[:, :], ALU.mult))
            nc.vector.tensor_tensor(xn[:, 1, :], xn[:, 1, :], b_bc[:, :], ALU.add).then_inc(tile1_out, 1)

        @block.tensor
        def _(pe):
            def chunk_ready(g):
                pe.wait_ge(lo_done, g + 4)

            def weights(slot, k, at, n):
                return [w[:, slot, k + at:k + at + n] for w in (w_hi, w_lo)]

            def product(dst, left, right, start, stop=False):
                (lh, ll), (rh, rl) = left, right
                nc.tensor.matmul(dst, lh, rh, start=start, stop=False, skip_group_check=True)
                nc.tensor.matmul(dst, lh, rl, start=False, stop=False, skip_group_check=True)
                return nc.tensor.matmul(dst, ll, rh, start=False, stop=stop, skip_group_check=True)

            def turn_norm(src, ready):
                for half in range(2):
                    for t in range(T):
                        pe.wait_ge(*ready(t, half))
                        for k in range(4 * half, 4 * half + 4):
                            at = k * SEQ + t * P
                            last = nc.tensor.transpose(work_flat[:, at:at + P], src[:, t, k * P:(k + 1) * P], ident[:, :])
                            if k % 2 == 1:
                                last.then_inc(xT, 1)

            def keep_clock():
                for _ in range(WARM):
                    nc.tensor.matmul(work[:, 3, :], zero[:, 0:P], zero[:, :], start=True, stop=True)

            def by_tokens(g, slot, bank, norm=None):
                chunk_ready(g)
                for k in range(KD):
                    if norm is not None and k % 2 == 0:
                        pe.wait_ge(aT_lo, norm * KD + (k + 2))
                    for t in range(T):
                        tok = slice(t * P, (t + 1) * P)
                        last = product(work[:, bank, t * BLK:(t + 1) * BLK], (a_hi[:, k, tok], a_lo[:, k, tok]),
                                       weights(slot, k * BLK, 0, BLK), start=(k == 0 and t == 0), stop=(k == KD - 1))
                last.then_inc(used, 1)

            def by_features(g, slot, bank, norm=None, layer_norm=False):
                chunk_ready(g)
                for k in range(KD):
                    if norm is not None:
                        if k % 2 == 0 and not layer_norm:
                            pe.wait_ge(aT_lo, norm * KD + (k + 2))
                        elif layer_norm:
                            if k % 2 == 0:
                                pe.wait_ge(affine_done, (norm - 2 * DEPTH) * KD + (k + 2))
                            pe.wait_ge(aT_lo, norm * KD + (k + 1))
                    for m in range(2):
                        last = product(work[:, bank, m * SEQ:(m + 1) * SEQ], weights(slot, k * BLK, m * P, P),
                                       (a_hi[:, k, :], a_lo[:, k, :]), start=(k == 0 and m == 0), stop=(k == KD - 1))
                last.then_inc(used, 1)

            def down(g, slot, left, nk, dst=acc, start=False, stop=False, quarters=False):
                chunk_ready(g)

                def part_of(k, t, n):
                    hi, lo = left(k)
                    tok = slice(t * P, (t + 1) * P)
                    return product(dst[:, 2 * t + n, :], (hi[:, tok], lo[:, tok]), weights(slot, k * D, n * 512, 512),
                                   start=start and k == 0, stop=stop and k == nk - 1)

                if quarters:
                    for t in range(T):
                        for n in range(2):
                            for k in range(nk):
                                last = part_of(k, t, n)
                            last.then_inc(used if t == T - 1 and n == 1 else sums, 1)
                else:
                    for k in range(nk):
                        for t in range(T):
                            for n in range(2):
                                last = part_of(k, t, n)
                    last.then_inc(used, 1)

            def open_sums():
                for b in range(4):
                    nc.tensor.matmul(acc[:, b, 0:2], zero[:, 0:P], zero[:, 0:2], start=True, stop=False, skip_group_check=True)

            pe.sem_inc(used, RING)
            def score(l, e):
                if e >= 2:
                    pe.wait_ge(exp_done, l * 16 + (e - 1))
                h = HEADS[e]
                if e < NHA:
                    g, i, qT, kT = h // GROUP, h % GROUP, qkTA, 4
                    if e == 0:
                        pe.wait_ge(qkA_T, l + 1)
                else:
                    g, i, qT = h % 2, (h - NHA) // 2, qkTB
                    kT = 4 + i
                    if e == NHA:
                        pe.wait_ge(qB_T, l + 1)
                        pe.wait_ge(kB_T, l + 1)
                rows_ = slice(HD * g, HD * g + HD)
                for t in range(T):
                    last = nc.tensor.matmul(work[:, 2 + e % 2, t * SEQ:(t + 1) * SEQ], qT[rows_, i, t * P:(t + 1) * P],
                                            qT[rows_, kT, :], start=True, stop=True)
                last.then_inc(s_ready, 1)

            def turn(l, e):
                pe.wait_ge(exp_done, l * 16 + (e + 1))
                bank = turned_bank(e)
                if e < 2:
                    pe.wait_ge(qB_T, l + 1)
                    pe.wait_ge(kB_T, l + 1)
                elif e < 4:
                    pe.wait_ge(proj_ready, l * WIN + WIN)
                elif e < NHA + 2:
                    pe.wait_ge(pTA, l * 8 + (e - 1))
                else:
                    pe.wait_ge(pTB, l * 8 + (e - NHA - 1))
                for kt in range(T):
                    for t in range(T):
                        last = nc.tensor.transpose(bank[:, kt * SEQ + t * P:kt * SEQ + (t + 1) * P],
                                                   prob[:, e % 2, t * SEQ + kt * P:t * SEQ + (kt + 1) * P], ident[:, :])
                last.then_inc(pT_ps, 1)

            def apply(l, e):
                h = HEADS[e]
                if e < NHA:
                    pe.wait_ge(pTA, l * 8 + (e + 1))
                    v0, b0 = VA0 + (h // GROUP) * HD, 2
                else:
                    pe.wait_ge(pTB, l * 8 + (e - NHA + 1))
                    v0, b0 = VB0 + (h - NHA) * HD, 0
                at = (h % NHA) * HD
                for t in range(T):
                    for kt in range(T):
                        last = nc.tensor.matmul(acc[:, b0 + t, at:at + HD], probT[:, e % 2, kt * SEQ + t * P:kt * SEQ + (t + 1) * P],
                                                proj[:, kt, v0:v0 + HD], start=(kt == 0), stop=(kt == T - 1))
                last.then_inc(pv_done, 1)

            def out(l, j):
                k0, nk, group = sum(OUT1[:j]), OUT1[j], j // 2
                pe.wait_ge(yT_lo, l * 8 + 4 * (group + 1))
                down(g1(l, WIN + j), (WIN + j) % RING, lambda k: (a_hi[:, k0 + k, :], a_lo[:, k0 + k, :]), nk,
                     (work, acc)[group], start=(j % 2 == 0), stop=(j % 2 == 1), quarters=(j == len(OUT1) - 1))

            pe.wait_ge(id_loaded, 16)
            pe.wait_ge(zeroed, 1)
            pe.wait_ge(rows_loaded, 16 * 3)
            at = 0
            for n in range(3):
                nc.tensor.transpose(acc[:, 0, at:at + NROWS[n]], rows[n][0:NROWS[n], :], ident[0:NROWS[n], 0:NROWS[n]])\
                    .then_inc(rowsT, 1)
                at += NROWS[n]
            pe.wait_ge(cols_ready, 4)

            with pe.Fori(0, DEPTH) as l:
                turn_norm(x_tok, lambda t, half: (x_done, l * 8 + (2 * t + half + 1)))
                for kind, n in PLAN1:
                    if kind == "chunk":
                        if n >= 2:
                            pe.wait_ge(proj_ready, l * WIN + (n - 1))
                        by_tokens(g1(l, n), n % RING, n % 2, l * 2 if n == 0 else None)
                    elif kind == "tA":
                        for t in range(T):
                            pe.wait_ge(ropeA_done, l * T + (t + 1))
                            for i in range(5):
                                last = nc.tensor.transpose(acc_flat[:, i * SEQ + t * P:i * SEQ + (t + 1) * P],
                                                           qkA[:, t, i * P:(i + 1) * P], ident[:, :])
                        last.then_inc(qkA_ps, 1)
                    elif kind == "tB":
                        pe.wait_ge(qkA_T, l + 1)
                        for t in range(T):
                            pe.wait_ge(ropeB_done, l * T + (t + 1))
                            for i in range(8):
                                last = nc.tensor.transpose(acc_flat[:, i * SEQ + t * P:i * SEQ + (t + 1) * P],
                                                           proj[:, t, QB0 + i * P:QB0 + (i + 1) * P], ident[:, :])
                        last.then_inc(qkB_ps, 1)
                    elif kind == "score":
                        score(l, n)
                    elif kind == "turn":
                        turn(l, n)
                    elif kind == "pv":
                        apply(l, n)
                    elif kind == "out":
                        out(l, n)
                    elif kind == "yturn":
                        dst = acc_flat[:, 1024:2048]
                        pe.wait_ge(y_ready, l * 4 + (2 * n + T))
                        for t in range(T):
                            for k in range(4):
                                last = nc.tensor.transpose(dst[:, k * SEQ + t * P:k * SEQ + (t + 1) * P],
                                                           y_tok[:, t, n * 512 + k * P:n * 512 + (k + 1) * P], ident[:, :])
                        last.then_inc(yT_ps, 1)
                out(l, 1)
                out(l, 2)
                out(l, 3)
                turn_norm(x_tok, lambda t, half: (x_done, l * 8 + (2 * t + half + 5)))

                def hidden(slot):
                    return lambda k: (h_hi[:, slot, k * SEQ:(k + 1) * SEQ], h_lo[:, slot, k * SEQ:(k + 1) * SEQ])

                by_features(g1(l, MLP0), MLP0 % RING, 0, l * 2 + 1)
                open_sums()
                with pe.Fori(0, (NI1 - 1) // 3) as it:
                    for j in range(3):
                        i, c = it * 3 + (1 + j), MLP0 + 1 + 2 * j
                        pe.wait_ge(relu_done, l * NI1 + i)
                        by_features(g1(l, c) + it * 6, c % RING, 0)
                        pe.wait_ge(h1_lo, l * NI1 + i)
                        down(g1(l, c + 1) + it * 6, (c + 1) % RING, hidden(j % 3), 2)
                pe.wait_ge(h1_lo, l * NI1 + NI1)
                down(g1(l, CH1 - 1), (CH1 - 1) % RING, hidden((NI1 - 1) % 3), 2, stop=True, quarters=True)


            def ffn(l, f, cb, norm):
                def hidden(slot):
                    return lambda k: (h_hi[:, slot, k * SEQ:(k + 1) * SEQ], h_lo[:, slot, k * SEQ:(k + 1) * SEQ])

                m = (l * 2 + f) * NI2
                by_features(g2(l, cb), 0, 0, norm, layer_norm=True)
                by_features(g2(l, cb + 1), 1, 1)
                open_sums()
                with pe.Fori(0, NI2 - 1) as it:
                    pe.wait_ge(silu_done, m + it + 1)
                    by_features(g2(l, cb + 2) + it * 3, 2, 0)
                    pe.wait_ge(h2_f, m + it + 1)
                    by_features(g2(l, cb + 3) + it * 3, 0, 1)
                    pe.wait_ge(h2_lo, m + it + 1)
                    down(g2(l, cb + 4) + it * 3, 1, hidden(0), 2)
                pe.wait_ge(h2_lo, m + NI2)
                down(g2(l, cb + FFN - 1), 2, hidden(1), 2, stop=True, quarters=True)

            with pe.Fori(0, DEPTH) as l:
                norm0 = l * 3 + (2 * DEPTH + 1)
                keep_clock()
                turn_norm(xn, lambda t, half: (xn_ready[t], l * 6 + (half + 1)))
                ffn(l, 0, 0, norm0 - 1)
                keep_clock()
                turn_norm(xn, lambda t, half: (xn_ready[t], l * 6 + (half + 3)))
                pe.wait_ge(sgu_masked, l + 1)
                for h in range(AH):
                    last = nc.tensor.transpose(acc[:, 2, h * P:(h + 1) * P], sgu_rows[:, h, :], ident[:, :])
                last.then_inc(sgu_ps, 1)
                for j in range(WIN):
                    c = FFN + j
                    if j >= 2:
                        pe.wait_ge(z_done, l * 8 + (j - 1))
                    if j in (2, 3):
                        by_tokens(g2(l, c), c % RING, j % 2)
                    else:
                        by_features(g2(l, c), c % RING, j % 2, norm0 if j == 0 else None, layer_norm=True)
                    if j == 2:
                        pe.wait_ge(mix_bd, l * 64 + 64)
                        pe.wait_ge(conv_done, l * CT + CT)
                        for n in range(2):
                            dst = (work_flat[:, 1024:2048], acc_flat[:, 0:1024])[n]
                            for i in range(CT):
                                last = nc.tensor.matmul(dst[:, i * SEQ:(i + 1) * SEQ], bd[:, n, i, :], xr[:, i * SEQ:(i + 1) * SEQ],
                                                        start=True, stop=True)
                            last.then_inc(gate_ps, 1)
                    if j == 5:
                        pe.wait_ge(v_done, l * T + T)
                        pe.wait_ge(sgu_T, l + 1)
                        for t in range(T):
                            for h in range(AH):
                                at = t * 256 + h * HD
                                last = nc.tensor.matmul(acc[:, 2, at:at + HD], sguT[:, h, :], vn[:, at:at + HD], start=True, stop=True)
                        last.then_inc(mix_ps, 1)
                    if j == 6:
                        pe.wait_ge(ya_done, l * AH + AH)
                        for t in range(T):
                            for k in range(2):
                                last = nc.tensor.transpose(acc[:, 3, k * SEQ + t * P:k * SEQ + (t + 1) * P],
                                                           ya[:, t * 256 + k * P:t * 256 + (k + 1) * P], ident[:, :])
                        last.then_inc(yaT_ps, 1)
                k0 = 0
                for j, nk in enumerate(OUT2):
                    pe.wait_ge(y2_lo, l * 4 + (2, 3, 3, 3, 3, 4)[j])
                    if j == 0:
                        pe.wait_ge(sig_done, l * 2 * CT + 2 * CT)
                    down(g2(l, FFN + WIN + j), j % RING, lambda k, k0=k0: mixed(k0 + k), nk,
                         start=(j == 0), stop=(j == len(OUT2) - 1), quarters=(j == len(OUT2) - 1))
                    k0 += nk
                keep_clock()
                turn_norm(xn, lambda t, half: (xn_ready[t], l * 6 + (half + 5)))
                ffn(l, 1, FFN + WIN + len(OUT2), norm0 + 1)


def tables():
    pos = np.arange(SEQ)

    def rotation(p, half, theta):
        freqs = np.float32(theta) ** (-np.arange(half, dtype=np.float32) / np.float32(half))
        ang = p.astype(np.float32)[:, None] * freqs.astype(np.float32)[None, :]
        cos, sin = np.cos(ang.astype(np.float64)), np.sin(ang.astype(np.float64))
        return np.concatenate([cos, cos], -1), np.concatenate([-sin, sin], -1)

    def tiled(a):
        return np.ascontiguousarray(a.reshape(T, P, -1).transpose(1, 0, 2).astype(np.float32))

    (cr, sr), (cc, sc) = rotation(pos // 64, 16, 10000.0), rotation(pos % 64, 16, 10000.0)
    cp, sn = rotation(pos, 8, 500000.0)
    d = np.abs(pos[:, None] - pos[None, :])
    count = sum((d % dil == 0) & (d <= window // 2) for window, dil in ((128, 1), (512, 4), (2048, 16)))
    logc = np.where(count > 0, np.log(np.maximum(count, 1)), -1e30)
    return {"c_ident": np.eye(P, dtype=np.float32), "c_rope_ax": tiled(np.concatenate([cr, cc, sr, sc], -1)),
            "c_rope_pt": tiled(np.concatenate([cp, sn], -1)), "c_logc": tiled(logc)}


_INS = {
    "x": (SEQ, D), "w_in": None, "q_norm": None, "k_norm": None, "w_out": None, "w_mlp_in": None, "w_mlp_out": None,
    "final_norm": None, "ln_g_2": (-1, D), "ln_b_2": (-1, D), "ffn_w_gate_2": (2 * DEPTH, D, FF2), "ffn_w_up_2": (2 * DEPTH, D, FF2),
    "ffn_w_down_2": (2 * DEPTH, FF2, D), "w_in_2": None, "sgu_ln_g_2": None, "sgu_ln_b_2": None, "sgu_w_2": None,
    "rg_w_a_2": None, "rg_w_i_2": None, "w_out_2": None,
}


def kernel(**inputs):
    import concourse.bacc as _bacc
    from concourse.bass_utils import run_bass_kernel_spmd as _run

    nc = _bacc.Bacc("TRN2", target_bir_lowering=False, num_devices=1)
    arrays, ins = {}, {}
    for name, shape in _INS.items():
        a = np.ascontiguousarray(inputs[name])
        arrays[name] = a if shape is None else a.reshape(shape)
    arrays.update(tables())
    arrays["rows"] = np.concatenate([np.asarray(inputs[name]).reshape(-1, P)[l * n:(l + 1) * n]
                                     for group in ROWS for name, l, n in group])
    for name, a in arrays.items():
        ins[name] = nc.dram_tensor(name, a.shape, mybir.dt.from_np(a.dtype), kind="ExternalInput").ap()
    out = nc.dram_tensor("y", (SEQ, D), mybir.dt.float32, kind="ExternalOutput").ap()
    program(nc, ins, out)
    r = _run(nc, [arrays], core_ids=[0])
    return r.results[0]["y"].reshape(1, SEQ, D)
```
